# Optimizing a Trainium2 kernel written in Bass

```python
import math
import jax, jax.numpy as jnp
from jax import lax
import numpy as np

D_MODEL = 1024
BATCH = 1
SEQ = 512
DEPTH = 2

GRID_W = 64
CTX_LEN = 256
D_MIX = D_MODEL
BRANCH_W = D_MIX // 2
A_HEADS = 8
A_QK = BRANCH_W // (2 * A_HEADS)
A_V = 2 * A_QK
CONV_W = 3
C_HEADS = 8
C_HEAD_DIM = BRANCH_W // C_HEADS
NA_KH = 8
NA_KW = 16
D_GROUPS = 8
D_GROUP_W = BRANCH_W // D_GROUPS
Q_BLOCK = 128
ROPE_BASE = 10000.0
EPS = 1e-6
N_EVEN = (DEPTH + 1) // 2
N_ODD = DEPTH // 2
EVEN_IN = 8 * BRANCH_W
ODD_IN = 6 * BRANCH_W


def rms_norm(x, g):
    xf = x.astype(jnp.float32)
    y = xf * lax.rsqrt(jnp.mean(xf * xf, axis=-1, keepdims=True) + EPS)
    return (y * g.astype(jnp.float32)).astype(x.dtype)

def lambda_init(layer):
    return 0.8 - 0.6 * math.exp(-0.3 * layer)

def axial_rope(x, row, col):
    half = x.shape[-1] // 2
    nf = half // 2
    inv_freq = ROPE_BASE ** (-jnp.arange(nf, dtype=jnp.float32) / nf)

    def rotate(u, pos):
        ang = pos.astype(jnp.float32)[:, None] * inv_freq
        cos = jnp.cos(ang)[None, :, None, None, :]
        sin = jnp.sin(ang)[None, :, None, None, :]
        u1, u2 = u[..., :nf], u[..., nf:]
        return jnp.concatenate([u1 * cos - u2 * sin, u2 * cos + u1 * sin], axis=-1)

    xf = x.astype(jnp.float32)
    y = jnp.concatenate([rotate(xf[..., :half], row), rotate(xf[..., half:], col)], axis=-1)
    return y.astype(x.dtype)

def diff_attend(q, k, v, lam):
    s = jnp.einsum('bqhmd,bkhmd->bhmqk', q, k).astype(jnp.float32) * (A_QK ** -0.5)
    p = jax.nn.softmax(s, axis=-1)
    a = p[:, :, 0] - lam * p[:, :, 1]
    return jnp.einsum('bhqk,bkhd->bqhd', a, v.astype(jnp.float32))

def diff_attention_post(o, subln, lam_init):
    B, N = o.shape[:2]
    return (rms_norm(o, subln) * (1.0 - lam_init)).reshape(B, N, BRANCH_W)

def short_conv(b, c, u, w):
    z = c * u
    y = lax.conv_general_dilated(z, w.reshape(CONV_W, 1, BRANCH_W).astype(z.dtype),
                                 window_strides=(1,), padding='SAME',
                                 dimension_numbers=('NWC', 'WIO', 'NWC'),
                                 feature_group_count=BRANCH_W)
    return b * y

def fourier_mix(u):
    B, N, _ = u.shape
    ug = u.astype(jnp.float32).reshape(B, N, D_GROUPS, D_GROUP_W)
    y = jnp.fft.fft2(ug, axes=(1, 3), norm='ortho').real
    return y.reshape(B, N, BRANCH_W).astype(u.dtype)

def dense_attend(q, k, v):
    s = jnp.einsum('bqhd,bkhd->bhqk', q, k).astype(jnp.float32) * (C_HEAD_DIM ** -0.5)
    p = jax.nn.softmax(s, axis=-1)
    return jnp.einsum('bhqk,bkhd->bqhd', p, v.astype(jnp.float32))

def neighbourhood_attention(q, k, v, k_c, v_c, rpb):
    B, S, H, d = q.shape
    rows = S // GRID_W
    kh = min(NA_KH, rows)
    kw = NA_KW
    r = jnp.arange(rows)
    cq = jnp.arange(GRID_W)
    rs = jnp.clip(r - kh // 2, 0, rows - kh)
    cs = jnp.clip(cq - kw // 2, 0, GRID_W - kw)
    col_idx = cs[:, None] + jnp.arange(kw)[None, :]
    row_off = rs[:, None] + jnp.arange(kh)[None, :] - r[:, None] + (NA_KH - 1)
    col_off = col_idx - cq[:, None] + (NA_KW - 1)
    scale = d ** -0.5
    qg = jnp.moveaxis(q.reshape(B, rows, GRID_W, H, d), 1, 0)
    kg = k.reshape(B, rows, GRID_W, H, d)
    vg = v.reshape(B, rows, GRID_W, H, d)
    s_c_all = None

    def one_row(args):
        q_r, r0, roff = args
        kb = lax.dynamic_slice_in_dim(kg, r0, kh, axis=1)
        vb = lax.dynamic_slice_in_dim(vg, r0, kh, axis=1)
        kwin = kb[:, :, col_idx]
        vwin = vb[:, :, col_idx]
        bias = rpb[:, roff][:, :, col_off]
        s_w = jnp.einsum('bqhd,biqjhd->bhqij', q_r, kwin).astype(jnp.float32) * scale
        s_w = s_w + jnp.transpose(bias, (0, 2, 1, 3))[None].astype(jnp.float32)
        s_w = s_w.reshape(B, H, GRID_W, kh * kw)
        s_c = jnp.einsum('bqhd,bkhd->bhqk', q_r, k_c).astype(jnp.float32) * scale
        p = jax.nn.softmax(jnp.concatenate([s_w, s_c], axis=-1), axis=-1)
        p_w = p[..., :kh * kw].reshape(B, H, GRID_W, kh, kw)
        p_c = p[..., kh * kw:]
        return (jnp.einsum('bhqij,biqjhd->bqhd', p_w, vwin.astype(jnp.float32))
                + jnp.einsum('bhqk,bkhd->bqhd', p_c, v_c.astype(jnp.float32)))

    o = lax.map(one_row, (qg, rs, row_off))
    return jnp.moveaxis(o, 0, 1).reshape(B, S, H * d)

def even_mixer(px, pc, lam_p, subln, conv_w, lam_init, row, col, need_ctx):
    B, S, _ = px.shape
    L = pc.shape[1]
    qa, ka, va, ga, bb, cb, ub, gb = jnp.split(px, 8, axis=-1)
    qa = axial_rope(qa.reshape(B, S, A_HEADS, 2, A_QK), row, col)
    ka = axial_rope(ka.reshape(B, S, A_HEADS, 2, A_QK), row, col)
    va = va.reshape(B, S, A_HEADS, A_V)
    if need_ctx:
        qc, kc, vc, gc, bbc, cbc, ubc, gbc = jnp.split(pc, 8, axis=-1)
    else:
        kc, vc = jnp.split(pc, 2, axis=-1)
    kc = kc.reshape(B, L, A_HEADS, 2, A_QK)
    vc = vc.reshape(B, L, A_HEADS, A_V)
    lp = lam_p.astype(jnp.float32)
    lam = jnp.exp(jnp.sum(lp[0] * lp[1])) - jnp.exp(jnp.sum(lp[2] * lp[3])) + lam_init
    k_all = jnp.concatenate([kc, ka], axis=1)
    v_all = jnp.concatenate([vc, va], axis=1)
    nb = S // Q_BLOCK
    q_blocks = jnp.moveaxis(qa.reshape(B, nb, Q_BLOCK, A_HEADS, 2, A_QK), 1, 0)
    o = lax.map(lambda qb: diff_attend(qb, k_all, v_all, lam), q_blocks)
    o = jnp.moveaxis(o, 0, 1).reshape(B, S, A_HEADS, A_V)
    out_a = diff_attention_post(o, subln, lam_init).astype(px.dtype) * jax.nn.silu(ga)
    out_b = short_conv(bb, cb, ub, conv_w) * jax.nn.silu(gb)
    out_x = jnp.concatenate([out_a, out_b], axis=-1)
    if not need_ctx:
        return out_x, None
    oc = diff_attend(qc.reshape(B, L, A_HEADS, 2, A_QK), kc, vc, lam)
    out_ac = diff_attention_post(oc, subln, lam_init).astype(pc.dtype) * jax.nn.silu(gc)
    out_bc = short_conv(bbc, cbc, ubc, conv_w) * jax.nn.silu(gbc)
    return out_x, jnp.concatenate([out_ac, out_bc], axis=-1)

def odd_mixer(px, pc, rpb, need_ctx):
    B, S, _ = px.shape
    L = pc.shape[1]

    def heads(u):
        return u.reshape(u.shape[0], u.shape[1], C_HEADS, C_HEAD_DIM)

    qn, kn, vn, gn, ud, gd = jnp.split(px, 6, axis=-1)
    if need_ctx:
        qc, kc, vc, gc, udc, gdc = jnp.split(pc, 6, axis=-1)
    else:
        kc, vc = jnp.split(pc, 2, axis=-1)
    kc, vc = heads(kc), heads(vc)
    o_n = neighbourhood_attention(heads(qn), heads(kn), heads(vn), kc, vc, rpb)
    out_x = jnp.concatenate([o_n.astype(px.dtype) * jax.nn.silu(gn),
                             fourier_mix(ud) * jax.nn.silu(gd)], axis=-1)
    if not need_ctx:
        return out_x, None
    o_nc = dense_attend(heads(qc), kc, vc).reshape(B, L, BRANCH_W)
    out_c = jnp.concatenate([o_nc.astype(pc.dtype) * jax.nn.silu(gc),
                             fourier_mix(udc) * jax.nn.silu(gdc)], axis=-1)
    return out_x, out_c

def first_inputs(seed: int = 0) -> dict:
    key = jax.random.key(seed)
    ks = jax.random.split(key, 15)
    f = jnp.float32
    nrm = jax.random.normal
    return {
        'x': nrm(ks[0], (BATCH, SEQ, D_MODEL), f),
        'c': nrm(ks[1], (BATCH, D_MODEL), f),
        'ctx': nrm(ks[2], (BATCH, CTX_LEN, D_MODEL), f),
        'c_ctx': nrm(ks[3], (D_MODEL,), f),
        'w_mod': nrm(ks[4], (DEPTH, D_MODEL, 3 * D_MODEL), f) * D_MODEL ** -0.5,
        'b_mod': 0.02 * nrm(ks[5], (DEPTH, 3 * D_MODEL), f),
        'norm_pre': 1.0 + 0.1 * nrm(ks[6], (DEPTH, D_MODEL), f),
        'norm_post': 1.0 + 0.1 * nrm(ks[7], (DEPTH, D_MODEL), f),
        'w_in_even': nrm(ks[8], (N_EVEN, D_MODEL, EVEN_IN), f) * D_MODEL ** -0.5,
        'lam_a': 0.1 * nrm(ks[9], (N_EVEN, 4, A_QK), f),
        'subln_a': 1.0 + 0.1 * nrm(ks[10], (N_EVEN, A_V), f),
        'conv_b': nrm(ks[11], (N_EVEN, CONV_W, BRANCH_W), f) * CONV_W ** -0.5,
        'w_in_odd': nrm(ks[12], (N_ODD, D_MODEL, ODD_IN), f) * D_MODEL ** -0.5,
        'rpb_c': 0.1 * nrm(ks[13], (N_ODD, C_HEADS, 2 * NA_KH - 1, 2 * NA_KW - 1), f),
        'w_out': nrm(ks[14], (DEPTH, D_MIX, D_MODEL), f) * D_MIX ** -0.5,
    }

def first_block(x, c, ctx, c_ctx, w_mod, b_mod, norm_pre, norm_post, w_in_even, lam_a,
              subln_a, conv_b, w_in_odd, rpb_c, w_out):
    S = x.shape[1]
    t = jnp.arange(S)
    row = t // GRID_W
    col = t % GRID_W
    silu_c = jax.nn.silu(c)
    silu_cc = jax.nn.silu(c_ctx)
    for l in range(DEPTH):
        need_ctx = l < DEPTH - 1
        j = l // 2
        mod_x = (silu_c @ w_mod[l] + b_mod[l])[:, None, :]
        mod_c = (silu_cc @ w_mod[l] + b_mod[l])[None, None, :]
        sh_x, sc_x, g_x = jnp.split(mod_x, 3, axis=-1)
        sh_c, sc_c, g_c = jnp.split(mod_c, 3, axis=-1)
        hx = rms_norm(x, norm_pre[l]) * (1.0 + sc_x) + sh_x
        hc = rms_norm(ctx, norm_pre[l]) * (1.0 + sc_c) + sh_c
        w_in = w_in_even[j] if l % 2 == 0 else w_in_odd[j]
        px = hx @ w_in
        pc = hc @ (w_in if need_ctx else w_in[:, BRANCH_W:3 * BRANCH_W])
        if l % 2 == 0:
            mx, mc = even_mixer(px, pc, lam_a[j], subln_a[j], conv_b[j], lambda_init(l),
                                row, col, need_ctx)
        else:
            mx, mc = odd_mixer(px, pc, rpb_c[j], need_ctx)
        x = x + g_x * rms_norm(mx @ w_out[l], norm_post[l])
        if need_ctx:
            ctx = ctx + g_c * rms_norm(mc @ w_out[l], norm_post[l])
    return x


DEPTH_2 = 1

SSD_HEADS = 8
SSD_HEAD_DIM = 64
SSD_D = SSD_HEADS * SSD_HEAD_DIM
SSD_GROUPS = 2
SSD_STATE = 128
SSD_CONV = 4
SSD_CHUNK = 128
SSD_CONV_DIM = SSD_D + 2 * SSD_GROUPS * SSD_STATE
SSD_COLS = SSD_D + SSD_CONV_DIM + SSD_HEADS

RWKV_HEADS = 8
RWKV_HEAD_DIM = 64
RWKV_D = RWKV_HEADS * RWKV_HEAD_DIM
DECAY_LORA = 64
AAA_LORA = 64
GATE_LORA = 128
RWKV_COLS = 3 * RWKV_D + DECAY_LORA + AAA_LORA + GATE_LORA
RWKV_GN_EPS = 64e-5

D_MIX_2 = SSD_D + RWKV_D
D_IN = SSD_COLS + RWKV_COLS

D_FF = 2816
FFN_CONV = 3
NORM_EPS = 1e-6


def _rms_norm(x, g):
    xf = x.astype(jnp.float32)
    y = xf * lax.rsqrt(jnp.mean(xf * xf, axis=-1, keepdims=True) + NORM_EPS)
    return (y * g.astype(jnp.float32)).astype(x.dtype)

def _causal_dwconv(x, w, b):
    K, C = w.shape
    y = lax.conv_general_dilated(
        x, w[:, None, :].astype(x.dtype), window_strides=(1,), padding=[(K - 1, 0)],
        dimension_numbers=("NWC", "WIO", "NWC"), feature_group_count=C)
    return y + b.astype(x.dtype)

def _token_shift(x):
    return jnp.pad(x, ((0, 0), (1, 0), (0, 0)))[:, :-1]

def _segsum(a):
    cs = jnp.cumsum(a, axis=-1)
    diff = cs[..., :, None] - cs[..., None, :]
    L = a.shape[-1]
    mask = jnp.tril(jnp.ones((L, L), dtype=bool))
    return jnp.where(mask, diff, -jnp.inf)

def _ssd_chunked(xh, dt, A, Bg, Cg):
    b, T, h, p = xh.shape
    g, n = Bg.shape[2], Bg.shape[3]
    c, L = T // SSD_CHUNK, SSD_CHUNK
    Bh = jnp.repeat(Bg, h // g, axis=2).reshape(b, c, L, h, n)
    Ch = jnp.repeat(Cg, h // g, axis=2).reshape(b, c, L, h, n)
    X = (xh * dt[..., None]).reshape(b, c, L, h, p)
    a = (dt * A).reshape(b, c, L, h).transpose(0, 3, 1, 2)
    a_cs = jnp.cumsum(a, axis=-1)
    decay_in = jnp.exp(_segsum(a))
    scores = jnp.einsum("bclhn,bcshn->bhcls", Ch, Bh)
    y_diag = jnp.einsum("bhcls,bcshp->bclhp", scores * decay_in, X)
    decay_states = jnp.exp(a_cs[..., -1:] - a_cs)
    states = jnp.einsum("bclhn,bhcl,bclhp->bchpn", Bh, decay_states, X)
    chunk_decay = jnp.pad(a_cs[..., -1], ((0, 0), (0, 0), (1, 0)))
    decay_chunk = jnp.exp(_segsum(chunk_decay))
    states_p = jnp.concatenate([jnp.zeros_like(states[:, :1]), states], axis=1)
    states_in = jnp.einsum("bhzc,bchpn->bzhpn", decay_chunk, states_p)[:, :-1]
    y_off = jnp.einsum("bclhn,bchpn,bhcl->bclhp", Ch, states_in, jnp.exp(a_cs))
    return (y_diag + y_off).reshape(b, T, h, p)

def _ssd_mixer(p, conv_w, conv_b, dt_bias, a_log, d_skip, norm_g):
    b, T, _ = p.shape
    z, xbc, dt = jnp.split(p, [SSD_D, SSD_D + SSD_CONV_DIM], axis=-1)
    xbc = jax.nn.silu(_causal_dwconv(xbc, conv_w.astype(jnp.float32), conv_b.astype(jnp.float32)))
    xs, Bm, Cm = jnp.split(xbc, [SSD_D, SSD_D + SSD_GROUPS * SSD_STATE], axis=-1)
    xh = xs.reshape(b, T, SSD_HEADS, SSD_HEAD_DIM)
    Bm = Bm.reshape(b, T, SSD_GROUPS, SSD_STATE)
    Cm = Cm.reshape(b, T, SSD_GROUPS, SSD_STATE)
    dt = jax.nn.softplus(dt + dt_bias.astype(jnp.float32))
    A = -jnp.exp(a_log.astype(jnp.float32))
    y = _ssd_chunked(xh, dt, A, Bm, Cm) + d_skip.astype(jnp.float32)[:, None] * xh
    y = y.reshape(b, T, SSD_D) * jax.nn.silu(z)
    y = y.reshape(b, T, SSD_GROUPS, SSD_D // SSD_GROUPS)
    y = y * lax.rsqrt(jnp.mean(y * y, axis=-1, keepdims=True) + NORM_EPS)
    return y.reshape(b, T, SSD_D) * norm_g.astype(jnp.float32)

def _rwkv7_scan(r, w, k, v, za, zb):
    b, T, h, n = r.shape

    def step(S, inp):
        r_t, w_t, k_t, v_t, a_t, b_t = inp
        sa = jnp.einsum("bhij,bhj->bhi", S, a_t)
        S = S * w_t[:, :, None, :] + sa[..., None] * b_t[:, :, None, :] + v_t[..., None] * k_t[:, :, None, :]
        return S, jnp.einsum("bhij,bhj->bhi", S, r_t)

    xs = tuple(jnp.moveaxis(t, 1, 0) for t in (r, w, k, v, za, zb))
    S0 = jnp.zeros((b, h, n, n), dtype=r.dtype)
    _, ys = lax.scan(step, S0, xs)
    return jnp.moveaxis(ys, 0, 1)

def _rwkv7_mixer(p, mu, w0, w2, a0, a2, g2, k_k, k_a, r_k, ln_w, ln_b):
    b, T, _ = p.shape
    f32 = lambda t: t.astype(jnp.float32)
    p = p + (_token_shift(p) - p) * f32(mu)
    i1 = RWKV_D
    i2 = i1 + DECAY_LORA
    i3 = i2 + RWKV_D
    i4 = i3 + RWKV_D
    i5 = i4 + AAA_LORA
    r, w_lo, k, v, a_lo, g_lo = jnp.split(p, [i1, i2, i3, i4, i5], axis=-1)
    w_log = -jax.nn.softplus(-(f32(w0) + jnp.tanh(w_lo) @ f32(w2))) - 0.5
    decay = jnp.exp(-jnp.exp(w_log))
    a = jax.nn.sigmoid(f32(a0) + a_lo @ f32(a2))
    g = jax.nn.sigmoid(g_lo) @ f32(g2)
    heads = lambda t: t.reshape(b, T, RWKV_HEADS, RWKV_HEAD_DIM)
    kk = heads(k * f32(k_k))
    kk = kk / jnp.maximum(jnp.sqrt(jnp.sum(kk * kk, axis=-1, keepdims=True)), 1e-12)
    k = k * (1.0 + (a - 1.0) * f32(k_a))
    rh, kh, vh, ah = heads(r), heads(k), heads(v), heads(a)
    y = _rwkv7_scan(rh, heads(decay), kh, vh, -kk, kk * ah)
    mean = jnp.mean(y, axis=-1, keepdims=True)
    var = jnp.mean(jnp.square(y - mean), axis=-1, keepdims=True)
    y = ((y - mean) * lax.rsqrt(var + RWKV_GN_EPS)).reshape(b, T, RWKV_D) * f32(ln_w) + f32(ln_b)
    bonus = jnp.sum(rh * kh * f32(r_k), axis=-1, keepdims=True) * vh
    return (y + bonus.reshape(b, T, RWKV_D)) * g

def second_inputs(seed: int = 0) -> dict:
    key = jax.random.key(seed)
    ks = jax.random.split(key, 32)
    nrm = lambda k, shape, s: jax.random.normal(k, shape, jnp.float32) * s
    L = DEPTH_2
    dt = jnp.exp(jax.random.uniform(ks[5], (L, SSD_HEADS), jnp.float32) * (np.log(0.1) - np.log(0.001)) + np.log(0.001))
    dt = jnp.clip(dt, 1e-4)
    return {
        "x": nrm(ks[0], (BATCH, SEQ, D_MODEL), 1.0),
        "pre_mix_norm": 1.0 + nrm(ks[1], (L, D_MODEL), 0.05),
        "w_in": nrm(ks[2], (L, D_MODEL, D_IN), D_MODEL ** -0.5),
        "ssd_conv_w": nrm(ks[3], (L, SSD_CONV, SSD_CONV_DIM), SSD_CONV ** -0.5),
        "ssd_conv_b": nrm(ks[4], (L, SSD_CONV_DIM), 0.02),
        "ssd_dt_bias": dt + jnp.log(-jnp.expm1(-dt)),
        "ssd_a_log": jnp.log(jax.random.uniform(ks[6], (L, SSD_HEADS), jnp.float32, 1.0, 16.0)),
        "ssd_d": 1.0 + nrm(ks[7], (L, SSD_HEADS), 0.1),
        "ssd_norm": 1.0 + nrm(ks[8], (L, SSD_D), 0.05),
        "rwkv_mu": jax.random.uniform(ks[9], (L, RWKV_COLS), jnp.float32),
        "rwkv_w0": jax.random.uniform(ks[10], (L, RWKV_D), jnp.float32, -6.0, 1.0),
        "rwkv_w2": nrm(ks[11], (L, DECAY_LORA, RWKV_D), 0.1 * DECAY_LORA ** -0.5),
        "rwkv_a0": nrm(ks[12], (L, RWKV_D), 0.1),
        "rwkv_a2": nrm(ks[13], (L, AAA_LORA, RWKV_D), 0.5 * AAA_LORA ** -0.5),
        "rwkv_g2": nrm(ks[14], (L, GATE_LORA, RWKV_D), GATE_LORA ** -0.5),
        "rwkv_k_k": 0.85 + nrm(ks[15], (L, RWKV_D), 0.05),
        "rwkv_k_a": 1.0 + nrm(ks[16], (L, RWKV_D), 0.05),
        "rwkv_r_k": nrm(ks[17], (L, RWKV_HEADS, RWKV_HEAD_DIM), 0.1),
        "rwkv_ln_w": 1.0 + nrm(ks[18], (L, RWKV_D), 0.05),
        "rwkv_ln_b": nrm(ks[19], (L, RWKV_D), 0.02),
        "w_out": nrm(ks[20], (L, D_MIX_2, D_MODEL), D_MIX_2 ** -0.5),
        "post_mix_norm": 1.0 + nrm(ks[21], (L, D_MODEL), 0.05),
        "pre_ffn_norm": 1.0 + nrm(ks[22], (L, D_MODEL), 0.05),
        "ffn_w_up": nrm(ks[23], (L, D_MODEL, 2 * D_FF), D_MODEL ** -0.5),
        "ffn_conv_w": nrm(ks[24], (L, FFN_CONV, 2 * D_FF), FFN_CONV ** -0.5),
        "ffn_conv_b": nrm(ks[25], (L, 2 * D_FF), 0.02),
        "ffn_w_down": nrm(ks[26], (L, D_FF, D_MODEL), D_FF ** -0.5),
        "post_ffn_norm": 1.0 + nrm(ks[27], (L, D_MODEL), 0.05),
    }

def second_block(x, pre_mix_norm, w_in, ssd_conv_w, ssd_conv_b, ssd_dt_bias, ssd_a_log, ssd_d, ssd_norm,
              rwkv_mu, rwkv_w0, rwkv_w2, rwkv_a0, rwkv_a2, rwkv_g2, rwkv_k_k, rwkv_k_a, rwkv_r_k,
              rwkv_ln_w, rwkv_ln_b, w_out, post_mix_norm, pre_ffn_norm, ffn_w_up, ffn_conv_w,
              ffn_conv_b, ffn_w_down, post_ffn_norm):
    h = x
    for l in range(DEPTH_2):
        xn = _rms_norm(h, pre_mix_norm[l])
        proj = (xn @ w_in[l]).astype(jnp.float32)
        p_ssd, p_rwkv = jnp.split(proj, [SSD_COLS], axis=-1)
        y_ssd = _ssd_mixer(p_ssd, ssd_conv_w[l], ssd_conv_b[l], ssd_dt_bias[l], ssd_a_log[l],
                           ssd_d[l], ssd_norm[l])
        y_rwkv = _rwkv7_mixer(p_rwkv, rwkv_mu[l], rwkv_w0[l], rwkv_w2[l], rwkv_a0[l], rwkv_a2[l],
                              rwkv_g2[l], rwkv_k_k[l], rwkv_k_a[l], rwkv_r_k[l], rwkv_ln_w[l], rwkv_ln_b[l])
        mix = jnp.concatenate([y_ssd, y_rwkv], axis=-1).astype(h.dtype) @ w_out[l]
        h = h + _rms_norm(mix, post_mix_norm[l])
        hn = _rms_norm(h, pre_ffn_norm[l])
        u = _causal_dwconv(hn @ ffn_w_up[l], ffn_conv_w[l], ffn_conv_b[l])
        gate, val = jnp.split(u, 2, axis=-1)
        f = (jax.nn.silu(gate) * val) @ ffn_w_down[l]
        h = h + _rms_norm(f, post_ffn_norm[l])
    return h


def setup_inputs(seed=0):
    out = dict(first_inputs(seed))
    for name, value in second_inputs(seed + 1).items():
        if name != "x":
            out[name + "_2"] = value
    return out


def reference(
    x, c, ctx, c_ctx, w_mod, b_mod, norm_pre, norm_post, w_in_even, lam_a, subln_a, conv_b,
    w_in_odd, rpb_c, w_out, pre_mix_norm_2, w_in_2, ssd_conv_w_2, ssd_conv_b_2, ssd_dt_bias_2,
    ssd_a_log_2, ssd_d_2, ssd_norm_2, rwkv_mu_2, rwkv_w0_2, rwkv_w2_2, rwkv_a0_2, rwkv_a2_2,
    rwkv_g2_2, rwkv_k_k_2, rwkv_k_a_2, rwkv_r_k_2, rwkv_ln_w_2, rwkv_ln_b_2, w_out_2,
    post_mix_norm_2, pre_ffn_norm_2, ffn_w_up_2, ffn_conv_w_2, ffn_conv_b_2, ffn_w_down_2,
    post_ffn_norm_2,
):
    x = first_block(
        x, c, ctx, c_ctx, w_mod, b_mod, norm_pre, norm_post, w_in_even, lam_a, subln_a, conv_b,
        w_in_odd, rpb_c, w_out,
    )
    return second_block(
        x, pre_mix_norm_2, w_in_2, ssd_conv_w_2, ssd_conv_b_2, ssd_dt_bias_2, ssd_a_log_2,
        ssd_d_2, ssd_norm_2, rwkv_mu_2, rwkv_w0_2, rwkv_w2_2, rwkv_a0_2, rwkv_a2_2, rwkv_g2_2,
        rwkv_k_k_2, rwkv_k_a_2, rwkv_r_k_2, rwkv_ln_w_2, rwkv_ln_b_2, w_out_2, post_mix_norm_2,
        pre_ffn_norm_2, ffn_w_up_2, ffn_conv_w_2, ffn_conv_b_2, ffn_w_down_2, post_ffn_norm_2,
    )


_drawn_inputs = setup_inputs


def setup_inputs(seed=0):
    import zlib

    import numpy as np

    out = dict(_drawn_inputs(seed))
    spreads = {}
    factors = {'lam_a': 8.0,
     'rpb_c': 6.343,
     'ssd_conv_b_2': 3.525,
     'ssd_d_2': 3.027,
     'rwkv_w2_2': 8.0,
     'rwkv_a0_2': 4.118,
     'rwkv_k_k_2': 3.667,
     'rwkv_k_a_2': 2.803,
     'rwkv_ln_w_2': 3.634,
     'rwkv_ln_b_2': 8.0,
     'ffn_conv_b_2': 3.793}
    for name, (base, spread) in spreads.items():
        noise = np.random.default_rng([zlib.crc32(name.encode()), seed]).standard_normal(out[name].shape)
        drawn = base * np.exp(spread * noise) if base else spread * noise
        out[name] = __import__('jax').numpy.asarray(drawn.astype(out[name].dtype))
    for name, factor in factors.items():
        out[name] = (out[name] * factor).astype(out[name].dtype)
    return out
```

```python
from contextlib import ExitStack

import concourse.bass as bass
import numpy as np
from concourse import mybir

F32 = mybir.dt.float32
ALU = mybir.AluOpType
ACT = mybir.ActivationFunctionType
AX = mybir.AxisListType

P = 128
D = 1024
KD = D // P
S = 512
L = 256
TX = S // P
TC = L // P
NT = TX + TC
ST = S + L
BW = 512
FT = BW // P
EPS = 1e-6
BANK = 512

A_HEADS = 8
A_QK = 32
A_V = 64
LAM_INIT0 = 0.2
C_HEADS = 8
C_HD = 64
GRID_W = 64
ROWS = S // GRID_W
NA_KW = 16
BIAS_SLOTS = 2 * ROWS - 2

SSD_HEADS = 8
SSD_STATE = 128
RW_CHUNK = 64
RW_DECAY_SCALE = float(np.exp(-0.5))
RWKV_GN_EPS = 64e-5
D_FF = 2816
FF_T = D_FF // P


class Steps:

    def __init__(self, eng, sem, base=0):
        self.eng, self.sem, self.base, self.n = eng, sem, base, 0

    def inc(self, instruction):
        self.n += 1
        instruction.then_inc(self.sem, 1)
        return self.n

    def link(self, instruction):
        self.inc(instruction)
        self.eng.wait_ge(self.sem, self.base + self.n)


class Env:

    def semaphore(self, name):
        handle = self.nc.alloc_semaphore(name)
        self.stage_semaphores.append(handle)
        return handle

    def clear_semaphores(self):
        with self.nc.Block() as block:

            @block.gpsimd
            def _(pool):
                for handle in self.stage_semaphores:
                    pool.sem_clear(handle)

        for handle in self.stage_semaphores:
            self.nc.release_semaphore(handle)
        self.stage_semaphores = []


def bank(env, b, width=BANK, at=0):
    return env.PS[:, b * BANK + at : b * BANK + at + width]


def load_weights(env, eng, slot, source):
    eng.dma_start(env.WR[slot][:], source).then_inc(env.w_loaded[slot], 16)
    env.w_count[slot] += 16


def stage_modulation(env):
    nc, A = env.nc, env.A
    NCH = 3 * D // BANK
    with ExitStack() as ctx:
        sem = lambda name: env.semaphore(name)
        sb = lambda name, shape: ctx.enter_context(nc.sbuf_tensor(name, shape, F32))
        mod_row = sb("mod_row", [2, 2 * 3 * D])
        bmod = sb("bmod", [2, 2 * 3 * D])
        npost = sb("npost", [P, 2, D])
        npre = sb("npre", [P, 2, KD, 2])
        cond = sb("cond", [P, KD, 2])
        lam = sb("lam", [P, 4, A_QK])
        lam_t = sb("lam_t", [P, A_QK])
        lam_s = sb("lam_s", [P, 2])
        sel = sb("sel", [2, 2, P])
        small_in, cond_ready, mod_ready, mod_added = sem("small_in"), sem("cond_ready"), sem("mod_ready"), sem("mod_added")
        cols_ready, rows_ready, rows_read = sem("cols_ready"), sem("rows_ready"), sem("rows_read")
        resid_in, lam_dot, lam_exp, dve_step = sem("resid_in"), sem("lam_dot"), sem("lam_exp"), sem("mod_dve_step")
        base = list(env.w_count)
        SMALL = 16 * 8
        with nc.Block() as block:

            @block.sync
            def _(sp):
                for s in range(2):
                    load_weights(env, sp, s, A["w_mod"][s])
                with sp.Fori(1, NCH) as i:
                    for s in range(2):
                        sp.wait_ge(mod_ready, 2 * i + s - 1)
                        sp.dma_start(env.WR[s][:], A["w_mod"][bass.ds(2 * i + s, 1)].rearrange("a p k n -> (a p) k n")).then_inc(
                            env.w_loaded[s], 16
                        )
                for s in range(2):
                    env.w_count[s] += 16 * (NCH - 1)

            @block.scalar
            def _(act):
                act.dma_start(cond[:], A["cond"]).then_inc(small_in, 16)
                act.dma_start(bmod[:], A["b_mod"].partition_broadcast(2)).then_inc(small_in, 16)
                act.dma_start(sel[:], A["sel"]).then_inc(small_in, 16)
                act.dma_start(npre[:], A["norm_pre"]).then_inc(small_in, 16)
                act.dma_start(npost[:], A["norm_post"].partition_broadcast(P)).then_inc(small_in, 16)
                act.dma_start(lam[:], A["lam_a"].partition_broadcast(P)).then_inc(small_in, 16)
                act.dma_start(env.ident[:], A["ident"]).then_inc(small_in, 16)
                act.dma_start(env.subln[:], A["subln"]).then_inc(small_in, 16)
                act.dma_start(env.X[:], A["x"].rearrange("(t p) d -> p t d", p=P)).then_inc(resid_in, 16)
                act.dma_start(env.CX[:], A["ctx"].rearrange("(t p) d -> p t d", p=P)).then_inc(resid_in, 16)
                act.wait_ge(small_in, SMALL)
                nc.scalar.activation(cond[:], cond[:], ACT.Silu).then_inc(cond_ready, 1)
                act.wait_ge(lam_dot, 2)
                nc.scalar.activation(lam_s[:], lam_s[:], ACT.Exp).then_inc(lam_exp, 1)
                act.wait_ge(resid_in, 32)

            @block.tensor
            def _(pe):
                pe.wait_ge(cond_ready, 1)
                with pe.Fori(0, NCH) as i:
                    for s in range(2):
                        pe.wait_ge(env.w_loaded[s], base[s] + 16 + 16 * i)
                        pe.wait_ge(mod_added, 2 * i)
                        for k in range(KD):
                            m = nc.tensor.matmul(bank(env, s)[0:2], cond[:, k, :], env.WR[s][:, k, :], start=k == 0, stop=k == KD - 1)
                        m.then_inc(mod_ready, 1)
                pe.wait_ge(mod_added, 2 * NCH)
                for l in range(2):
                    for j in range(2):
                        for k in range(KD):
                            at = ((l * 2 + j) * KD + k) * 2
                            src = l * 3 * D + j * D + k * P
                            m = nc.tensor.transpose(bank(env, 2, 2, at), mod_row[0:2, src : src + P], env.ident[0:2, 0:2])
                m.then_inc(cols_ready, 1)
                for n, (l, r) in enumerate(((0, 0), (0, 1), (1, 0))):
                    for h in range(2):
                        if n == 2:
                            pe.wait_ge(rows_read, 1)
                        src = l * 3 * D + 2 * D + h * BANK
                        m = nc.tensor.matmul(
                            bank(env, 4 + 2 * (n % 2) + h), sel[0:2, r, :], mod_row[0:2, src : src + BANK], start=True, stop=True
                        )
                    m.then_inc(rows_ready, 1)

            @block.vector
            def _(dve):
                st = Steps(dve, dve_step)
                dve.wait_ge(small_in, SMALL)
                for j in range(2):
                    nc.vector.tensor_tensor_reduce(
                        lam_t[:], lam[:, 2 * j, :], lam[:, 2 * j + 1, :], 1.0, 0.0, ALU.mult, ALU.add, lam_s[:, j : j + 1]
                    ).then_inc(lam_dot, 1)
                    dve.wait_ge(lam_dot, j + 1)
                dve.wait_ge(lam_exp, 1)
                st.link(nc.vector.tensor_tensor(env.neg_lam[:], lam_s[:, 1:2], lam_s[:, 0:1], ALU.subtract))
                st.link(nc.vector.tensor_scalar(env.neg_lam[:], env.neg_lam[:], -LAM_INIT0, None, ALU.add))
                st.link(nc.vector.tensor_scalar(env.subln[:], env.subln[:], 1.0 - LAM_INIT0, None, ALU.mult))
                with dve.Fori(0, NCH) as i:
                    for s in range(2):
                        dve.wait_ge(mod_ready, 2 * i + s + 1)
                        cols = bass.ds((2 * i + s) * BANK, BANK)
                        nc.vector.tensor_tensor(mod_row[0:2, cols], bank(env, s)[0:2], bmod[0:2, cols], ALU.add).then_inc(mod_added, 1)
                dve.wait_ge(cols_ready, 1)
                cols = bank(env, 2, 2 * 2 * KD * 2).rearrange("p (l j k r) -> p l j k r", l=2, j=2, k=KD)
                for l in range(2):
                    st.link(
                        nc.vector.scalar_tensor_tensor(env.gain[:, l], cols[:, l, 1], 1.0, npre[:, l], ALU.add, ALU.mult)
                    )
                    st.link(nc.vector.tensor_copy(env.shift[:, l], cols[:, l, 0]))
                for n, l in enumerate((0, 0, 1)):
                    dve.wait_ge(rows_ready, n + 1)
                    m = nc.vector.tensor_tensor(
                        env.gate[:, n, :], env.PS[:, (4 + 2 * (n % 2)) * BANK : (6 + 2 * (n % 2)) * BANK], npost[:, l, :], ALU.mult
                    )
                    m.then_inc(rows_read, 1)


def stage_norm(env, name, streams, prefetch):
    nc = env.nc
    tiles = sum(s[1] for s in streams)
    with ExitStack() as ctx:
        sem = lambda n: env.semaphore(f"{name}_{n}")
        xs = ctx.enter_context(nc.sbuf_tensor(f"{name}_xs", [P, tiles, D], F32))
        ss = ctx.enter_context(nc.sbuf_tensor(f"{name}_ss", [P, tiles], F32))
        squares, mean_ready, root_ready, scaled, dve_step = sem("squares"), sem("mean"), sem("root"), sem("scaled"), sem("step")
        turned, act_out, dve_out = sem("turned"), sem("act_out"), sem("dve_out")
        jobs = [(s, k) for k in range(KD) for s in streams]
        with nc.Block() as block:

            @block.sync
            def _(sp):
                for s, source in enumerate(prefetch):
                    load_weights(env, sp, s, source)

            @block.scalar
            def _(act):
                for x, n, t0, _g, _s in streams:
                    for t in range(n):
                        nc.scalar.activation(xs[:, t0 + t, :], x[:, t, :], ACT.Square, accum_out=ss[:, t0 + t : t0 + t + 1]).then_inc(
                            squares, 1
                        )
                act.wait_ge(mean_ready, 1)
                nc.scalar.activation(ss[:], ss[:], ACT.Sqrt).then_inc(root_ready, 1)
                for j, ((x, n, t0, gain, shift), k) in enumerate(jobs):
                    if j % 2 == 0:
                        act.wait_ge(turned, j + 1)
                        out = env.HT[:, k, t0 * P : (t0 + n) * P]
                        if shift is None:
                            m = nc.scalar.activation(out, bank(env, j % 8, n * P), ACT.Copy, scale=gain(k))
                        else:
                            m = nc.scalar.activation(out, bank(env, j % 8, n * P), ACT.Identity, bias=shift(k), scale=gain(k))
                        m.then_inc(act_out, 1)

            @block.vector
            def _(dve):
                st = Steps(dve, dve_step)
                dve.wait_ge(squares, tiles)
                nc.vector.tensor_scalar(ss[:], ss[:], 1.0 / D, EPS, ALU.mult, ALU.add).then_inc(mean_ready, 1)
                dve.wait_ge(root_ready, 1)
                st.link(nc.vector.reciprocal(ss[:], ss[:]))
                for x, n, t0, _g, _s in streams:
                    for t in range(n):
                        nc.vector.tensor_scalar(xs[:, t0 + t, :], x[:, t, :], ss[:, t0 + t : t0 + t + 1], None, ALU.mult).then_inc(scaled, 1)
                for j, ((x, n, t0, gain, shift), k) in enumerate(jobs):
                    if j % 2 == 1:
                        dve.wait_ge(turned, j + 1)
                        out = env.HT[:, k, t0 * P : (t0 + n) * P]
                        if shift is None:
                            m = nc.vector.tensor_scalar(out, bank(env, j % 8, n * P), gain(k), None, ALU.mult)
                        else:
                            m = nc.vector.tensor_scalar(out, bank(env, j % 8, n * P), gain(k), shift(k), ALU.mult, ALU.add)
                        m.then_inc(dve_out, 1)

            @block.tensor
            def _(pe):
                for j, ((x, n, t0, _g, _s), k) in enumerate(jobs):
                    if j >= 8:
                        pe.wait_ge(act_out if j % 2 == 0 else dve_out, (j - 8) // 2 + 1)
                    for t in range(n):
                        pe.wait_ge(scaled, t0 + t + 1)
                        m = nc.tensor.transpose(bank(env, j % 8, P, t * P), xs[:, t0 + t, k * P : (k + 1) * P], env.ident[:])
                    m.then_inc(turned, 1)


def stage_out(env, name, streams, mixT, kts, weights, loaded, temps=None):
    nc = env.nc
    jobs = [(x, t, t0 + t, gate) for x, n, t0, gate in streams for t in range(n)]
    with ExitStack() as ctx:
        sem = lambda n: env.semaphore(f"{name}_{n}")
        sb = lambda n, shape: ctx.enter_context(nc.sbuf_tensor(f"{name}_{n}", shape, F32))
        ss = sb("ss", [P, len(jobs)])
        junk, upd = (sb("junk", [P, D])[:], sb("upd", [P, 2, D])) if temps is None else temps
        product, squares, mean_ready, root_ready, read = sem("product"), sem("squares"), sem("mean"), sem("root"), sem("read")
        dve_step = sem("step")
        both = lambda j: env.PS[:, 2 * (j % 4) * BANK : (2 * (j % 4) + 2) * BANK]
        with nc.Block() as block:

            @block.tensor
            def _(pe):
                for j, (x, t, at, gate) in enumerate(jobs):
                    if j >= 4:
                        pe.wait_ge(read, j - 3)
                    for h in range(2):
                        for k in range(kts):
                            for at_k, semaphore, value in loaded:
                                if (j, h, k) == (0, 0, at_k):
                                    pe.wait_ge(semaphore, value)
                            m = nc.tensor.matmul(
                                bank(env, 2 * (j % 4) + h), mixT[:, k, at * P : (at + 1) * P], weights(k, h), start=k == 0, stop=k == kts - 1)
                    m.then_inc(product, 1)

            @block.scalar
            def _(act):
                for j in range(len(jobs)):
                    act.wait_ge(product, j + 1)
                    if j:
                        act.wait_ge(squares, j)
                    nc.scalar.activation(junk, both(j), ACT.Square, accum_out=ss[:, j : j + 1]).then_inc(squares, 1)
                    act.wait_ge(mean_ready, j + 1)
                    nc.scalar.activation(ss[:, j : j + 1], ss[:, j : j + 1], ACT.Sqrt).then_inc(root_ready, 1)

            @block.vector
            def _(dve):
                st = Steps(dve, dve_step)
                for j, (x, t, at, gate) in enumerate(jobs):
                    root = ss[:, j : j + 1]
                    dve.wait_ge(squares, j + 1)
                    nc.vector.tensor_scalar(root, root, 1.0 / D, EPS, ALU.mult, ALU.add).then_inc(mean_ready, 1)
                    dve.wait_ge(root_ready, j + 1)
                    st.link(nc.vector.reciprocal(root, root))
                    nc.vector.scalar_tensor_tensor(upd[:, j % 2, :], both(j), root, gate, ALU.mult, ALU.mult).then_inc(read, 1)
                    dve.wait_ge(read, j + 1)
                    st.link(nc.vector.tensor_tensor(x[:, t, :], x[:, t, :], upd[:, j % 2, :], ALU.add))


def ring_out(env, name, streams):
    stage_out(
        env, name, streams, env.HT, KD, lambda k, h: env.WR[h][:, k, :], [(0, env.w_loaded[s], env.w_count[s]) for s in range(2)])


E_Q, E_K, E_GA, E_GB, E_CB, E_UB, E_BB = range(7)


def stage_even_proj(env, pT, vN):
    nc, A = env.nc, env.A
    with ExitStack() as ctx:
        sem = lambda name: env.semaphore("even_" + name)
        tile_ready, x_out, c_out, v_ready, v_out = sem("tile_ready"), sem("x_out"), sem("c_out"), sem("v_ready"), sem("v_out")
        base = [n - 16 for n in env.w_count]
        with nc.Block() as block:

            @block.sync
            def _(sp):
                with sp.Fori(1, 4) as i:
                    for s in range(2):
                        sp.wait_ge(tile_ready, FT * (2 * i + s - 1))
                        sp.dma_start(env.WR[s][:], A["w_in_even"][bass.ds(2 * i + s, 1)].rearrange("a p k n -> (a p) k n")).then_inc(
                            env.w_loaded[s], 16
                        )
                for s in range(2):
                    env.w_count[s] += 48
                for s in range(2):
                    if s == 0:
                        sp.wait_ge(tile_ready, 7 * FT)
                    else:
                        sp.wait_ge(v_ready, NT)
                    load_weights(env, sp, s, env.w_out_half(0, s))

            @block.tensor
            def _(pe):
                def chunk(s, n0, loaded):
                    pe.wait_ge(env.w_loaded[s], loaded)
                    for f in range(FT):
                        free = n0 + f if f == 0 else n0 + f - 1
                        pe.wait_ge(x_out, free)
                        pe.wait_ge(c_out, free)
                        for k in range(KD):
                            w = env.WR[s][:, k, f * P : (f + 1) * P]
                            nc.tensor.matmul(bank(env, f % 2), w, env.HT[:, k, 0:S], start=k == 0, stop=k == KD - 1)
                            m = nc.tensor.matmul(bank(env, 2 + f % 2, L), w, env.HT[:, k, S:ST], start=k == 0, stop=k == KD - 1)
                        m.then_inc(tile_ready, 1)

                with pe.Fori(0, 3) as i:
                    for s in range(2):
                        chunk(s, (2 * i + s) * FT, base[s] + 16 + 16 * i)
                chunk(0, 6 * FT, base[0] + 64)
                pe.wait_ge(env.w_loaded[1], base[1] + 64)
                for t in range(NT):
                    if t >= 2:
                        pe.wait_ge(v_out, t - 1)
                    for k in range(KD):
                        m = nc.tensor.matmul(
                            bank(env, 4 + t % 2), env.HT[:, k, t * P : (t + 1) * P], env.WR[1][:, k, :], start=k == 0, stop=k == KD - 1
                        )
                    m.then_inc(v_ready, 1)

            @block.vector
            def _(dve):
                def chunk(c, n0):
                    for f in range(FT):
                        dve.wait_ge(tile_ready, n0 + f + 1)
                        out = pT[:, bass.ds(c, 1), f, 0:S].rearrange("p a t -> p (a t)")
                        nc.vector.tensor_copy(out, bank(env, f % 2)).then_inc(x_out, 1)

                with dve.Fori(0, 3) as i:
                    for s in range(2):
                        chunk(2 * i + s, (2 * i + s) * FT)
                chunk(6, 6 * FT)

            @block.scalar
            def _(act):
                def chunk(c, n0):
                    for f in range(FT):
                        act.wait_ge(tile_ready, n0 + f + 1)
                        out = pT[:, bass.ds(c, 1), f, S:ST].rearrange("p a t -> p (a t)")
                        nc.scalar.copy(out, bank(env, 2 + f % 2, L)).then_inc(c_out, 1)

                with act.Fori(0, 3) as i:
                    for s in range(2):
                        chunk(2 * i + s, (2 * i + s) * FT)
                chunk(6, 6 * FT)
                for t in range(NT):
                    act.wait_ge(v_ready, t + 1)
                    nc.scalar.copy(vN[:, t, :], bank(env, 4 + t % 2)).then_inc(v_out, 1)


def stage_rope_conv(env, pT):
    nc, A = env.nc, env.A
    with ExitStack() as ctx:
        sem = lambda name: env.semaphore("rc_" + name)
        sb = lambda name, shape: ctx.enter_context(nc.sbuf_tensor("rc_" + name, shape, F32))
        rope = sb("rope", [P, 2, 2, S])
        swap, taps = sb("swap", [P, P]), sb("taps", [P, FT, 3])
        t1, t2 = sb("t1", [P, 2, S]), sb("t2", [P, 2, S])
        tables_in, silu_done, swapped, z_ready, bg_ready = sem("tables_in"), sem("silu"), sem("swapped"), sem("z"), sem("bg")
        rope_read, conv_ready, dve_step = sem("rope_read"), sem("conv_ready"), sem("step")
        mixed = sem("mixed")
        with nc.Block() as block:

            @block.sync
            def _(sp):
                sp.dma_start(swap[:], A["rope_swap"]).then_inc(tables_in, 16)
                sp.dma_start(rope[:], A["rope"]).then_inc(tables_in, 16)
                sp.dma_start(taps[:], A["conv_b"]).then_inc(tables_in, 16)

            @block.scalar
            def _(act):
                for g in (E_GB, E_GA):
                    nc.scalar.activation(pT[:, g], pT[:, g], ACT.Silu).then_inc(silu_done, 1)

            @block.tensor
            def _(pe):
                pe.wait_ge(tables_in, 48)
                for n in range(2 * FT):
                    if n >= 4:
                        pe.wait_ge(rope_read, n - 3)
                    nc.tensor.matmul(bank(env, n % 4), swap[:], pT[:, n // FT, n % FT, 0:S], start=True, stop=True).then_inc(swapped, 1)

            @block.gpsimd
            def _(pool):
                nc.gpsimd.tensor_tensor(pT[:, E_CB], pT[:, E_CB], pT[:, E_UB], ALU.mult).then_inc(z_ready, 1)
                pool.wait_ge(silu_done, 1)
                nc.gpsimd.tensor_tensor(pT[:, E_GB], pT[:, E_BB], pT[:, E_GB], ALU.mult).then_inc(bg_ready, 1)
                pool.wait_ge(bg_ready, 1)
                for f in range(FT):
                    pool.wait_ge(conv_ready, f + 1)
                    nc.gpsimd.tensor_tensor(env.HT[:, FT + f, :], pT[:, E_UB, f, :], pT[:, E_GB, f, :], ALU.mult).then_inc(mixed, 1)

            @block.vector
            def _(dve):
                st = Steps(dve, dve_step)
                dve.wait_ge(tables_in, 48)
                for n in range(2 * FT):
                    j, f = n // FT, n % FT
                    u = pT[:, j, f, 0:S]
                    st.inc(nc.vector.tensor_tensor(t1[:, n % 2, :], u, rope[:, j, 0, :], ALU.mult))
                    dve.wait_ge(swapped, n + 1)
                    nc.vector.tensor_tensor(t2[:, n % 2, :], bank(env, n % 4), rope[:, j, 1, :], ALU.mult).then_inc(rope_read, 1)
                    dve.wait_ge(rope_read, n + 1)
                    dve.wait_ge(dve_step, st.n)
                    st.link(nc.vector.tensor_tensor(u, t1[:, n % 2, :], t2[:, n % 2, :], ALU.add))
                st.link(nc.vector.tensor_scalar(pT[:, E_Q, :, S:ST], pT[:, E_Q, :, S:ST], A_QK**-0.5, None, ALU.mult))
                dve.wait_ge(z_ready, 1)
                for f in range(FT):
                    z, y = pT[:, E_CB, f, :], pT[:, E_UB, f, :]
                    st.link(nc.vector.tensor_scalar(y, z, taps[:, f, 1:2], None, ALU.mult))
                    for n, (a, b) in enumerate(((0, S), (S, ST))):
                        st.link(nc.vector.scalar_tensor_tensor(
                            y[:, a + 1 : b], z[:, a : b - 1], taps[:, f, 0:1], y[:, a + 1 : b], ALU.mult, ALU.add))
                        m = nc.vector.scalar_tensor_tensor(
                            y[:, a : b - 1], z[:, a + 1 : b], taps[:, f, 2:3], y[:, a : b - 1], ALU.mult, ALU.add)
                        if n == 0:
                            st.link(m)
                        else:
                            m.then_inc(conv_ready, 1)
                            dve.wait_ge(conv_ready, f + 1)


def stage_diff_attention(env, pT, vN, O):
    nc = env.nc
    UNITS = 2 * NT
    with ExitStack() as ctx:
        sem = lambda name: env.semaphore("da_" + name)
        sb = lambda name, shape: ctx.enter_context(nc.sbuf_tensor("da_" + name, shape, F32))
        qS, kS = sb("q", [P, ST]), sb("k", [P, ST])
        neg_max, sums, recip, ratio = sb("neg_max", [P, 2]), sb("sums", [P, 2, 2]), sb("recip", [P, 4, 2]), sb("ratio", [P, 1])
        ex = [[pT[:, E_CB, 2 * b + m, :] for m in range(2)] for b in range(2)]
        at = [pT[:, E_UB, b, :] for b in range(2)]
        atT = [pT[:, E_UB, 2 + b, :] for b in range(2)]
        staged, scores_ready = sem("staged"), [sem(f"scores{m}") for m in range(2)]
        max_ready, exp_done, combined, turned = sem("max"), [sem(f"exp{m}") for m in range(2)], sem("combined"), sem("turned")
        turned_out, pv_ready, o_out, dve_step = sem("turned_out"), sem("pv"), sem("o_out"), sem("step")
        T0, O0 = 4 * BANK, 6 * BANK

        def unit(u):
            hh, qt = u // NT, u % NT
            return hh, qt, (ST if qt < TX else L), (list(range(NT)) if qt < TX else list(range(TX, NT)))

        with nc.Block() as block:

            @block.gpsimd
            def _(pool):
                with pool.Fori(0, A_HEADS // 2) as i:
                    pool.wait_ge(scores_ready[1], UNITS * i)
                    nc.gpsimd.tensor_copy(qS[:], pT[:, E_Q, bass.ds(i, 1), :].rearrange("p a t -> p (a t)")).then_inc(staged, 1)
                    nc.gpsimd.tensor_copy(kS[:], pT[:, E_K, bass.ds(i, 1), :].rearrange("p a t -> p (a t)")).then_inc(staged, 1)

            @block.tensor
            def _(pe):
                with pe.Fori(0, A_HEADS // 2) as i:
                    n0 = UNITS * i
                    pe.wait_ge(staged, 2 * i + 2)

                    def scores(u):
                        hh, qt, n, _ = unit(u)
                        for m in range(2):
                            o = hh * 2 * A_QK + m * A_QK
                            q = qS[o : o + A_QK, qt * P : (qt + 1) * P]
                            pe.wait_ge(exp_done[m], n0 + u)
                            if n == ST:
                                nc.tensor.matmul(bank(env, 2 * m), q, kS[o : o + A_QK, 0:S], start=True, stop=True)
                                r = nc.tensor.matmul(bank(env, 2 * m + 1, L), q, kS[o : o + A_QK, S:ST], start=True, stop=True)
                            else:
                                r = nc.tensor.matmul(bank(env, 2 * m, L), q, kS[o : o + A_QK, S:ST], start=True, stop=True)
                            r.then_inc(scores_ready[m], 1)

                    def turn(u):
                        _, _, _, kts = unit(u)
                        pe.wait_ge(combined, n0 + u + 1)
                        pe.wait_ge(turned_out, n0 + u)
                        for j in range(len(kts)):
                            r = nc.tensor.transpose(env.PS[:, T0 + j * P : T0 + (j + 1) * P], at[u % 2][:, j * P : (j + 1) * P], env.ident[:])
                        r.then_inc(turned, 1)

                    def pv(u):
                        hh, _, _, kts = unit(u)
                        pe.wait_ge(turned_out, n0 + u + 1)
                        pe.wait_ge(o_out, n0 + max(u - 1, 0))
                        for j, kt in enumerate(kts):
                            v = vN[:, kt, bass.ds(i * 2 * A_V + hh * A_V, A_V)]
                            r = nc.tensor.matmul(
                                env.PS[:, O0 + (u % 2) * BANK : O0 + (u % 2) * BANK + A_V],
                                atT[u % 2][:, j * P : (j + 1) * P], v, start=j == 0, stop=j == len(kts) - 1)
                        r.then_inc(pv_ready, 1)

                    for u in range(UNITS + 2):
                        if u < UNITS:
                            scores(u)
                        if 1 <= u <= UNITS:
                            turn(u - 1)
                        if u >= 2:
                            pv(u - 2)

            @block.scalar
            def _(act):
                with act.Fori(0, A_HEADS // 2) as i:
                    n0 = UNITS * i

                    def exps(u):
                        _, _, n, _ = unit(u)
                        act.wait_ge(combined, n0 + max(u - 1, 0))
                        for m in range(2):
                            act.wait_ge(max_ready, 2 * n0 + 2 * u + m + 1)
                            nc.scalar.activation(
                                ex[u % 2][m][:, 0:n], env.PS[:, 2 * m * BANK : 2 * m * BANK + n], ACT.Exp,
                                bias=neg_max[:, m : m + 1], accum_out=sums[:, u % 2, m : m + 1]).then_inc(exp_done[m], 1)

                    def copy_out(u):
                        _, _, n, _ = unit(u)
                        act.wait_ge(turned, n0 + u + 1)
                        act.wait_ge(pv_ready, n0 + max(u - 1, 0))
                        nc.scalar.copy(atT[u % 2][:, 0:n], env.PS[:, T0 : T0 + n]).then_inc(turned_out, 1)

                    for u in range(UNITS + 1):
                        if u < UNITS:
                            exps(u)
                        if u >= 1:
                            copy_out(u - 1)

            @block.vector
            def _(dve):
                with dve.Fori(0, A_HEADS // 2) as i:
                    n0 = UNITS * i
                    st = Steps(dve, dve_step, 2 * UNITS * i)

                    def maxima(u):
                        _, _, n, _ = unit(u)
                        for m in range(2):
                            dve.wait_ge(scores_ready[m], n0 + u + 1)
                            nc.vector.tensor_reduce(
                                neg_max[:, m : m + 1], env.PS[:, 2 * m * BANK : 2 * m * BANK + n], AX.X, ALU.max, negate=True
                            ).then_inc(max_ready, 1)

                    def combine(u):
                        _, _, n, _ = unit(u)
                        for m in range(2):
                            dve.wait_ge(exp_done[m], n0 + u + 1)
                        st.link(nc.vector.reciprocal(recip[:, u % 4, :], sums[:, u % 2, :]))
                        st.link(nc.vector.scalar_tensor_tensor(
                            ratio[:], recip[:, u % 4, 1:2], env.neg_lam[:], sums[:, u % 2, 0:1], ALU.mult, ALU.mult))
                        dve.wait_ge(turned, n0 + max(u - 1, 0))
                        nc.vector.scalar_tensor_tensor(
                            at[u % 2][:, 0:n], ex[u % 2][1][:, 0:n], ratio[:], ex[u % 2][0][:, 0:n], ALU.mult, ALU.add
                        ).then_inc(combined, 1)

                    def out(u):
                        hh, qt, _, _ = unit(u)
                        dve.wait_ge(pv_ready, n0 + u + 1)
                        nc.vector.tensor_scalar(
                            O[:, qt, bass.ds(i * 2 * A_V + hh * A_V, A_V)],
                            env.PS[:, O0 + (u % 2) * BANK : O0 + (u % 2) * BANK + A_V],
                            recip[:, u % 4, 0:1], None, ALU.mult).then_inc(o_out, 1)

                    for u in range(UNITS + 3):
                        if u < UNITS:
                            maxima(u)
                        if 1 <= u <= UNITS:
                            combine(u - 1)
                        if u >= 3:
                            out(u - 3)


def stage_diff_post(env, pT, O):
    nc = env.nc
    G = NT * A_HEADS
    with ExitStack() as ctx:
        sem = lambda name: env.semaphore("dp_" + name)
        sb = lambda name, shape: ctx.enter_context(nc.sbuf_tensor("dp_" + name, shape, F32))
        ss = sb("ss", [P, G])
        sq = pT[:, E_CB].rearrange("p f t -> p (f t)")
        heads = O[:].rearrange("p t (h d) -> p (t h) d", d=A_V)
        step, mean_ready, root_ready, normed, turned, mixed = (
            sem("step"), sem("mean"), sem("root"), sem("normed"), sem("turned"), sem("mixed"))
        with nc.Block() as block:

            @block.vector
            def _(dve):
                st = Steps(dve, step)
                o = O[:].rearrange("p t c -> p (t c)")
                st.link(nc.vector.tensor_tensor(sq, o, o, ALU.mult))
                st.link(nc.vector.tensor_reduce(ss[:], sq.rearrange("p (g d) -> p g d", d=A_V), AX.X, ALU.add))
                nc.vector.tensor_scalar(ss[:], ss[:], 1.0 / A_V, EPS, ALU.mult, ALU.add).then_inc(mean_ready, 1)
                dve.wait_ge(root_ready, 1)
                st.link(nc.vector.reciprocal(ss[:], ss[:]))
                nc.vector.tensor_tensor(heads, heads, ss[:].unsqueeze(2).to_broadcast([P, G, A_V]), ALU.mult).then_inc(normed, 1)
                for f in range(FT):
                    for n, (a, b) in enumerate(((0, S), (S, ST))):
                        dve.wait_ge(turned, 2 * f + n + 1)
                        nc.vector.scalar_tensor_tensor(
                            env.HT[:, f, a:b], bank(env, (2 * f + n) % 8, b - a), env.subln[:], pT[:, E_GA, f, a:b], ALU.mult, ALU.mult
                        ).then_inc(mixed, 1)

            @block.scalar
            def _(act):
                act.wait_ge(mean_ready, 1)
                nc.scalar.activation(ss[:], ss[:], ACT.Sqrt).then_inc(root_ready, 1)

            @block.tensor
            def _(pe):
                pe.wait_ge(normed, 1)
                for f in range(FT):
                    for n, tiles in enumerate((range(TX), range(TX, NT))):
                        for j, t in enumerate(tiles):
                            m = nc.tensor.transpose(bank(env, (2 * f + n) % 8, P, j * P), O[:, t, f * P : (f + 1) * P], env.ident[:])
                        m.then_inc(turned, 1)


O_Q, O_GN, O_GD, O_K = range(4)


def stage_odd_proj(env, pT, kcT, vN, uN):
    nc, A = env.nc, env.A
    with ExitStack() as ctx:
        sem = lambda name: env.semaphore("odd_" + name)
        tile_ready, x_out, c_ready, c_out, n_ready, n_out = (
            sem("tile_ready"), sem("x_out"), sem("c_ready"), sem("c_out"), sem("natural_ready"), sem("natural_out"))
        base = [n - 16 for n in env.w_count]
        jobs = [(0, vN, t) for t in range(NT)] + [(1, uN, t) for t in range(TX)]
        with nc.Block() as block:

            @block.sync
            def _(sp):
                for s in range(2):
                    sp.wait_ge(tile_ready, FT * (s + 1))
                    load_weights(env, sp, s, A["w_in_odd"][2 + s])
                sp.wait_ge(tile_ready, FT * 3)
                load_weights(env, sp, 0, A["w_in_odd"][4])
                sp.wait_ge(c_ready, FT)
                load_weights(env, sp, 1, A["w_in_odd"][5])
                sp.wait_ge(n_ready, NT)
                load_weights(env, sp, 0, env.w_out_half(1, 0))
                sp.wait_ge(n_ready, NT + TX)
                load_weights(env, sp, 1, env.w_out_half(1, 1))

            @block.tensor
            def _(pe):
                with pe.Fori(0, 2) as i:
                    for s in range(2):
                        pe.wait_ge(env.w_loaded[s], base[s] + 16 + 16 * i)
                        for f in range(FT):
                            n = 2 * FT * i + s * FT + f
                            pe.wait_ge(x_out, n - 1 if s or f else n)
                            for k in range(KD):
                                m = nc.tensor.matmul(
                                    bank(env, f % 2), env.WR[s][:, k, f * P : (f + 1) * P], env.HT[:, k, 0:S], start=k == 0, stop=k == KD - 1)
                            m.then_inc(tile_ready, 1)
                for f in range(FT):
                    if f >= 2:
                        pe.wait_ge(c_out, f - 1)
                    for k in range(KD):
                        m = nc.tensor.matmul(
                            bank(env, 2 + f % 2, L), env.WR[1][:, k, f * P : (f + 1) * P], env.HT[:, k, S:ST], start=k == 0, stop=k == KD - 1)
                    m.then_inc(c_ready, 1)
                for j, (s, _, t) in enumerate(jobs):
                    if t == 0:
                        pe.wait_ge(env.w_loaded[s], base[s] + 48)
                    if j >= 2:
                        pe.wait_ge(n_out, j - 1)
                    for k in range(KD):
                        m = nc.tensor.matmul(
                            bank(env, 4 + j % 2), env.HT[:, k, t * P : (t + 1) * P], env.WR[s][:, k, :], start=k == 0, stop=k == KD - 1)
                    m.then_inc(n_ready, 1)

            @block.vector
            def _(dve):
                with dve.Fori(0, 2) as i:
                    for s in range(2):
                        for f in range(FT):
                            dve.wait_ge(tile_ready, 2 * FT * i + s * FT + f + 1)
                            out = pT[:, bass.ds(2 * i + s, 1), f, :].rearrange("p a t -> p (a t)")
                            nc.vector.tensor_copy(out, bank(env, f % 2)).then_inc(x_out, 1)
                for f in range(FT):
                    dve.wait_ge(c_ready, f + 1)
                    nc.vector.tensor_copy(kcT[:, f, :], bank(env, 2 + f % 2, L)).then_inc(c_out, 1)

            @block.scalar
            def _(act):
                for j, (_, dst, t) in enumerate(jobs):
                    act.wait_ge(n_ready, j + 1)
                    nc.scalar.copy(dst[:, t, :], bank(env, 4 + j % 2)).then_inc(n_out, 1)


def stage_fourier(env, pT, uN):
    nc, A = env.nc, env.A
    with ExitStack() as ctx:
        sem = lambda name: env.semaphore("ff_" + name)
        sb = lambda name, shape: ctx.enter_context(nc.sbuf_tensor("ff_" + name, shape, F32))
        dft_t, dft_f = sb("dft_t", [P, 2, TX, S]), sb("dft_f", [P, 2, P])
        mid = sb("mid", [P, FT, 2, S])
        tables_in, token_ready, token_out, feat_ready, mixed, gated, scaled = (
            sem("tables_in"), sem("token"), sem("token_out"), sem("feature"), sem("mixed"), sem("gated"), sem("scaled"))
        with nc.Block() as block:

            @block.sync
            def _(sp):
                sp.dma_start(dft_t[:], A["dft_t"]).then_inc(tables_in, 16)
                sp.dma_start(dft_f[:], A["dft_f"]).then_inc(tables_in, 16)

            @block.scalar
            def _(act):
                for n, g in enumerate((O_GD, O_GN)):
                    nc.scalar.activation(pT[:, g], pT[:, g], ACT.Silu).then_inc(gated, 1)
                for j in range(1, 2 * FT, 2):
                    act.wait_ge(token_ready, j + 1)
                    nc.scalar.copy(mid[:, j // 2, j % 2, :], bank(env, j % 4)).then_inc(token_out, 1)

            @block.tensor
            def _(pe):
                pe.wait_ge(tables_in, 32)
                for j in range(2 * FT):
                    if j >= 4:
                        pe.wait_ge(mixed if j % 2 == 0 else token_out, j // 2 - 1)
                    for t in range(TX):
                        m = nc.tensor.matmul(
                            bank(env, j % 4), uN[:, t, (j // 2) * P : (j // 2 + 1) * P], dft_t[:, j % 2, t, :], start=t == 0, stop=t == TX - 1)
                    m.then_inc(token_ready, 1)
                for f in range(FT):
                    pe.wait_ge(mixed, f + 1)
                    pe.wait_ge(token_out, f + 1)
                    for c in range(2):
                        m = nc.tensor.matmul(bank(env, 4 + f), dft_f[:, c, :], mid[:, f, c, :], start=c == 0, stop=c == 1)
                    m.then_inc(feat_ready, 1)

            @block.vector
            def _(dve):
                for f in range(FT):
                    dve.wait_ge(token_ready, 2 * f + 1)
                    nc.vector.tensor_copy(mid[:, f, 0, :], bank(env, 2 * f % 4)).then_inc(mixed, 1)
                nc.vector.tensor_scalar(pT[:, O_Q], pT[:, O_Q], C_HD**-0.5, None, ALU.mult).then_inc(scaled, 1)
                dve.wait_ge(gated, 1)
                for f in range(FT):
                    dve.wait_ge(feat_ready, f + 1)
                    nc.vector.tensor_tensor(env.HT[:, FT + f, 0:S], bank(env, 4 + f), pT[:, O_GD, f, :], ALU.mult).then_inc(mixed, 1)


def stage_neighbourhood(env, pT, kcT, vN, O):
    nc, A = env.nc, env.A
    UNITS = 2 * TX
    with ExitStack() as ctx:
        sem = lambda name: env.semaphore("na_" + name)
        sb = lambda name, shape: ctx.enter_context(nc.sbuf_tensor("na_" + name, shape, F32))
        bias = sb("bias", [P, C_HEADS, BIAS_SLOTS * GRID_W])
        qS, kS = sb("q", [P, S]), sb("k", [P, ST])
        scored = [sb(f"scored{b}", [P, S]) for b in range(2)]
        ex = [sb(f"exp{b}", [P, ST]) for b in range(2)]
        exT = [sb(f"expT{b}", [P, ST]) for b in range(2)]
        top, neg_max, sums, recip = sb("top", [P, 2, 2]), sb("neg_max", [P, 2]), sb("sums", [P, 4, 2]), sb("recip", [P, 4])
        bias_in, staged, scores_ready = sem("bias_in"), sem("staged"), sem("scores")
        max_ready, exp_done, turned, turned_out = sem("max"), sem("exp"), sem("turned"), sem("turned_out")
        pv_ready, o_out, dve_step = sem("pv"), sem("o_out"), sem("step")
        T0, O0 = 4 * BANK, 6 * BANK
        with nc.Block() as block:

            @block.sync
            def _(sp):
                sp.dma_start(bias[:], A["na_bias"]).then_inc(bias_in, 16)

            @block.gpsimd
            def _(pool):
                with pool.Fori(0, C_HEADS // 2) as i:
                    pool.wait_ge(scores_ready, UNITS * i)
                    nc.gpsimd.tensor_copy(qS[:], pT[:, O_Q, bass.ds(i, 1), :].rearrange("p a t -> p (a t)")).then_inc(staged, 1)
                    nc.gpsimd.tensor_copy(kS[:, 0:S], pT[:, O_K, bass.ds(i, 1), :].rearrange("p a t -> p (a t)")).then_inc(staged, 1)
                    nc.gpsimd.tensor_copy(kS[:, S:ST], kcT[:, bass.ds(i, 1), :].rearrange("p a t -> p (a t)")).then_inc(staged, 1)

            @block.tensor
            def _(pe):
                with pe.Fori(0, C_HEADS // 2) as i:
                    n0 = UNITS * i
                    pe.wait_ge(staged, 3 * i + 3)

                    def scores(u):
                        o, qt = (u // TX) * C_HD, u % TX
                        q = qS[o : o + C_HD, qt * P : (qt + 1) * P]
                        pe.wait_ge(exp_done, n0 + max(u - 1, 0))
                        nc.tensor.matmul(bank(env, 2 * (u % 2)), q, kS[o : o + C_HD, 0:S], start=True, stop=True)
                        nc.tensor.matmul(bank(env, 2 * (u % 2) + 1, L), q, kS[o : o + C_HD, S:ST], start=True, stop=True).then_inc(scores_ready, 1)

                    def turn(u):
                        pe.wait_ge(exp_done, n0 + u + 1)
                        pe.wait_ge(turned_out, n0 + u)
                        for j in range(NT):
                            r = nc.tensor.transpose(env.PS[:, T0 + j * P : T0 + (j + 1) * P], ex[u % 2][:, j * P : (j + 1) * P], env.ident[:])
                        r.then_inc(turned, 1)

                    def pv(u):
                        pe.wait_ge(turned_out, n0 + u + 1)
                        pe.wait_ge(o_out, n0 + max(u - 1, 0))
                        for j in range(NT):
                            v = vN[:, j, bass.ds(i * 2 * C_HD + (u // TX) * C_HD, C_HD)]
                            r = nc.tensor.matmul(
                                env.PS[:, O0 + (u % 2) * BANK : O0 + (u % 2) * BANK + C_HD],
                                exT[u % 2][:, j * P : (j + 1) * P], v, start=j == 0, stop=j == NT - 1)
                        r.then_inc(pv_ready, 1)

                    for u in range(UNITS + 2):
                        if u < UNITS:
                            scores(u)
                        if 1 <= u <= UNITS:
                            turn(u - 1)
                        if u >= 2:
                            pv(u - 2)

            @block.scalar
            def _(act):
                with act.Fori(0, C_HEADS // 2) as i:
                    n0 = UNITS * i

                    def exps(u):
                        act.wait_ge(max_ready, n0 + u + 1)
                        act.wait_ge(turned, n0 + max(u - 1, 0))
                        nc.scalar.activation(ex[u % 2][:, 0:S], scored[u % 2][:], ACT.Exp, bias=neg_max[:, u % 2 : u % 2 + 1], accum_out=sums[:, u % 4, 0:1])
                        nc.scalar.activation(
                            ex[u % 2][:, S:ST], bank(env, 2 * (u % 2) + 1, L), ACT.Exp, bias=neg_max[:, u % 2 : u % 2 + 1],
                            accum_out=sums[:, u % 4, 1:2]).then_inc(exp_done, 1)

                    def copy_out(u):
                        act.wait_ge(turned, n0 + u + 1)
                        act.wait_ge(pv_ready, n0 + max(u - 1, 0))
                        nc.scalar.copy(exT[u % 2][:], env.PS[:, T0 : T0 + ST]).then_inc(turned_out, 1)

                    for u in range(UNITS + 1):
                        if u < UNITS:
                            exps(u)
                        if u >= 1:
                            copy_out(u - 1)

            @block.vector
            def _(dve):
                dve.wait_ge(bias_in, 16)
                with dve.Fori(0, C_HEADS // 2) as i:
                    n0 = UNITS * i
                    st = Steps(dve, dve_step, 5 * UNITS * i)

                    def maxima(u):
                        dve.wait_ge(scores_ready, n0 + u + 1)
                        dve.wait_ge(exp_done, n0 + max(u - 1, 0))
                        st.link(nc.vector.tensor_reduce(top[:, u % 2, 0:1], bank(env, 2 * (u % 2) + 1, L), AX.X, ALU.max))
                        first = (ROWS - 1 - 2 * (u % TX) - 1) * GRID_W
                        rows = bias[:, bass.ds(2 * i + u // TX, 1), first : first + S].rearrange("p a t -> p (a t)")
                        st.link(nc.vector.tensor_tensor(scored[u % 2][:], bank(env, 2 * (u % 2)), rows, ALU.add))
                        st.link(nc.vector.tensor_reduce(top[:, u % 2, 1:2], scored[u % 2][:], AX.X, ALU.max))
                        nc.vector.tensor_reduce(neg_max[:, u % 2 : u % 2 + 1], top[:, u % 2, :], AX.X, ALU.max, negate=True).then_inc(max_ready, 1)

                    def total(u):
                        dve.wait_ge(exp_done, n0 + u + 1)
                        st.link(nc.vector.tensor_tensor(recip[:, u % 4 : u % 4 + 1], sums[:, u % 4, 0:1], sums[:, u % 4, 1:2], ALU.add))
                        st.link(nc.vector.reciprocal(recip[:, u % 4 : u % 4 + 1], recip[:, u % 4 : u % 4 + 1]))

                    def out(u):
                        dve.wait_ge(pv_ready, n0 + u + 1)
                        nc.vector.tensor_scalar(
                            O[:, u % TX, bass.ds(i * 2 * C_HD + (u // TX) * C_HD, C_HD)],
                            env.PS[:, O0 + (u % 2) * BANK : O0 + (u % 2) * BANK + C_HD],
                            recip[:, u % 4 : u % 4 + 1], None, ALU.mult).then_inc(o_out, 1)

                    for u in range(UNITS + 3):
                        if u < UNITS:
                            maxima(u)
                        if 1 <= u <= UNITS:
                            total(u - 1)
                        if u >= 3:
                            out(u - 3)


def stage_neighbourhood_post(env, pT, O):
    nc = env.nc
    with ExitStack() as ctx:
        sem = lambda name: env.semaphore("np_" + name)
        turned, mixed = sem("turned"), sem("mixed")
        with nc.Block() as block:

            @block.tensor
            def _(pe):
                for f in range(FT):
                    for t in range(TX):
                        m = nc.tensor.transpose(bank(env, f, P, t * P), O[:, t, f * P : (f + 1) * P], env.ident[:])
                    m.then_inc(turned, 1)

            @block.vector
            def _(dve):
                for f in range(FT):
                    dve.wait_ge(turned, f + 1)
                    nc.vector.tensor_tensor(env.HT[:, f, 0:S], bank(env, f), pT[:, O_GN, f, :], ALU.mult).then_inc(mixed, 1)


def layer_odd(env, gain, shift):
    nc, A = env.nc, env.A
    with ExitStack() as layer:
        stage_norm(
            env, "norm1", [(env.X, TX, 0, gain(1, 0), shift(1, 0)), (env.CX, TC, TX, gain(1, 1), shift(1, 1))],
            [A["w_in_odd"][0], A["w_in_odd"][1]])
        sb = lambda name, shape: layer.enter_context(nc.sbuf_tensor("odd_" + name, shape, F32))
        pT, kcT = sb("pT", [P, 4, FT, S]), sb("kcT", [P, FT, L])
        vN = sb("v", [P, NT, BW])
        with ExitStack() as fourier:
            uN = fourier.enter_context(nc.sbuf_tensor("odd_u", [P, TX, BW], F32))
            stage_odd_proj(env, pT, kcT, vN, uN)
            stage_fourier(env, pT, uN)
        O = sb("o", [P, TX, BW])
        stage_neighbourhood(env, pT, kcT, vN, O)
        stage_neighbourhood_post(env, pT, O)
    ring_out(env, "out1", [(env.X, TX, 0, env.gate[:, 2, :])])


T_XS, T_B, T_C, T_R, T_K, T_V, T_LO, T_GL = 0, 4, 6, 8, 12, 16, 20, 21
RW_TILES = 14
SECOND_CHUNKS = 7


def stage_second_proj(env, pT, zN, dtN):
    nc, A = env.nc, env.A
    with ExitStack() as ctx:
        sem = lambda name: env.semaphore("sec_" + name)
        tile_ready, x_out, n_ready, n_out, consts_in = sem("tile_ready"), sem("x_out"), sem("natural_ready"), sem("natural_out"), sem("consts_in")
        base = [n - 16 for n in env.w_count]
        with nc.Block() as block:

            @block.sync
            def _(sp):
                for c in range(2, 6):
                    sp.wait_ge(tile_ready, FT * (c - 1))
                    load_weights(env, sp, c % 2, A["w_in_2"][c])
                sp.wait_ge(tile_ready, FT * 5)
                load_weights(env, sp, 0, A["w_in_2"][6])

            @block.gpsimd
            def _(pool):
                for name, tensor in env.C2.items():
                    source = A["c2_" + name]
                    if name in ROWS2:
                        source = source.partition_broadcast(P)
                    pool.dma_start(tensor[:], source).then_inc(consts_in, 16)
                pool.wait_ge(consts_in, 16 * len(env.C2))

            @block.tensor
            def _(pe):
                def tile(s, f, n, free):
                    pe.wait_ge(x_out, free)
                    for k in range(KD):
                        m = nc.tensor.matmul(
                            bank(env, f % 2), env.WR[s][:, k, f * P : (f + 1) * P], env.HT[:, k, 0:S], start=k == 0, stop=k == KD - 1)
                    m.then_inc(tile_ready, 1)

                with pe.Fori(0, 2) as i:
                    for s in range(2):
                        pe.wait_ge(env.w_loaded[s], base[s] + 16 + 16 * i)
                        for f in range(FT):
                            n = 2 * FT * i + s * FT + f
                            tile(s, f, n, n - 1 if s or f else n)
                for s in range(2):
                    pe.wait_ge(env.w_loaded[s], base[s] + 48)
                    for f in range(FT if s == 0 else 2):
                        n = (4 + s) * FT + f
                        tile(s, f, n, n - 1)
                for t in range(TX):
                    for k in range(KD):
                        m = nc.tensor.matmul(
                            bank(env, 6, SSD_HEADS, t * SSD_HEADS), env.HT[:, k, t * P : (t + 1) * P],
                            env.WR[1][:, k, 2 * P : 2 * P + SSD_HEADS], start=k == 0, stop=k == KD - 1)
                m.then_inc(n_ready, 1)
                pe.wait_ge(env.w_loaded[0], base[0] + 64)
                for t in range(TX):
                    if t >= 2:
                        pe.wait_ge(n_out, t)
                    for k in range(KD):
                        m = nc.tensor.matmul(
                            bank(env, 4 + t % 2), env.HT[:, k, t * P : (t + 1) * P], env.WR[0][:, k, :], start=k == 0, stop=k == KD - 1)
                    m.then_inc(n_ready, 1)

            @block.vector
            def _(dve):
                with dve.Fori(0, 2) as i:
                    for j in range(2 * FT):
                        dve.wait_ge(tile_ready, 2 * FT * i + j + 1)
                        out = pT[:, bass.ds(2 * FT * i + j, 1), :].rearrange("p a t -> p (a t)")
                        nc.vector.tensor_copy(out, bank(env, j % 2)).then_inc(x_out, 1)
                for n in range(4 * FT, 5 * FT + 2):
                    dve.wait_ge(tile_ready, n + 1)
                    nc.vector.tensor_copy(pT[:, n, :], bank(env, n % 2)).then_inc(x_out, 1)

            @block.scalar
            def _(act):
                act.wait_ge(n_ready, 1)
                nc.scalar.copy(dtN[:], bank(env, 6, TX * SSD_HEADS)).then_inc(n_out, 1)
                for t in range(TX):
                    act.wait_ge(n_ready, t + 2)
                    nc.scalar.activation(zN[:, t, :], bank(env, 4 + t % 2), ACT.Silu).then_inc(n_out, 1)


GH = SSD_HEADS // 2
TH = TX * SSD_HEADS
HD = 64


def stage_ssd_prep(env, pT, dtN, V):
    nc, C2 = env.nc, env.C2
    with ExitStack() as ctx:
        sem = lambda name: env.semaphore("ssp_" + name)
        sb = lambda name, shape: ctx.enter_context(nc.sbuf_tensor("ssp_" + name, shape, F32))
        xd, mag, a, neg_a = sb("xd", [P, TH]), sb("mag", [P, TH]), sb("a", [P, TH]), sb("neg_a", [P, TH])
        conv_done, silu_done, turned, turned_out = sem("conv"), sem("silu"), sem("turned"), sem("turned_out")
        dt_in, dt_act, a_ready, cum_ready, cum_act, step, act_step = (
            sem("dt_in"), sem("dt_act"), sem("a"), sem("cum"), sem("cum_act"), sem("step"), sem("act_step"))
        with nc.Block() as block:

            @block.vector
            def _(dve):
                st = Steps(dve, step)
                nc.vector.tensor_tensor(xd[:], dtN[:], C2["dt_bias"][:], ALU.add).then_inc(dt_in, 1)
                dve.wait_ge(dt_act, 1)
                st.link(nc.vector.scalar_tensor_tensor(V["dt"][:], xd[:], 0.0, mag[:], ALU.max, ALU.add))
                nc.vector.scalar_tensor_tensor(a[:], V["dt"][:], -1.0, neg_a[:], ALU.mult, ALU.mult).then_inc(a_ready, 1)
                dve.wait_ge(a_ready, 1)
                dve.wait_ge(cum_ready, 1)
                st.link(nc.vector.tensor_copy(V["acs"][:], bank(env, 7, TH)))
                nc.vector.tensor_tensor(V["dstate"][:], bank(env, 7, TH, TH), V["acs"][:], ALU.subtract).then_inc(cum_act, 1)
                st.link(nc.vector.tensor_copy(V["a"][:], a[:]))
                for f in range(8):
                    y = V["conv"][:, f, :]
                    st.link(nc.vector.tensor_scalar(y, pT[:, f, :], C2["ssd_taps"][:, f, 3:4], C2["ssd_conv_b"][:, f : f + 1], ALU.mult, ALU.add))
                    for i in range(3):
                        back = 3 - i
                        m = nc.vector.scalar_tensor_tensor(
                            y[:, back:S], pT[:, f, 0 : S - back], C2["ssd_taps"][:, f, i : i + 1], y[:, back:S], ALU.mult, ALU.add)
                        if i < 2:
                            st.link(m)
                        else:
                            m.then_inc(conv_done, 1)
                for t in range(TX):
                    dve.wait_ge(turned, t + 1)
                    nc.vector.tensor_copy(V["xs"][:, t, :], bank(env, 2 * (t % 2))).then_inc(turned_out, 1)
                    nc.vector.tensor_copy(V["B"][:, t, :], bank(env, 2 * (t % 2) + 1, 2 * SSD_STATE)).then_inc(turned_out, 1)
                dve.wait_ge(turned_out, 2 * TX)
                xs = V["xs"][:].rearrange("p t (h d) -> p (t h) d", d=HD)
                wide = lambda v: v[:].unsqueeze(2).to_broadcast([P, TH, HD])
                for t in range(TX):
                    st.inc(nc.vector.tensor_tensor(V["skip"][:, t, :], V["xs"][:, t, :], C2["ssd_d"][:], ALU.mult))
                st.link(nc.vector.tensor_tensor(V["xdt"][:].rearrange("p t (h d) -> p (t h) d", d=HD), xs, wide(V["dt"]), ALU.mult))
                dve.wait_ge(cum_act, 2)
                st.link(nc.vector.tensor_tensor(
                    V["xds"][:].rearrange("p t (h d) -> p (t h) d", d=HD),
                    V["xdt"][:].rearrange("p t (h d) -> p (t h) d", d=HD), wide(V["dstate"]), ALU.mult))

            @block.scalar
            def _(act):
                st = Steps(act, act_step)
                st.link(nc.scalar.activation(neg_a[:], C2["a_log"][:], ACT.Exp))
                act.wait_ge(dt_in, 1)
                st.link(nc.scalar.activation(mag[:], xd[:], ACT.Abs))
                st.link(nc.scalar.activation(mag[:], mag[:], ACT.Exp, scale=-1.0))
                nc.scalar.activation(mag[:], mag[:], ACT.Ln, bias=1.0).then_inc(dt_act, 1)
                act.wait_ge(cum_act, 1)
                st.inc(nc.scalar.activation(V["eacs"][:], V["acs"][:], ACT.Exp))
                st.inc(nc.scalar.activation(V["etot"][:], bank(env, 7, TH, TH), ACT.Exp))
                nc.scalar.activation(V["dstate"][:], V["dstate"][:], ACT.Exp).then_inc(cum_act, 1)
                for f in range(8):
                    act.wait_ge(conv_done, f + 1)
                    nc.scalar.activation(V["conv"][:, f, :], V["conv"][:, f, :], ACT.Silu).then_inc(silu_done, 1)

            @block.tensor
            def _(pe):
                pe.wait_ge(a_ready, 1)
                nc.tensor.matmul(bank(env, 7, TH), C2["upto"][:], a[:], start=True, stop=True)
                nc.tensor.matmul(bank(env, 7, TH, TH), C2["ones"][:], a[:], start=True, stop=True).then_inc(cum_ready, 1)
                pe.wait_ge(silu_done, T_C)
                for t in range(TX):
                    if t >= 2:
                        pe.wait_ge(turned_out, 2 * (t - 1))
                    for f in range(FT):
                        nc.tensor.transpose(bank(env, 2 * (t % 2), P, f * P), V["conv"][:, f, t * P : (t + 1) * P], env.ident[:])
                    for g in range(2):
                        m = nc.tensor.transpose(bank(env, 2 * (t % 2) + 1, P, g * P), V["conv"][:, T_B + g, t * P : (t + 1) * P], env.ident[:])
                    m.then_inc(turned, 1)


def stage_ssd(env, V, zN):
    nc, C2 = env.nc, env.C2
    with ExitStack() as ctx:
        sem = lambda name: env.semaphore("ssd_" + name)
        sb = lambda name, shape: ctx.enter_context(nc.sbuf_tensor("ssd_" + name, shape, F32))
        tri_a, decay, scores = sb("tri_a", [P, 2, GH, P]), sb("decay", [P, 2, GH, P]), sb("scores", [P, 2, P])
        state, y, ss = sb("state", [P, BW]), sb("y", [P, TX, BW]), sb("ss", [P, TX * 2])
        sq = V["xs"][:].rearrange("p t c -> p (t c)")
        tri_ready, row_ready, diff_ready, decayed, weighed, scores_read = (
            sem("tri"), sem("row"), sem("diff"), sem("decayed"), sem("weighed"), sem("scores_read"))
        diag_ready, scores_ready, new_ready, y_read, state_ready, step, root_ready, mean_ready, turned, normed, mixed = (
            sem("diag"), sem("scores"), sem("new"), sem("y_read"), sem("state"), sem("step"), sem("root"), sem("mean"), sem("turned"),
            sem("normed"), sem("mixed"))
        units = [(t, g) for t in range(TX) for g in range(2)]
        with nc.Block() as block:

            @block.gpsimd
            def _(pool):
                for n, (t, g) in enumerate(units):
                    if n >= 2:
                        pool.wait_ge(row_ready, n - 1)
                    for h in range(GH):
                        th = t * SSD_HEADS + g * GH + h
                        m = nc.gpsimd.tensor_scalar(tri_a[:, n % 2, h, :], C2["upto"][:], V["a"][:, th : th + 1], None, ALU.mult)
                    m.then_inc(tri_ready, 1)

            @block.tensor
            def _(pe):
                def rows(n):
                    t, g = units[n]
                    tok = slice(t * P, (t + 1) * P)
                    pe.wait_ge(tri_ready, n + 1)
                    if n >= 2:
                        pe.wait_ge(scores_read, n - 1)
                        pe.wait_ge(diff_ready, n - 1)
                    nc.tensor.matmul(bank(env, n % 2), C2["ones"][:], tri_a[:, n % 2].rearrange("p h l -> p (h l)"), start=True, stop=True).then_inc(
                        row_ready, 1)
                    nc.tensor.matmul(
                        bank(env, 2 + n % 2, P), V["conv"][:, T_B + g, tok], V["conv"][:, T_C + g, tok], start=True, stop=True).then_inc(
                        scores_ready, 1)

                rows(0)
                for n, (t, g) in enumerate(units):
                    tok = slice(t * P, (t + 1) * P)
                    if n + 1 < len(units):
                        rows(n + 1)
                    pe.wait_ge(weighed, n + 1)
                    if t >= 1:
                        pe.wait_ge(y_read, t)
                    for h in range(GH):
                        c = (g * GH + h) * HD
                        m = nc.tensor.matmul(
                            bank(env, 4, HD, c), decay[:, n % 2, h, :], V["xdt"][:, t, c : c + HD], start=True, stop=True)
                    m.then_inc(diag_ready, 1)
                    if g == 1:
                        if t >= 1:
                            pe.wait_ge(state_ready, t)
                            for q in range(2):
                                m = nc.tensor.matmul(
                                    bank(env, 5, 2 * P, q * 2 * P), V["conv"][:, T_C + q, tok], state[:, q * 2 * P : (q + 1) * 2 * P], start=True, stop=True)
                        for q in range(2):
                            m = nc.tensor.matmul(
                                bank(env, 6, 2 * P, q * 2 * P), V["B"][:, t, q * P : (q + 1) * P], V["xds"][:, t, q * 2 * P : (q + 1) * 2 * P], start=True, stop=True)
                        m.then_inc(new_ready, 1)
                pe.wait_ge(normed, 1)
                for f in range(FT):
                    for t in range(TX):
                        m = nc.tensor.transpose(bank(env, f, P, t * P), y[:, t, f * P : (f + 1) * P], env.ident[:])
                    m.then_inc(turned, 1)

            @block.scalar
            def _(act):
                for n in range(len(units)):
                    act.wait_ge(diff_ready, n + 1)
                    nc.scalar.activation(decay[:, n % 2], decay[:, n % 2], ACT.Exp).then_inc(decayed, 1)
                act.wait_ge(mean_ready, 1)
                nc.scalar.activation(ss[:], ss[:], ACT.Sqrt).then_inc(root_ready, 1)

            @block.vector
            def _(dve):
                st = Steps(dve, step)

                def differ(n):
                    t, g = units[n]
                    dve.wait_ge(row_ready, n + 1)
                    if n >= 2:
                        dve.wait_ge(diag_ready, n - 1)
                    for h in range(GH):
                        th = t * SSD_HEADS + g * GH + h
                        m = nc.vector.tensor_scalar(
                            decay[:, n % 2, h, :], bank(env, n % 2, P, h * P), V["acs"][:, th : th + 1], 0.0, ALU.subtract, ALU.min)
                    m.then_inc(diff_ready, 1)
                    dve.wait_ge(scores_ready, n + 1)
                    nc.vector.tensor_tensor(scores[:, n % 2, :], bank(env, 2 + n % 2, P), C2["upto"][:], ALU.mult).then_inc(scores_read, 1)

                differ(0)
                for n, (t, g) in enumerate(units):
                    if n + 1 < len(units):
                        differ(n + 1)
                    dve.wait_ge(decayed, n + 1)
                    dve.wait_ge(scores_read, n + 1)
                    nc.vector.tensor_tensor(
                        decay[:, n % 2], decay[:, n % 2], scores[:, n % 2, :].unsqueeze(1).to_broadcast([P, GH, P]), ALU.mult).then_inc(weighed, 1)
                    if g == 0:
                        continue
                    th = slice(t * SSD_HEADS, (t + 1) * SSD_HEADS)
                    wide = lambda v: v[:, th].unsqueeze(2).to_broadcast([P, SSD_HEADS, HD])
                    by_head = lambda v: v.rearrange("p (h d) -> p h d", d=HD)
                    out = y[:, t, :]
                    dve.wait_ge(new_ready, t + 1)
                    st.link(nc.vector.tensor_tensor(out, bank(env, 4), V["skip"][:, t, :], ALU.add))
                    if t >= 1:
                        st.link(nc.vector.tensor_tensor(by_head(sq[:, 0:BW]), by_head(bank(env, 5)), wide(V["eacs"]), ALU.mult))
                        st.link(nc.vector.tensor_tensor(out, out, sq[:, 0:BW], ALU.add))
                        st.link(nc.vector.tensor_tensor(by_head(state[:]), by_head(state[:]), wide(V["etot"]), ALU.mult))
                        m = nc.vector.tensor_tensor(state[:], state[:], bank(env, 6), ALU.add)
                    else:
                        m = nc.vector.tensor_copy(state[:], bank(env, 6))
                    m.then_inc(state_ready, 1)
                    dve.wait_ge(state_ready, t + 1)
                    nc.vector.tensor_tensor(out, out, zN[:, t, :], ALU.mult).then_inc(y_read, 1)
                dve.wait_ge(y_read, TX)
                flat = y[:].rearrange("p t c -> p (t c)")
                st.link(nc.vector.tensor_tensor(sq[:], flat, flat, ALU.mult))
                st.link(nc.vector.tensor_reduce(ss[:], sq[:].rearrange("p (g c) -> p g c", c=2 * P), AX.X, ALU.add))
                nc.vector.tensor_scalar(ss[:], ss[:], 1.0 / (2 * P), EPS, ALU.mult, ALU.add).then_inc(mean_ready, 1)
                dve.wait_ge(root_ready, 1)
                st.link(nc.vector.reciprocal(ss[:], ss[:]))
                groups = flat.rearrange("p (g c) -> p g c", c=2 * P)
                nc.vector.tensor_tensor(groups, groups, ss[:].unsqueeze(2).to_broadcast([P, TX * 2, 2 * P]), ALU.mult).then_inc(normed, 1)
                for f in range(FT):
                    dve.wait_ge(turned, f + 1)
                    nc.vector.tensor_scalar(env.HT[:, f, :], bank(env, f), C2["ssd_norm"][:, f : f + 1], None, ALU.mult).then_inc(mixed, 1)


LEVELS = RW_CHUNK.bit_length() - 1
CHUNKS = S // RW_CHUNK


def stage_rwkv_shift(env, pT):
    nc, C2 = env.nc, env.C2
    with ExitStack() as ctx:
        sem = lambda name: env.semaphore("rws_" + name)
        keep = ctx.enter_context(nc.sbuf_tensor("rws_keep", [P, RW_TILES], F32))
        diff, step, mixed = sem("diff"), sem("step"), sem("mixed")
        slot = lambda n: env.WR[n // KD][:, n % KD, 0 : S - 1]
        with nc.Block() as block:

            @block.gpsimd
            def _(pool):
                for n in range(0, RW_TILES, 2):
                    p = pT[:, T_R + n, :]
                    nc.gpsimd.tensor_tensor(slot(n), p[:, 0 : S - 1], p[:, 1:S], ALU.subtract).then_inc(diff, 1)

            @block.vector
            def _(dve):
                st = Steps(dve, step)
                st.link(nc.vector.tensor_scalar(keep[:], C2["mu"][:], -1.0, 1.0, ALU.mult, ALU.add))
                for n in range(1, RW_TILES, 2):
                    p = pT[:, T_R + n, :]
                    st.link(nc.vector.tensor_tensor(slot(n), p[:, 0 : S - 1], p[:, 1:S], ALU.subtract))
                for k, n in enumerate([*range(1, RW_TILES, 2), *range(0, RW_TILES, 2)]):
                    if n % 2 == 0:
                        dve.wait_ge(diff, n // 2 + 1)
                    p = pT[:, T_R + n, :]
                    nc.vector.scalar_tensor_tensor(p[:, 1:S], slot(n), C2["mu"][:, n : n + 1], p[:, 1:S], ALU.mult, ALU.add).then_inc(mixed, 1)
                first = pT[:, T_R : T_R + RW_TILES, 0:1].rearrange("p n a -> p (n a)")
                nc.vector.tensor_tensor(first, first, keep[:], ALU.mult).then_inc(mixed, 1)


def stage_rwkv_features(env, pT, W):
    nc, C2 = env.nc, env.C2
    with ExitStack() as ctx:
        sem = lambda name: env.semaphore("rwf_" + name)
        sb = lambda name: ctx.enter_context(nc.sbuf_tensor("rwf_" + name, [P, FT, S], F32))
        half = lambda s, h: env.WR[s][:, h * FT : (h + 1) * FT, :]
        lw, cum, inv, pex = half(0, 0), half(0, 1), half(1, 0), half(1, 1)
        kkn, a, pin = sb("kkn"), sb("a"), sb("pin")
        less_ka = ctx.enter_context(nc.sbuf_tensor("rwf_less_ka", [P, FT], F32))
        r, k, v = (pT[:, x : x + FT, :] for x in (T_R, T_K, T_V))
        bT, kT = pT[:, 0:FT, :], pT[:, FT : 2 * FT, :]
        lora_act, u_ready, sig_done, g_ready, g_out, sq_done = sem("lora"), sem("u"), sem("sig"), sem("g"), sem("g_out"), sem("sq")
        norm_ready, norm_out, cum_ready, exp_done, step, act_step = sem("norm"), sem("norm_out"), sem("cum"), sem("exp"), sem("step"), sem("act_step")
        b_ready, k_ready, rk_ready, kp_ready, r_done, turned, turned_out, bonus_ready = (
            sem("b"), sem("k"), sem("rk"), sem("kp"), sem("r"), sem("turned"), sem("turned_out"), sem("bonus"))
        naturals = [(W["v"], v), (W["b"], bT), (W["k"], kT)]
        with nc.Block() as block:

            @block.scalar
            def _(act):
                st = Steps(act, act_step)
                lo, gl = pT[:, T_LO, :], pT[:, T_GL, :]
                nc.scalar.activation(lo[0:HD], lo[0:HD], ACT.Tanh).then_inc(lora_act, 1)
                nc.scalar.activation(gl, gl, ACT.Sigmoid).then_inc(lora_act, 1)
                for f in range(FT):
                    act.wait_ge(u_ready, 2 * f + 1)
                    nc.scalar.activation(lw[:, f, :], bank(env, f % 2), ACT.Sigmoid, bias=C2["w0"][:, f : f + 1]).then_inc(sig_done, 1)
                    act.wait_ge(u_ready, 2 * f + 2)
                    nc.scalar.activation(a[:, f, :], bank(env, 2 + f % 2), ACT.Sigmoid, bias=C2["a0"][:, f : f + 1]).then_inc(sig_done, 1)
                for f in range(FT):
                    nc.scalar.activation(kkn[:, f, :], k[:, f, :], ACT.Square, scale=C2["k_k"][:, f : f + 1]).then_inc(sq_done, 1)
                for f in range(FT):
                    act.wait_ge(g_ready, f + 1)
                    nc.scalar.copy(W["g"][:, f, :], bank(env, f % 2)).then_inc(g_out, 1)
                for f in range(FT):
                    act.wait_ge(norm_ready, f + 1)
                    nc.scalar.activation(pin[:, f, :], bank(env, 4 + f), ACT.Sqrt).then_inc(norm_out, 1)
                act.wait_ge(cum_ready, 1)
                nc.scalar.activation(inv, cum, ACT.Exp, scale=-1.0).then_inc(exp_done, 1)
                act.wait_ge(cum_ready, 2)
                nc.scalar.activation(pex, pex, ACT.Exp).then_inc(exp_done, 1)
                act.wait_ge(cum_ready, 3)
                nc.scalar.activation(pin[:], cum, ACT.Exp).then_inc(exp_done, 1)
                for n in range(3 * TX):
                    act.wait_ge(turned, n + 1)
                    nc.scalar.copy(naturals[n // TX][0][:, n % TX, :], bank(env, n % 4)).then_inc(turned_out, 1)

            @block.tensor
            def _(pe):
                pe.wait_ge(lora_act, 1)
                for f in range(FT):
                    if f >= 2:
                        pe.wait_ge(sig_done, 2 * (f - 1))
                    for j, rows in enumerate((slice(0, HD), slice(HD, P))):
                        nc.tensor.matmul(
                            bank(env, 2 * j + f % 2), C2["lora"][rows, f * P : (f + 1) * P], pT[rows, T_LO, :], start=True, stop=True
                        ).then_inc(u_ready, 1)
                pe.wait_ge(lora_act, 2)
                pe.wait_ge(sig_done, 2 * FT)
                for f in range(FT):
                    if f >= 2:
                        pe.wait_ge(g_out, f - 1)
                    nc.tensor.matmul(bank(env, f % 2), C2["g2"][:, f * P : (f + 1) * P], pT[:, T_GL, :], start=True, stop=True).then_inc(g_ready, 1)
                for f in range(FT):
                    pe.wait_ge(sq_done, f + 1)
                    nc.tensor.matmul(bank(env, 4 + f), C2["pair"][:], kkn[:, f, :], start=True, stop=True).then_inc(norm_ready, 1)
                pe.wait_ge(g_out, FT)
                for n in range(3 * TX):
                    if n >= 4:
                        pe.wait_ge(turned_out, n - 3)
                    src, t = naturals[n // TX][1], n % TX
                    if n == TX:
                        pe.wait_ge(b_ready, 1)
                    if n == 2 * TX:
                        pe.wait_ge(k_ready, 1)
                    for f in range(FT):
                        m = nc.tensor.transpose(bank(env, n % 4, P, f * P), src[:, f, t * P : (t + 1) * P], env.ident[:])
                    m.then_inc(turned, 1)
                pe.wait_ge(rk_ready, 1)
                pe.wait_ge(norm_out, FT)
                for t in range(TX):
                    for f in range(FT):
                        m = nc.tensor.matmul(
                            bank(env, 4, SSD_HEADS, t * SSD_HEADS), lw[:, f, t * P : (t + 1) * P], C2["r_k"][:, f, :], start=f == 0, stop=f == FT - 1)
                m.then_inc(bonus_ready, 1)

            @block.gpsimd
            def _(pool):
                pool.wait_ge(kp_ready, 1)
                nc.gpsimd.tensor_tensor(lw, r, kT, ALU.mult).then_inc(rk_ready, 1)
                pool.wait_ge(rk_ready, 1)
                pool.wait_ge(exp_done, 3)
                nc.gpsimd.tensor_tensor(r, r, pin[:], ALU.mult).then_inc(r_done, 1)

            @block.vector
            def _(dve):
                st = Steps(dve, step)
                st.link(nc.vector.tensor_scalar(less_ka[:], C2["k_a"][:], -1.0, 1.0, ALU.mult, ALU.add))
                for f in range(FT):
                    dve.wait_ge(sig_done, 2 * f + 1)
                    st.link(nc.vector.tensor_scalar(lw[:, f, :], lw[:, f, :], -RW_DECAY_SCALE, None, ALU.mult))
                    m = nc.vector.tensor_tensor_scan(cum[:, f, :], C2["reset"][:], lw[:, f, :], 0.0, ALU.mult, ALU.add)
                    if f < FT - 1:
                        st.link(m)
                m.then_inc(cum_ready, 1)
                dve.wait_ge(cum_ready, 1)
                nc.vector.tensor_tensor(pex, cum, lw, ALU.subtract).then_inc(cum_ready, 1)
                dve.wait_ge(norm_out, FT)
                st.link(nc.vector.tensor_scalar(pin[:], pin[:], 1e-12, None, ALU.max))
                st.link(nc.vector.reciprocal(pin[:], pin[:]))
                for f in range(FT):
                    m = nc.vector.scalar_tensor_tensor(kkn[:, f, :], k[:, f, :], C2["k_k"][:, f : f + 1], pin[:, f, :], ALU.mult, ALU.mult)
                    if f < FT - 1:
                        st.inc(m)
                m.then_inc(cum_ready, 1)
                dve.wait_ge(cum_ready, 3)
                dve.wait_ge(step, st.n)
                dve.wait_ge(sig_done, 2 * FT)
                st.link(nc.vector.tensor_tensor(bT, kkn[:], a[:], ALU.mult))
                dve.wait_ge(exp_done, 1)
                nc.vector.tensor_tensor(bT, bT, inv, ALU.mult).then_inc(b_ready, 1)
                for f in range(FT):
                    st.link(nc.vector.tensor_scalar(a[:, f, :], a[:, f, :], C2["k_a"][:, f : f + 1], less_ka[:, f : f + 1], ALU.mult, ALU.add))
                nc.vector.tensor_tensor(kT, k, a[:], ALU.mult).then_inc(kp_ready, 1)
                dve.wait_ge(exp_done, 2)
                dve.wait_ge(kp_ready, 1)
                st.link(nc.vector.scalar_tensor_tensor(k, kkn[:], -1.0, pex, ALU.mult, ALU.mult))
                dve.wait_ge(rk_ready, 1)
                nc.vector.tensor_tensor(kT, kT, inv, ALU.mult).then_inc(k_ready, 1)
                dve.wait_ge(exp_done, 3)
                ends = pin[:].rearrange("p f (c j) -> p f c j", j=RW_CHUNK)[:, :, :, RW_CHUNK - 1]
                st.link(nc.vector.tensor_copy(W["end"][:], ends))
                dve.wait_ge(bonus_ready, 1)
                st.link(nc.vector.tensor_copy(W["bonus"][:], bank(env, 4, TH)))


def stage_rwkv_matrices(env, pT, W):
    nc, C2 = env.nc, env.C2
    batches = [(t, q) for t in range(TX) for q in range(2)]
    with ExitStack() as ctx:
        sem = lambda name: env.semaphore("rwm_" + name)
        product, masked, kept, values, values_out = sem("product"), sem("masked"), sem("kept"), sem("values"), sem("values_out")
        AM = [env.WR[b][:].rearrange("p k n -> p (k n)")[:, 0 : GH * 4 * P].rearrange("p (h m l) -> p h m l", h=GH, m=4) for b in range(2)]
        with nc.Block() as block:

            @block.tensor
            def _(pe):
                def products(n):
                    t, q = batches[n]
                    tok = slice(t * P, (t + 1) * P)
                    for hl in range(GH):
                        h = q * GH + hl
                        f, rows = h // 2, slice((h % 2) * HD, (h % 2 + 1) * HD)
                        if n:
                            pe.wait_ge(masked, (n - 1) * GH + hl + 1)
                        ra = pT[rows, T_R + f : T_K + f + 1 : FT, tok]
                        nc.tensor.matmul(bank(env, hl, 2 * P), pT[rows, f, tok], ra, start=True, stop=True)
                        nc.tensor.matmul(bank(env, hl, 2 * P, 2 * P), pT[rows, FT + f, tok], ra, start=True, stop=True).then_inc(product, 1)

                def times_v(n):
                    t, q = batches[n]
                    pe.wait_ge(masked, (n + 1) * GH)
                    if n >= 2:
                        pe.wait_ge(values_out, 2 * (n - 1))
                    for m in (3, 2):
                        for hl in range(GH):
                            c = (q * GH + hl) * HD
                            x = nc.tensor.matmul(
                                bank(env, 4 + 2 * (n % 2) + (3 - m), HD, hl * HD), AM[n % 2][:, hl, m, :], W["v"][:, t, c : c + HD], start=True, stop=True)
                        x.then_inc(values, 1)

                products(0)
                for n in range(len(batches)):
                    if n + 1 < len(batches):
                        products(n + 1)
                    times_v(n)

            @block.vector
            def _(dve):
                for n in range(len(batches)):
                    if n >= 2:
                        dve.wait_ge(values, 2 * (n - 1))
                        dve.wait_ge(kept, 2 * (n - 1))
                    for hl in range(GH):
                        dve.wait_ge(product, n * GH + hl + 1)
                        nc.vector.tensor_tensor(AM[n % 2][:, hl], bank(env, hl).rearrange("p (m l) -> p m l", m=4), C2["within"][:], ALU.mult).then_inc(masked, 1)

            @block.gpsimd
            def _(pool):
                for n, (t, q) in enumerate(batches):
                    pool.wait_ge(masked, (n + 1) * GH)
                    heads = slice(q * GH, (q + 1) * GH)
                    nc.gpsimd.tensor_copy(W["rb"][:, t, heads, :], AM[n % 2][:, :, 0, :]).then_inc(kept, 1)
                    nc.gpsimd.tensor_copy(W["inv"][:, t, heads, :], AM[n % 2][:, :, 1, :]).then_inc(kept, 1)

            @block.scalar
            def _(act):
                for n, (t, q) in enumerate(batches):
                    for m, out in enumerate((W["akv"], W["rkv"])):
                        act.wait_ge(values, 2 * n + m + 1)
                        nc.scalar.copy(out[:, t, q * GH * HD : (q + 1) * GH * HD], bank(env, 4 + 2 * (n % 2) + m, GH * HD)).then_inc(values_out, 1)


def stage_rwkv_inverse(env, W):
    nc, C2 = env.nc, env.C2
    batches = [(t, q) for t in range(TX) for q in range(2)]
    with ExitStack() as ctx:
        sem = lambda name: env.semaphore("rwi_" + name)
        cut, first, first_out, second, third, x_out, xt_out = ([sem(f"{n}{b}") for b in range(2)] for n in (
            "cut", "first", "first_out", "second", "third", "x_out", "xt_out"))
        flat = [env.WR[b][:].rearrange("p k n -> p (k n)") for b in range(2)]
        part = lambda b, j: flat[b][:, j * GH * P : (j + 1) * GH * P].rearrange("p (h l) -> p h l", h=GH)
        ident4 = env.ident[:].unsqueeze(1).to_broadcast([P, GH, P])
        steps = [(p, lv) for p in range(len(batches) // 2) for lv in range(LEVELS)]
        nT = lambda b, n: part(b, n % 2)
        t1 = lambda b: part(b, 2)
        x = lambda b: part(b, 3)
        xt = lambda b: part(b, 4)

        def home(b, p):
            t, q = batches[2 * p + b]
            return W["inv"][:, t, q * GH : (q + 1) * GH, :]

        bk = lambda b, j: bank(env, 3 * b + j).rearrange("p (h l) -> p h l", h=GH)
        with nc.Block() as block:

            @block.gpsimd
            def _(pool):
                for n, (p, lv) in enumerate(steps):
                    for b in range(2):
                        if n >= 2:
                            pool.wait_ge(first[b], n - 1)
                        nc.gpsimd.tensor_tensor(nT(b, n), home(b, p), C2["level"][:, lv, :].unsqueeze(1).to_broadcast([P, GH, P]), ALU.mult).then_inc(cut[b], 1)

            @block.tensor
            def _(pe):
                def one(b, n):
                    p, lv = steps[n]
                    pe.wait_ge(cut[b], n + 1)
                    if n:
                        pe.wait_ge(x_out[b], n)
                        pe.wait_ge(xt_out[b], n)
                        pe.wait_ge(first_out[b], n)
                    for h in range(GH):
                        m = nc.tensor.matmul(bk(b, 0)[:, h], nT(b, n)[:, h], env.ident[:] if lv == 0 else x(b)[:, h], start=True, stop=True)
                    m.then_inc(first[b], 1)

                def two(b, n):
                    p, lv = steps[n]
                    pe.wait_ge(first_out[b], n + 1)
                    for h in range(GH):
                        m = nc.tensor.matmul(bk(b, 1)[:, h], env.ident[:] if lv == 0 else xt(b)[:, h], t1(b)[:, h], start=True, stop=True)
                    m.then_inc(second[b], 1)
                    for h in range(GH):
                        m = nc.tensor.matmul(bk(b, 2)[:, h], t1(b)[:, h], env.ident[:] if lv == 0 else xt(b)[:, h], start=True, stop=True)
                    m.then_inc(third[b], 1)

                for n in range(len(steps)):
                    for b in range(2):
                        one(b, n)
                    for b in range(2):
                        two(b, n)

            @block.scalar
            def _(act):
                for n in range(len(steps)):
                    for b in range(2):
                        act.wait_ge(first[b], n + 1)
                        if n:
                            act.wait_ge(third[b], n)
                        nc.scalar.copy(t1(b), bk(b, 0)).then_inc(first_out[b], 1)

            @block.vector
            def _(dve):
                for n, (p, lv) in enumerate(steps):
                    for b in range(2):
                        dve.wait_ge(second[b], n + 1)
                        nc.vector.tensor_tensor(x(b), bk(b, 1), ident4 if lv == 0 else x(b), ALU.add).then_inc(x_out[b], 1)
                        dve.wait_ge(third[b], n + 1)
                        dve.wait_ge(cut[b], n + 1)
                        out = home(b, p) if lv == LEVELS - 1 else xt(b)
                        nc.vector.tensor_tensor(out, bk(b, 2), ident4 if lv == 0 else xt(b), ALU.add).then_inc(xt_out[b], 1)


def stage_rwkv_scan(env, pT, W, y):
    nc, C2 = env.nc, env.C2
    with ExitStack() as ctx:
        sem = lambda name: env.semaphore("rwk_" + name)
        state, new = (pT[:, FT + j, :].rearrange("p (f n) -> p f n", f=FT) for j in range(2))
        rhs, U = pT[:, FT + 2, :], pT[:, FT + 3, :]
        zeroed, as_ready, rhs_ready, u_ready, u_out, y_ready, y_out, new_ready, state_ready, step = (
            sem("zeroed"), sem("as"), sem("rhs"), sem("u"), sem("u_out"), sem("y"), sem("y_out"), sem("new"), sem("state"), sem("step"))
        with nc.Block() as block:

            @block.sync
            def _(sp):
                for s in range(2):
                    load_weights(env, sp, s, env.A["w_out_2"].rearrange("(k p) n -> p k n", p=P)[:, :, s * BANK : (s + 1) * BANK])

            @block.tensor
            def _(pe):
                for c in range(CHUNKS):
                    t, half = c // 2, slice((c % 2) * HD, (c % 2 + 1) * HD)
                    tok = slice(t * P, (t + 1) * P)
                    pe.wait_ge(state_ready, c + 1)
                    for f in range(FT):
                        m = nc.tensor.matmul(bank(env, 0, P, f * P), pT[:, T_K + f, tok], state[:, f, :], start=True, stop=True)
                    m.then_inc(as_ready, 1)
                    pe.wait_ge(rhs_ready, c + 1)
                    for h in range(SSD_HEADS):
                        m = nc.tensor.matmul(bank(env, 1, HD, h * HD), W["inv"][:, t, h, :], rhs[:, h * HD : (h + 1) * HD], start=True, stop=True)
                    m.then_inc(u_ready, 1)
                    pe.wait_ge(u_out, c + 1)
                    for f in range(FT):
                        cols = slice(f * P, (f + 1) * P)
                        nc.tensor.matmul(bank(env, 4 + c % 2, P, f * P), W["b"][half, t, cols], U[half, cols], start=True, stop=False)
                        m = nc.tensor.matmul(bank(env, 4 + c % 2, P, f * P), W["k"][half, t, cols], W["v"][half, t, cols], start=False, stop=True)
                    m.then_inc(new_ready, 1)
                    if c >= 2:
                        pe.wait_ge(y_out, c - 1)
                    for f in range(FT):
                        nc.tensor.matmul(bank(env, 2 + c % 2, P, f * P), pT[:, T_R + f, tok], state[:, f, :], start=True, stop=False, skip_group_check=True)
                        for h in (2 * f, 2 * f + 1):
                            m = nc.tensor.matmul(
                                bank(env, 2 + c % 2, HD, h * HD), W["rb"][:, t, h, :], U[:, h * HD : (h + 1) * HD], start=False, stop=True, skip_group_check=True)
                    m.then_inc(y_ready, 1)

            @block.scalar
            def _(act):
                for c in range(CHUNKS):
                    act.wait_ge(u_ready, c + 1)
                    if c:
                        act.wait_ge(y_ready, c)
                    nc.scalar.copy(U, bank(env, 1)).then_inc(u_out, 1)

            @block.vector
            def _(dve):
                st = Steps(dve, step)
                nc.vector.memset(state, 0.0).then_inc(state_ready, 1)
                for c in range(CHUNKS):
                    t, half = c // 2, slice((c % 2) * HD, (c % 2 + 1) * HD)
                    dve.wait_ge(as_ready, c + 1)
                    nc.vector.tensor_tensor(rhs, bank(env, 0), W["akv"][:, t, :], ALU.add).then_inc(rhs_ready, 1)
                    dve.wait_ge(new_ready, c + 1)
                    b = bank(env, 4 + c % 2).rearrange("p (f n) -> p f n", f=FT)
                    st.link(nc.vector.tensor_tensor(new, b, C2["pair"][:].unsqueeze(1).to_broadcast([P, FT, P]), ALU.mult))
                    st.link(nc.vector.tensor_tensor(new, new, state, ALU.add))
                    dve.wait_ge(y_ready, c + 1)
                    nc.vector.tensor_tensor(
                        state, new, W["end"][:, :, c : c + 1].to_broadcast([P, FT, P]), ALU.mult).then_inc(state_ready, 1)
                    nc.vector.tensor_tensor(y[half, t, :], env.PS[half, (2 + c % 2) * BANK : (3 + c % 2) * BANK], W["rkv"][half, t, :], ALU.add).then_inc(y_out, 1)


def stage_rwkv_post(env, W, y):
    nc, C2 = env.nc, env.C2
    with ExitStack() as ctx:
        sem = lambda name: env.semaphore("rwp_" + name)
        sb = lambda name, shape: ctx.enter_context(nc.sbuf_tensor("rwp_" + name, shape, F32))
        mean, var = sb("mean", [P, TH]), sb("var", [P, TH])
        sq = W["rb"][:].rearrange("p t h l -> p (t h l)")[:, 0 : TX * BW]
        step, var_ready, root_ready, bonus_ready, normed, turned, mixed = (
            sem("step"), sem("var"), sem("root"), sem("bonus"), sem("normed"), sem("turned"), sem("mixed"))
        heads = y.rearrange("p t (h d) -> p (t h) d", d=HD)
        wide = lambda v: v[:].unsqueeze(2).to_broadcast([P, TH, HD])
        rows = lambda v: v[:].unsqueeze(1).to_broadcast([P, TX, BW])
        with nc.Block() as block:

            @block.gpsimd
            def _(pool):
                v = W["v"][:].rearrange("p t (h d) -> p (t h) d", d=HD)
                nc.gpsimd.tensor_tensor(v, v, wide(W["bonus"]), ALU.mult).then_inc(bonus_ready, 1)

            @block.vector
            def _(dve):
                st = Steps(dve, step)
                st.link(nc.vector.tensor_reduce(mean[:], heads, AX.X, ALU.add))
                st.link(nc.vector.tensor_scalar(mean[:], mean[:], 1.0 / HD, None, ALU.mult))
                st.link(nc.vector.tensor_tensor(heads, heads, wide(mean), ALU.subtract))
                st.link(nc.vector.tensor_tensor(sq, y.rearrange("p t c -> p (t c)"), y.rearrange("p t c -> p (t c)"), ALU.mult))
                st.link(nc.vector.tensor_reduce(var[:], sq.rearrange("p (g d) -> p g d", d=HD), AX.X, ALU.add))
                nc.vector.tensor_scalar(var[:], var[:], 1.0 / HD, RWKV_GN_EPS, ALU.mult, ALU.add).then_inc(var_ready, 1)
                dve.wait_ge(root_ready, 1)
                st.link(nc.vector.reciprocal(var[:], var[:]))
                st.link(nc.vector.tensor_tensor(heads, heads, wide(var), ALU.mult))
                st.link(nc.vector.tensor_tensor(y, y, rows(C2["ln_w"]), ALU.mult))
                st.link(nc.vector.tensor_tensor(y, y, rows(C2["ln_b"]), ALU.add))
                dve.wait_ge(bonus_ready, 1)
                nc.vector.tensor_tensor(y, y, W["v"][:], ALU.add).then_inc(normed, 1)
                for f in range(FT):
                    dve.wait_ge(turned, f + 1)
                    nc.vector.tensor_tensor(env.HT[:, FT + f, :], bank(env, f), W["g"][:, f, :], ALU.mult).then_inc(mixed, 1)

            @block.scalar
            def _(act):
                act.wait_ge(var_ready, 1)
                nc.scalar.activation(var[:], var[:], ACT.Sqrt).then_inc(root_ready, 1)

            @block.tensor
            def _(pe):
                pe.wait_ge(normed, 1)
                for f in range(FT):
                    for t in range(TX):
                        m = nc.tensor.transpose(bank(env, f, P, t * P), y[:, t, f * P : (f + 1) * P], env.ident[:])
                    m.then_inc(turned, 1)


FF_CHUNKS = FF_T // 2
DOWN_EARLY = 16


def stage_ffn_up(env, fT, taps, conv_b, down_rest):
    nc, A = env.nc, env.A
    with ExitStack() as ctx:
        sem = lambda name: env.semaphore("ffu_" + name)
        sb = lambda name, shape: ctx.enter_context(nc.sbuf_tensor("ffu_" + name, shape, F32))
        yb = sb("y", [P, 2, 2, S])
        ready, based, conv_done, gated, done, step = sem("ready"), sem("based"), sem("conv"), sem("gated"), sem("done"), sem("step")
        base = [n - 16 for n in env.w_count]
        LOOPS = FF_CHUNKS // 2
        body = [(s, j) for s in range(2) for j in range(2)]
        with nc.Block() as block:

            @block.sync
            def _(sp):
                with sp.Fori(1, LOOPS) as i:
                    for s in range(2):
                        sp.wait_ge(ready, 4 * i + 2 * s - 2)
                        sp.dma_start(env.WR[s][:], A["ffn_up"][bass.ds(2 * i + s, 1)].rearrange("a p k n -> (a p) k n")).then_inc(env.w_loaded[s], 16)
                sp.wait_ge(ready, 4 * LOOPS - 2)
                sp.dma_start(env.WR[0][:], A["ffn_up"][FF_CHUNKS - 1]).then_inc(env.w_loaded[0], 16)
                env.w_count[0] += 16 * LOOPS
                env.w_count[1] += 16 * (LOOPS - 1)
                for s, done in ((1, 4 * LOOPS), (0, 4 * LOOPS + 2)):
                    sp.wait_ge(ready, done)
                    source, tiles = down_rest[s]
                    sp.dma_start(env.WR[s][:].rearrange("p k n -> p (k n)")[:, 0 : tiles * D].rearrange("p (k n) -> p k n", n=D), source).then_inc(
                        env.w_loaded[s], 16)
                    env.w_count[s] += 16

            @block.tensor
            def _(pe):
                def pair(s, j, n, q, wait):
                    if wait is not None:
                        pe.wait_ge(conv_done, wait)
                    for half in range(2):
                        for k in range(KD):
                            c = (2 * j + half) * P
                            m = nc.tensor.matmul(bank(env, 2 * q + half), env.WR[s][:, k, c : c + P], env.HT[:, k, :], start=k == 0, stop=k == KD - 1)
                    m.then_inc(ready, 1)

                with pe.Fori(0, LOOPS) as i:
                    for q, (s, j) in enumerate(body):
                        if j == 0:
                            pe.wait_ge(env.w_loaded[s], base[s] + 16 + 16 * i)
                        pair(s, j, 4 * i + q, q, 4 * i + max(q - 3, 0))
                pe.wait_ge(env.w_loaded[0], base[0] + 16 + 16 * LOOPS)
                for j in range(2):
                    pair(0, j, 4 * LOOPS + j, j, 4 * LOOPS + j - 3)

            def conv_scalar(n, q):
                for half in range(2):
                    tile = taps[:, half, bass.ds(n, 1), 2:3].rearrange("p a b -> p (a b)")
                    nc.scalar.activation(
                        yb[:, q % 2, half, :], bank(env, 2 * q + half), ACT.Identity, bias=conv_b[:, half, bass.ds(n, 1)], scale=tile).then_inc(based, 1)

            @block.scalar
            def _(act):
                def pair(n, q, wait):
                    act.wait_ge(ready, n + 1)
                    act.wait_ge(done, wait)
                    conv_scalar(n, q)
                    act.wait_ge(conv_done, n + 1)
                    nc.scalar.activation(yb[:, q % 2, 0, :], yb[:, q % 2, 0, :], ACT.Silu).then_inc(gated, 1)

                with act.Fori(0, LOOPS) as i:
                    for q in range(4):
                        pair(4 * i + q, q, 4 * i + max(q - 1, 0))
                for q in range(2):
                    pair(4 * LOOPS + q, q, 4 * LOOPS + q - 1)

            @block.vector
            def _(dve):
                def conv(n, q, st):
                    dve.wait_ge(based, 2 * n + 2)
                    for back in (1, 2):
                        for half in range(2):
                            tap = taps[:, half, bass.ds(n, 1), 2 - back : 3 - back].rearrange("p a b -> p (a b)")
                            out = yb[:, q % 2, half, back:S]
                            m = nc.vector.scalar_tensor_tensor(out, bank(env, 2 * q + half, S - back), tap, out, ALU.mult, ALU.add)
                            if back == 1:
                                st.inc(m)
                        if back == 1:
                            dve.wait_ge(step, st.base + st.n)
                    m.then_inc(conv_done, 1)

                def product(n, q):
                    dve.wait_ge(gated, n + 1)
                    dve.wait_ge(conv_done, n + 1)
                    out = fT[:, bass.ds(n, 1), :].rearrange("p a t -> p (a t)")
                    nc.vector.tensor_tensor(out, yb[:, q % 2, 0, :], yb[:, q % 2, 1, :], ALU.mult).then_inc(done, 1)

                with dve.Fori(0, LOOPS) as i:
                    st = Steps(dve, step, 8 * i)
                    for q in range(4):
                        conv(4 * i + q, q, st)
                        product(4 * i + q, q)
                st = Steps(dve, step, 8 * LOOPS)
                for q in range(2):
                    conv(4 * LOOPS + q, q, st)
                    product(4 * LOOPS + q, q)


ROWS2 = ("dt_bias", "a_log", "ssd_d", "ln_w", "ln_b")
SHAPES2 = {
    "upto": [P, P], "ones": [P, P], "pair": [P, P], "reset": [P, S], "within": [P, 4, P], "level": [P, LEVELS, P],
    "lora": [P, BW], "g2": [P, BW], "ssd_taps": [P, 8, 4], "ssd_conv_b": [P, 8], "mu": [P, RW_TILES],
    "w0": [P, FT], "a0": [P, FT], "k_k": [P, FT], "k_a": [P, FT], "r_k": [P, FT, SSD_HEADS], "ssd_norm": [P, FT],
    "dt_bias": [P, TH], "a_log": [P, TH], "ssd_d": [P, BW], "ln_w": [P, BW], "ln_b": [P, BW],
}


def layer_second(env, upto):
    nc, A = env.nc, env.A
    pre = lambda k: env.pre2[:, k : k + 1]
    with ExitStack() as block2:
        sb2 = lambda name, shape: block2.enter_context(nc.sbuf_tensor("b2_" + name, shape, F32))
        env.HT = sb2("turned", [P, KD, S])
        gates, env.pre2, pre_ffn = sb2("gates", [P, 2, D]), sb2("pre_mix", [P, KD]), sb2("pre_ffn", [P, KD])
        rows_in = block2.enter_context(nc.semaphore("b2_rows_in"))
        with nc.Block() as block:

            @block.scalar
            def _(act):
                act.dma_start(env.pre2[:], A["pre_mix"]).then_inc(rows_in, 16)
                act.dma_start(pre_ffn[:], A["pre_ffn"]).then_inc(rows_in, 16)
                act.dma_start(gates[:, 0, :], A["post_mix"].partition_broadcast(P)).then_inc(rows_in, 16)
                act.dma_start(gates[:, 1, :], A["post_ffn"].partition_broadcast(P)).then_inc(rows_in, 16)
                act.wait_ge(rows_in, 64)

        stage_norm(env, "norm2", [(env.X, TX, 0, pre, None)], [A["w_in_2"][0], A["w_in_2"][1]])
        with ExitStack() as mix:
            sb = lambda name, shape: mix.enter_context(nc.sbuf_tensor("mix_" + name, shape, F32))
            env.C2 = {n: sb(n, s) for n, s in SHAPES2.items()}
            pT = sb("pT", [P, 22, S])
            with ExitStack() as ssd:
                sbs = lambda name, shape: ssd.enter_context(nc.sbuf_tensor("ssd_" + name, shape, F32))
                zN, dtN = sbs("z", [P, TX, BW]), sbs("dt_raw", [P, TH])
                stage_second_proj(env, pT, zN, dtN)
                V = {n: sbs(n, [P, TH]) for n in ("dt", "a", "acs", "dstate", "eacs", "etot")}
                V |= {"conv": sbs("conv", [P, 8, S]), "xs": sbs("xs", [P, TX, BW]), "B": sbs("B", [P, TX, 2 * SSD_STATE]), "skip": sbs("skip", [P, TX, BW])}
                V |= {"xdt": pT[:, 0:FT, :], "xds": pT[:, FT : 2 * FT, :]}
                stage_ssd_prep(env, pT, dtN, V)
                stage_ssd(env, V, zN)
            stage_rwkv_shift(env, pT)
            W = {n: sb(n, [P, TX, BW]) for n in ("v", "b", "k")}
            W |= {"g": sb("g", [P, FT, S]), "end": sb("end", [P, FT, CHUNKS]), "bonus": sb("bonus", [P, TH])}
            stage_rwkv_features(env, pT, W)
            W |= {"inv": sb("inv", [P, TX, SSD_HEADS, P]), "rb": sb("rb", [P, TX, SSD_HEADS, P])}
            W |= {"akv": pT[:, T_V : T_V + FT, :], "rkv": env.HT[:, FT:KD, :]}
            stage_rwkv_matrices(env, pT, W)
            stage_rwkv_inverse(env, W)
            y = pT[:, 0:FT, :]
            stage_rwkv_scan(env, pT, W, y)
            stage_rwkv_post(env, W, y)
        ring_out(env, "out2", [(env.X, TX, 0, gates[:, 0, :])])
        if upto < 3:
            return
        with ExitStack() as ffn:
            sb = lambda name, shape: ffn.enter_context(nc.sbuf_tensor("ffn_" + name, shape, F32))
            down_rows = A["ffn_down"].rearrange("(k p) n -> p k n", p=P)
            w_down = sb("down", [P, DOWN_EARLY, D])
            ring_tiles = KD * BANK // D
            split = DOWN_EARLY + ring_tiles
            down_rest = {1: (down_rows[:, DOWN_EARLY:split, :], ring_tiles), 0: (down_rows[:, split:FF_T, :], FF_T - split)}
            taps, conv_b = sb("taps", [P, 2, FF_T, 3]), sb("conv_b", [P, 2, FF_T])
            down_in, small_in = ffn.enter_context(nc.semaphore("ffn_down_in")), ffn.enter_context(nc.semaphore("ffn_small_in"))
            with nc.Block() as block:

                @block.scalar
                def _(act):
                    act.dma_start(taps[:], A["ffn_taps"]).then_inc(small_in, 16)
                    act.dma_start(conv_b[:], A["ffn_conv_b"]).then_inc(small_in, 16)
                    act.wait_ge(small_in, 32)

            stage_norm(env, "norm3", [(env.X, TX, 0, lambda k: pre_ffn[:, k : k + 1], None)], [A["ffn_up"][0], A["ffn_up"][1]])
            fT = sb("fT", [P, FF_T, S])
            with nc.Block() as block:

                @block.sync
                def _(sp):
                    sp.dma_start(w_down[:], down_rows[:, 0:DOWN_EARLY, :]).then_inc(down_in, 16)

            stage_ffn_up(env, fT, taps, conv_b, down_rest)

            def down(k, h):
                if k < DOWN_EARLY:
                    return w_down[:, k, h * BANK : (h + 1) * BANK]
                slot, tile = (1, k - DOWN_EARLY) if k < split else (0, k - split)
                return env.WR[slot][:, 2 * tile + h, :]

            loaded = [(0, down_in, 16), (DOWN_EARLY, env.w_loaded[1], env.w_count[1]), (split, env.w_loaded[0], env.w_count[0])]
            spare = env.HT[:].rearrange("p k t -> p (k t)")
            stage_out(
                env, "out3", [(env.X, TX, 0, gates[:, 1, :])], fT, FF_T, down, loaded,
                (spare[:, 0:D], spare[:, D : 3 * D].rearrange("p (b d) -> p b d", b=2)))


def build_program(nc, A, out, upto=99):
    env = Env()
    env.nc, env.A = nc, A
    env.stage_semaphores = []
    with ExitStack() as ctx:
        sb = lambda name, shape: ctx.enter_context(nc.sbuf_tensor(name, shape, F32))
        env.PS = ctx.enter_context(nc.psum_tensor("banks", [P, 8 * BANK], F32))
        env.X = sb("resid_x", [P, TX, D])
        env.ident = sb("identity", [P, P])
        env.gain = sb("gain", [P, 2, KD, 2])
        env.shift = sb("shift", [P, 2, KD, 2])
        env.neg_lam = sb("neg_lam", [P, 1])
        env.subln = sb("subln_col", [P, 1])
        env.WR = [sb(f"weight_ring{s}", [P, KD, BANK]) for s in range(2)]
        env.w_loaded = [ctx.enter_context(nc.semaphore(f"weights_loaded{s}")) for s in range(2)]
        env.w_count = [0, 0]
        env.w_out_half = lambda l, s: A["w_out"][l].rearrange("(k p) n -> p k n", p=P)[:, :, s * BANK : (s + 1) * BANK]
        gain = lambda l, r: lambda k: env.gain[:, l, k, r : r + 1]
        shift = lambda l, r: lambda k: env.shift[:, l, k, r : r + 1]
        with ExitStack() as first:
            env.CX = first.enter_context(nc.sbuf_tensor("resid_ctx", [P, TC, D], F32))
            env.HT = first.enter_context(nc.sbuf_tensor("turned", [P, KD, ST], F32))
            env.gate = first.enter_context(nc.sbuf_tensor("gate", [P, 3, D], F32))
            stage_modulation(env)
            with ExitStack() as layer:
                stage_norm(
                    env, "norm0", [(env.X, TX, 0, gain(0, 0), shift(0, 0)), (env.CX, TC, TX, gain(0, 1), shift(0, 1))],
                    [A["w_in_even"][0], A["w_in_even"][1]])
                pT = layer.enter_context(nc.sbuf_tensor("even_pT", [P, 7, FT, ST], F32))
                vN = layer.enter_context(nc.sbuf_tensor("even_v", [P, NT, BW], F32))
                stage_even_proj(env, pT, vN)
                stage_rope_conv(env, pT)
                with ExitStack() as att:
                    O = att.enter_context(nc.sbuf_tensor("diff_o", [P, NT, BW], F32))
                    stage_diff_attention(env, pT, vN, O)
                    stage_diff_post(env, pT, O)
            ring_out(env, "out0", [(env.X, TX, 0, env.gate[:, 0, :]), (env.CX, TC, TX, env.gate[:, 1, :])])
            if upto >= 1:
                layer_odd(env, gain, shift)
            env.clear_semaphores()
        if upto >= 2:
            layer_second(env, upto)
        stored = ctx.enter_context(nc.semaphore("stored"))
        with nc.Block() as block:

            @block.sync
            def _(sp):
                sp.dma_start(out.rearrange("b (t p) d -> p (b t) d", p=P), env.X[:]).then_inc(stored, 16)
                sp.wait_ge(stored, 16)


def chunked(w, width=BANK):
    K, N = w.shape
    return np.ascontiguousarray(w.reshape(K // P, P, N // width, width).transpose(2, 1, 0, 3))


def columns(v, tile=P):
    return np.ascontiguousarray(v.reshape(-1, tile).T)


def rope_constants():
    nf = A_QK // 4
    inv = (np.float32(10000.0) ** (-np.arange(nf, dtype=np.float32) / np.float32(nf))).astype(np.float32)
    t = np.arange(S)
    pos = np.stack([t // GRID_W, t % GRID_W]).astype(np.float32)
    p = np.arange(P)
    e = p % (2 * nf)
    ang = (pos[(p % A_QK) // (2 * nf)] * inv[e % nf][:, None]).astype(np.float32).astype(np.float64)
    sign = np.where(e < nf, -1.0, 1.0)[:, None]
    cs = np.stack([np.cos(ang), sign * np.sin(ang)], 1)
    both = np.stack([cs * A_QK**-0.5, cs], 1).astype(np.float32)
    swap = np.zeros((P, P), np.float32)
    swap[np.where(e < nf, p + nf, p - nf), p] = 1.0
    return both, swap


def dft_constants():
    t = np.arange(S)
    f = np.arange(C_HD)
    at = 2 * np.pi * (np.outer(t, t) % S) / S
    af = 2 * np.pi * (np.outer(f, f) % C_HD) / C_HD
    scale = 1.0 / np.sqrt(S * C_HD)
    token = np.stack([np.cos(at), np.sin(at)]).reshape(2, TX, P, S).transpose(2, 0, 1, 3)
    pair = np.eye(P // C_HD)
    feature = np.stack([np.kron(pair, np.cos(af)), -np.kron(pair, np.sin(af))]) * scale
    return np.ascontiguousarray(token, np.float32), np.ascontiguousarray(feature.transpose(1, 0, 2), np.float32)


def window_bias(rpb):
    cq, kc = np.arange(GRID_W)[:, None], np.arange(GRID_W)[None]
    first = np.clip(cq - NA_KW // 2, 0, GRID_W - NA_KW)
    inside = (kc >= first) & (kc < first + NA_KW)
    padded = np.concatenate([rpb, np.full(rpb.shape[:2] + (1,), -1e30, rpb.dtype)], -1)
    col = np.where(inside, kc - cq + NA_KW - 1, rpb.shape[-1])
    laid = padded[:, :, col].transpose(2, 0, 1, 3)
    both = np.concatenate([laid[:, :, 1 : BIAS_SLOTS + 1], laid[:, :, 0:BIAS_SLOTS]])
    return np.ascontiguousarray(both.reshape(P, C_HEADS, BIAS_SLOTS * GRID_W))


def second_constants():
    s, l = np.arange(P)[:, None], np.arange(P)[None]
    same = s // RW_CHUNK == l // RW_CHUNK
    incl, strict = same & (s <= l), same & (s < l)
    level = [(s // (2 * m) == l // (2 * m)) & (s // m % 2 == 0) & (l // m % 2 == 1) for m in (1 << j for j in range(LEVELS))]
    c = {
        "upto": s <= l, "ones": np.ones((P, P)), "pair": same,
        "reset": np.broadcast_to(np.arange(S) % RW_CHUNK != 0, (P, S)),
        "within": np.stack([incl, strict, incl, strict], 1), "level": np.stack(level, 1),
    }
    return {k: np.ascontiguousarray(v, np.float32) for k, v in c.items()}


def second_arrays(I):
    a = {"c2_" + k: v for k, v in second_constants().items()}
    w = I["w_in_2"][0]
    z, xbc, dt, rw = w[:, 0:512], w[:, 512:1536], w[:, 1536:1544], w[:, 1544:]
    r, w_lo, k, v, a_lo, g_lo = np.split(rw, np.cumsum([512, 64, 512, 512, 64]), 1)
    pad = np.zeros((D, BANK - 2 * P - SSD_HEADS), w.dtype)
    a["w_in_2"] = chunked(np.concatenate([xbc, r, k, v, w_lo, a_lo, g_lo, dt, pad, z], 1))
    mr, mw, mk, mv, ma, mg = np.split(I["rwkv_mu_2"][0], np.cumsum([512, 64, 512, 512, 64]))
    a["c2_mu"] = columns(np.concatenate([mr, mk, mv, mw, ma, mg]))
    a["c2_ssd_taps"] = I["ssd_conv_w_2"][0].reshape(4, 8, P).transpose(2, 1, 0)
    a["c2_ssd_conv_b"] = columns(I["ssd_conv_b_2"][0])
    for name, key in (("w0", "rwkv_w0"), ("a0", "rwkv_a0"), ("k_k", "rwkv_k_k"), ("k_a", "rwkv_k_a"), ("ssd_norm", "ssd_norm")):
        a["c2_" + name] = columns(I[key + "_2"][0])
    a["c2_lora"] = np.concatenate([I["rwkv_w2_2"][0], I["rwkv_a2_2"][0]])
    a["c2_g2"] = I["rwkv_g2_2"][0]
    rk = np.zeros((SSD_HEADS, HD, SSD_HEADS), np.float32)
    rk[np.arange(SSD_HEADS), :, np.arange(SSD_HEADS)] = I["rwkv_r_k_2"][0]
    a["c2_r_k"] = rk.reshape(FT, P, SSD_HEADS).transpose(1, 0, 2)
    a["c2_dt_bias"], a["c2_a_log"] = np.tile(I["ssd_dt_bias_2"][0], TX), np.tile(I["ssd_a_log_2"][0], TX)
    a["c2_ssd_d"] = np.repeat(I["ssd_d_2"][0], HD)
    a["c2_ln_w"], a["c2_ln_b"] = I["rwkv_ln_w_2"][0], I["rwkv_ln_b_2"][0]
    a["w_out_2"] = I["w_out_2"][0]
    a["pre_mix"], a["pre_ffn"] = columns(I["pre_mix_norm_2"][0]), columns(I["pre_ffn_norm_2"][0])
    a["post_mix"], a["post_ffn"] = I["post_mix_norm_2"][0], I["post_ffn_norm_2"][0]
    up = I["ffn_w_up_2"][0].reshape(D, 2, FF_T, P).transpose(0, 2, 1, 3).reshape(D, 2 * D_FF)
    a["ffn_up"] = chunked(up)
    a["ffn_taps"] = I["ffn_conv_w_2"][0].reshape(3, 2, FF_T, P).transpose(3, 1, 2, 0)
    a["ffn_conv_b"] = I["ffn_conv_b_2"][0].reshape(2, FF_T, P).transpose(2, 0, 1)
    a["ffn_down"] = I["ffn_w_down_2"][0]
    return a


def host_arrays(I):
    a = {}
    a["x"], a["ctx"] = I["x"][0], I["ctx"][0]
    a["cond"] = np.ascontiguousarray(np.stack([I["c"][0], I["c_ctx"]], -1).reshape(KD, P, 2).transpose(1, 0, 2))
    a["w_mod"] = np.concatenate([chunked(I["w_mod"][l]) for l in range(2)])
    a["b_mod"] = I["b_mod"].reshape(-1)
    a["sel"] = np.ascontiguousarray(np.broadcast_to(np.eye(2, dtype=np.float32)[:, :, None], (2, 2, P)))
    a["norm_pre"] = np.ascontiguousarray(np.broadcast_to(I["norm_pre"].reshape(2, KD, P).transpose(2, 0, 1)[..., None], (P, 2, KD, 2)))
    a["norm_post"] = I["norm_post"]
    a["lam_a"] = I["lam_a"][0]
    a["ident"] = np.eye(P, dtype=np.float32)
    a["subln"] = np.ascontiguousarray(np.tile(I["subln_a"][0], 2)[:, None])
    a["w_in_even"] = chunked(I["w_in_even"][0])[[0, 1, 3, 7, 5, 6, 4, 2]]
    a["rope"], a["rope_swap"] = rope_constants()
    a["conv_b"] = np.ascontiguousarray(I["conv_b"][0].reshape(3, FT, P).transpose(2, 1, 0))
    a["w_out"] = I["w_out"]
    a["w_in_odd"] = chunked(I["w_in_odd"][0])[[0, 3, 5, 1, 2, 4]]
    a["dft_t"], a["dft_f"] = dft_constants()
    a |= second_arrays(I)
    a["na_bias"] = window_bias(I["rpb_c"][0])
    return a


UPTO = 99


def kernel(**inputs):
    from concourse import bacc
    from concourse.bass_utils import run_bass_kernel_spmd

    inputs = {k: np.asarray(v) for k, v in inputs.items()}
    arrays = {"in_" + k: np.ascontiguousarray(v) for k, v in host_arrays(inputs).items()}
    nc = bacc.Bacc("TRN2", target_bir_lowering=False, num_devices=1)
    A = {k[3:]: nc.dram_tensor(k, v.shape, mybir.dt.from_np(v.dtype), kind="ExternalInput").ap() for k, v in arrays.items()}
    out = nc.dram_tensor("out", (1, S, D), F32, kind="ExternalOutput").ap()
    build_program(nc, A, out, UPTO)
    r = run_bass_kernel_spmd(nc, [arrays], core_ids=[0])
    return r.results[0]["out"]
```

```python
from contextlib import ExitStack

import concourse.bass as bass
import numpy as np
from concourse import mybir

F32 = mybir.dt.float32
F32R = mybir.dt.float32r
ALU = mybir.AluOpType
ACT = mybir.ActivationFunctionType
AX = mybir.AxisListType

P = 128
D = 1024
KD = D // P
S = 512
L = 256
TX = S // P
TC = L // P
NT = TX + TC
ST = S + L
BW = 512
FT = BW // P
EPS = 1e-6
BANK = 512

A_HEADS = 8
A_QK = 32
A_V = 64
LAM_INIT0 = 0.2
C_HEADS = 8
C_HD = 64
GRID_W = 64
ROWS = S // GRID_W
NA_KW = 16
BIAS_SLOTS = 2 * ROWS - 2

SSD_HEADS = 8
SSD_STATE = 128
RW_CHUNK = 64
RW_DECAY_SCALE = float(np.exp(-0.5))
RWKV_GN_EPS = 64e-5
D_FF = 2816
FF_T = D_FF // P


class Steps:

    def __init__(self, eng, sem, base=0):
        self.eng, self.sem, self.base, self.n = eng, sem, base, 0

    def inc(self, instruction):
        self.n += 1
        instruction.then_inc(self.sem, 1)
        return self.n

    def link(self, instruction):
        self.inc(instruction)
        self.eng.wait_ge(self.sem, self.base + self.n)


class Env:

    def split_operands(self, scope, name, tokens):
        new = lambda n, shape: scope.enter_context(self.nc.sbuf_tensor(f"{name}_{n}", shape, F32R))
        self.parts = [new(f"weight_parts{s}", [P, 2, KD, CW]) for s in range(2)]
        self.tok = new("token_parts", [P, 2, KD, tokens])

    def semaphore(self, name):
        handle = self.nc.alloc_semaphore(name)
        self.stage_semaphores.append(handle)
        return handle

    def clear_semaphores(self):
        with self.nc.Block() as block:

            @block.gpsimd
            def _(pool):
                for handle in self.stage_semaphores:
                    pool.sem_clear(handle)

        for handle in self.stage_semaphores:
            self.nc.release_semaphore(handle)
        self.stage_semaphores = []


def bank(env, b, width=BANK, at=0):
    return env.PS[:, b * BANK + at : b * BANK + at + width]


CW = 256
PASSES = ((0, 0), (0, 1), (1, 0))


class Ring:

    def __init__(self, env, name, source, chunks):
        self.env, self.nc, self.source, self.chunks = env, env.nc, source, chunks
        self.hi_done, self.lo_done = env.semaphore(name + "_hi_done"), env.semaphore(name + "_lo_done")
        self.base = [n - 16 for n in env.raw_count]
        env.raw_count[0] += 16 * ((chunks - 1) // 2)
        env.raw_count[1] += 16 * (chunks // 2 - 1)

    @staticmethod
    def prefetch(env, eng, source):
        for s in range(2):
            eng.dma_start(env.raw[s][:], source[s]).then_inc(env.raw_in[s], 16)
            env.raw_count[s] += 16

    def load_rest(self, sp):
        def load(c, s):
            sp.wait_ge(self.lo_done, c - 1)
            src = self.source[bass.ds(c, 1)].rearrange("a p k n -> (a p) k n")
            sp.dma_start(self.env.raw[s][:], src).then_inc(self.env.raw_in[s], 16)

        if self.chunks >= 4:
            with sp.Fori(1, self.chunks // 2) as i:
                for s in range(2):
                    load(2 * i + s, s)
        if self.chunks % 2:
            load(self.chunks - 1, 0)

    def prefetch_next(self, sp, source):
        for s in range(2):
            sp.wait_ge(self.lo_done, self.chunks - (self.chunks - 1 - s) % 2)
            sp.dma_start(self.env.raw[s][:], source[s]).then_inc(self.env.raw_in[s], 16)
            self.env.raw_count[s] += 16

    def hi(self, act, i, s, freed=None):
        act.wait_ge(self.env.raw_in[s], self.base[s] + 16 + 16 * i)
        if freed is not None:
            act.wait_ge(*freed)
        self.nc.scalar.copy(self.env.parts[s][:, 0], self.env.raw[s][:]).then_inc(self.hi_done, 1)

    def all_lo(self, pool):
        def lo(c, s):
            pool.wait_ge(self.hi_done, c + 1)
            env = self.env
            self.nc.gpsimd.tensor_tensor(env.parts[s][:, 1], env.raw[s][:], env.parts[s][:, 0].bitcast(F32), ALU.subtract).then_inc(
                self.lo_done, 1)

        with pool.Fori(0, self.chunks // 2) as i:
            for s in range(2):
                lo(2 * i + s, s)
        if self.chunks % 2:
            lo(self.chunks - 1, 0)

    def transposed(self, s, f, out, tokens, cols=P):
        env = self.env
        n = 0
        for k in range(KD):
            for wp, tp in PASSES:
                w = env.parts[s][:, wp, k, f * P : f * P + cols]
                for o, (a, b) in zip(out, tokens):
                    m = self.nc.tensor.matmul(o, w, env.tok[:, tp, k, a:b], start=n == 0, stop=n == 3 * KD - 1)
                n += 1
        return m

    def natural(self, s, t, out):
        env = self.env
        n = 0
        for k in range(KD):
            for wp, tp in PASSES:
                m = self.nc.tensor.matmul(
                    out, env.tok[:, tp, k, t * P : (t + 1) * P], env.parts[s][:, wp, k, :], start=n == 0, stop=n == 3 * KD - 1)
                n += 1
        return m


def stage_modulation(env):
    nc, A = env.nc, env.A
    NCH = 3 * D // BANK
    with ExitStack() as ctx:
        sem = lambda name: env.semaphore(name)
        sb = lambda name, shape: ctx.enter_context(nc.sbuf_tensor(name, shape, F32))
        mod_row = sb("mod_row", [2, 2 * 3 * D])
        bmod = sb("bmod", [2, 2 * 3 * D])
        npost = sb("npost", [P, 2, D])
        npre = sb("npre", [P, 2, KD, 2])
        cond = sb("cond", [P, KD, 2])
        lam = sb("lam", [P, 4, A_QK])
        lam_t = sb("lam_t", [P, A_QK])
        lam_s = sb("lam_s", [P, 2])
        sel = sb("sel", [2, 2, P])
        small_in, cond_ready, mod_ready, mod_added = sem("small_in"), sem("cond_ready"), sem("mod_ready"), sem("mod_added")
        cols_ready, rows_ready, rows_read = sem("cols_ready"), sem("rows_ready"), sem("rows_read")
        resid_in, lam_dot, lam_exp, dve_step = sem("resid_in"), sem("lam_dot"), sem("lam_exp"), sem("mod_dve_step")
        wide = [sb(f"w_mod{s}", [P, KD, BANK]) for s in range(2)]
        w_in = [sem(f"w_mod_in{s}") for s in range(2)]
        SMALL = 16 * 8
        with nc.Block() as block:

            @block.sync
            def _(sp):
                for s in range(2):
                    sp.dma_start(wide[s][:], A["w_mod"][s]).then_inc(w_in[s], 16)
                with sp.Fori(1, NCH) as i:
                    for s in range(2):
                        sp.wait_ge(mod_ready, 2 * i + s - 1)
                        sp.dma_start(wide[s][:], A["w_mod"][bass.ds(2 * i + s, 1)].rearrange("a p k n -> (a p) k n")).then_inc(w_in[s], 16)
                Ring.prefetch(env, sp, A["w_in_even"])

            @block.scalar
            def _(act):
                act.dma_start(cond[:], A["cond"]).then_inc(small_in, 16)
                act.dma_start(bmod[:], A["b_mod"].partition_broadcast(2)).then_inc(small_in, 16)
                act.dma_start(sel[:], A["sel"]).then_inc(small_in, 16)
                act.dma_start(npre[:], A["norm_pre"]).then_inc(small_in, 16)
                act.dma_start(npost[:], A["norm_post"].partition_broadcast(P)).then_inc(small_in, 16)
                act.dma_start(lam[:], A["lam_a"].partition_broadcast(P)).then_inc(small_in, 16)
                act.dma_start(env.ident[:], A["ident"]).then_inc(small_in, 16)
                act.dma_start(env.subln[:], A["subln"]).then_inc(small_in, 16)
                act.dma_start(env.X[:], A["x"].rearrange("(t p) d -> p t d", p=P)).then_inc(resid_in, 16)
                act.dma_start(env.CX[:], A["ctx"].rearrange("(t p) d -> p t d", p=P)).then_inc(resid_in, 16)
                act.wait_ge(small_in, SMALL)
                nc.scalar.activation(cond[:], cond[:], ACT.Silu).then_inc(cond_ready, 1)
                act.wait_ge(lam_dot, 2)
                nc.scalar.activation(lam_s[:], lam_s[:], ACT.Exp).then_inc(lam_exp, 1)
                act.wait_ge(resid_in, 32)

            @block.tensor
            def _(pe):
                pe.wait_ge(cond_ready, 1)
                with pe.Fori(0, NCH) as i:
                    for s in range(2):
                        pe.wait_ge(w_in[s], 16 + 16 * i)
                        pe.wait_ge(mod_added, 2 * i + 1)
                        for k in range(KD):
                            m = nc.tensor.matmul(bank(env, s)[0:2], cond[:, k, :], wide[s][:, k, :], start=k == 0, stop=k == KD - 1)
                        m.then_inc(mod_ready, 1)
                pe.wait_ge(mod_added, 2 * NCH + 1)
                for l in range(2):
                    for j in range(2):
                        for k in range(KD):
                            at = ((l * 2 + j) * KD + k) * 2
                            src = l * 3 * D + j * D + k * P
                            m = nc.tensor.transpose(bank(env, 2, 2, at), mod_row[0:2, src : src + P], env.ident[0:2, 0:2])
                m.then_inc(cols_ready, 1)
                for n, (l, r) in enumerate(((0, 0), (0, 1), (1, 0))):
                    for h in range(2):
                        if n == 2:
                            pe.wait_ge(rows_read, 1)
                        src = l * 3 * D + 2 * D + h * BANK
                        m = nc.tensor.matmul(
                            bank(env, 4 + 2 * (n % 2) + h), sel[0:2, r, :], mod_row[0:2, src : src + BANK], start=True, stop=True
                        )
                    m.then_inc(rows_ready, 1)

            @block.vector
            def _(dve):
                st = Steps(dve, dve_step)
                dve.sem_inc(mod_added, 1)
                dve.wait_ge(small_in, SMALL)
                for j in range(2):
                    nc.vector.tensor_tensor_reduce(
                        lam_t[:], lam[:, 2 * j, :], lam[:, 2 * j + 1, :], 1.0, 0.0, ALU.mult, ALU.add, lam_s[:, j : j + 1]
                    ).then_inc(lam_dot, 1)
                    dve.wait_ge(lam_dot, j + 1)
                dve.wait_ge(lam_exp, 1)
                st.link(nc.vector.tensor_tensor(env.neg_lam[:], lam_s[:, 1:2], lam_s[:, 0:1], ALU.subtract))
                st.link(nc.vector.tensor_scalar(env.neg_lam[:], env.neg_lam[:], -LAM_INIT0, None, ALU.add))
                st.link(nc.vector.tensor_scalar(env.subln[:], env.subln[:], 1.0 - LAM_INIT0, None, ALU.mult))
                with dve.Fori(0, NCH) as i:
                    for s in range(2):
                        dve.wait_ge(mod_ready, 2 * i + s + 1)
                        cols = bass.ds((2 * i + s) * BANK, BANK)
                        nc.vector.tensor_tensor(mod_row[0:2, cols], bank(env, s)[0:2], bmod[0:2, cols], ALU.add).then_inc(mod_added, 1)
                dve.wait_ge(cols_ready, 1)
                cols = bank(env, 2, 2 * 2 * KD * 2).rearrange("p (l j k r) -> p l j k r", l=2, j=2, k=KD)
                for l in range(2):
                    st.link(
                        nc.vector.scalar_tensor_tensor(env.gain[:, l], cols[:, l, 1], 1.0, npre[:, l], ALU.add, ALU.mult)
                    )
                    st.link(nc.vector.tensor_copy(env.shift[:, l], cols[:, l, 0]))
                for n, l in enumerate((0, 0, 1)):
                    dve.wait_ge(rows_ready, n + 1)
                    m = nc.vector.tensor_tensor(
                        env.gate[:, n, :], env.PS[:, (4 + 2 * (n % 2)) * BANK : (6 + 2 * (n % 2)) * BANK], npost[:, l, :], ALU.mult
                    )
                    m.then_inc(rows_read, 1)


def stage_norm(env, name, streams, xs, tmp):
    nc = env.nc
    tiles = sum(s[1] for s in streams)
    with ExitStack() as ctx:
        sem = lambda n: env.semaphore(f"{name}_{n}")
        ss = ctx.enter_context(nc.sbuf_tensor(f"{name}_ss", [P, tiles], F32))
        squares, mean_ready, root_ready, scaled, dve_step = sem("squares"), sem("mean"), sem("root"), sem("scaled"), sem("step")
        turned, read, hi_done, lo_done = sem("turned"), sem("read"), sem("hi_done"), sem("lo_done")
        jobs = [(s, k) for k in range(KD) for s in streams]
        with nc.Block() as block:

            @block.scalar
            def _(act):
                for x, n, t0, _g, _s in streams:
                    for t in range(n):
                        nc.scalar.activation(xs[:, t0 + t, :], x[:, t, :], ACT.Square, accum_out=ss[:, t0 + t : t0 + t + 1]).then_inc(
                            squares, 1
                        )
                act.wait_ge(mean_ready, 1)
                nc.scalar.activation(ss[:], ss[:], ACT.Sqrt).then_inc(root_ready, 1)
                for j, ((x, n, t0, _g, _s), k) in enumerate(jobs):
                    act.wait_ge(read, j + 1)
                    nc.scalar.copy(env.tok[:, 0, k, t0 * P : (t0 + n) * P], tmp[:, j % 4, 0 : n * P]).then_inc(hi_done, 1)

            @block.gpsimd
            def _(pool):
                for j, ((x, n, t0, _g, _s), k) in enumerate(jobs):
                    pool.wait_ge(hi_done, j + 1)
                    cols = slice(t0 * P, (t0 + n) * P)
                    nc.gpsimd.tensor_tensor(env.tok[:, 1, k, cols], tmp[:, j % 4, 0 : n * P], env.tok[:, 0, k, cols].bitcast(F32), ALU.subtract).then_inc(
                        lo_done, 1)

            @block.vector
            def _(dve):
                st = Steps(dve, dve_step)
                dve.wait_ge(squares, tiles)
                nc.vector.tensor_scalar(ss[:], ss[:], 1.0 / D, EPS, ALU.mult, ALU.add).then_inc(mean_ready, 1)
                dve.wait_ge(root_ready, 1)
                st.link(nc.vector.reciprocal(ss[:], ss[:]))
                for x, n, t0, _g, _s in streams:
                    for t in range(n):
                        nc.vector.tensor_scalar(xs[:, t0 + t, :], x[:, t, :], ss[:, t0 + t : t0 + t + 1], None, ALU.mult).then_inc(scaled, 1)
                for j, ((x, n, t0, gain, shift), k) in enumerate(jobs):
                    dve.wait_ge(turned, j + 1)
                    if j >= 4:
                        dve.wait_ge(lo_done, j - 3)
                    out, src = tmp[:, j % 4, 0 : n * P], bank(env, j % 8, n * P)
                    if shift is None:
                        m = nc.vector.tensor_scalar(out, src, gain(k), None, ALU.mult)
                    else:
                        m = nc.vector.tensor_scalar(out, src, gain(k), shift(k), ALU.mult, ALU.add)
                    m.then_inc(read, 1)

            @block.tensor
            def _(pe):
                for j, ((x, n, t0, _g, _s), k) in enumerate(jobs):
                    if j >= 8:
                        pe.wait_ge(read, j - 7)
                    for t in range(n):
                        pe.wait_ge(scaled, t0 + t + 1)
                        m = nc.tensor.transpose(bank(env, j % 8, P, t * P), xs[:, t0 + t, k * P : (k + 1) * P], env.ident[:])
                    m.then_inc(turned, 1)


def stage_out(env, name, streams, mix, source, Y, following):
    nc = env.nc
    jobs = [(x, t, t0 + t, gate) for x, n, t0, gate in streams for t in range(n)]
    tiles = len(jobs)
    NC = D // CW
    units = [(c, t) for c in range(NC) for t in range(tiles)]
    with ExitStack() as ctx:
        sem = lambda n: env.semaphore(f"{name}_{n}")
        sb = lambda n, shape: ctx.enter_context(nc.sbuf_tensor(f"{name}_{n}", shape, F32))
        ss, total, junk = sb("ss", [P, tiles, NC]), sb("total", [P, tiles, 1]), sb("junk", [P, CW])
        hi_done, lo_done, product, read, squared = sem("mix_hi"), sem("mix_lo"), sem("product"), sem("read"), sem("squared")
        mean_ready, root_ready, step, updated = sem("mean"), sem("root"), sem("step"), sem("updated")
        ring = Ring(env, name, source, NC)
        with nc.Block() as block:

            @block.sync
            def _(sp):
                ring.load_rest(sp)
                ring.prefetch_next(sp, following)

            @block.gpsimd
            def _(pool):
                ring.all_lo(pool)

            @block.scalar
            def _(act):
                ring.hi(act, 0, 0)
                for k in range(KD):
                    nc.scalar.copy(env.tok[:, 0, k, :], mix[k]).then_inc(hi_done, 1)
                    if k == 3:
                        ring.hi(act, 0, 1)
                for n, (c, t) in enumerate(units):
                    if t == 0 and c >= 1 and c + 1 < NC:
                        ring.hi(act, (c + 1) // 2, (c + 1) % 2, (product, c * tiles))
                    act.wait_ge(read, n + 1)
                    if n:
                        act.wait_ge(squared, n)
                    nc.scalar.activation(junk[:], Y[:, t, c * CW : (c + 1) * CW], ACT.Square, accum_out=ss[:, t, c : c + 1]).then_inc(squared, 1)
                act.wait_ge(mean_ready, 1)
                nc.scalar.activation(total[:, :, 0], total[:, :, 0], ACT.Sqrt).then_inc(root_ready, 1)

            @block.tensor
            def _(pe):
                pe.wait_ge(lo_done, KD)
                for n, (c, t) in enumerate(units):
                    if t == 0:
                        pe.wait_ge(ring.lo_done, c + 1)
                    if n >= 8:
                        pe.wait_ge(read, n - 7)
                    ring.natural(c % 2, t, bank(env, n % 8, CW)).then_inc(product, 1)

            @block.vector
            def _(dve):
                st = Steps(dve, step)
                for k in range(KD):
                    dve.wait_ge(hi_done, k + 1)
                    nc.vector.tensor_tensor(env.tok[:, 1, k, :], mix[k], env.tok[:, 0, k, :].bitcast(F32), ALU.subtract).then_inc(lo_done, 1)
                for n, (c, t) in enumerate(units):
                    dve.wait_ge(product, n + 1)
                    nc.vector.tensor_copy(Y[:, t, c * CW : (c + 1) * CW], bank(env, n % 8, CW)).then_inc(read, 1)
                dve.wait_ge(squared, len(units))
                st.link(nc.vector.tensor_reduce(total[:], ss[:], AX.X, ALU.add))
                nc.vector.tensor_scalar(total[:, :, 0], total[:, :, 0], 1.0 / D, EPS, ALU.mult, ALU.add).then_inc(mean_ready, 1)
                dve.wait_ge(root_ready, 1)
                st.link(nc.vector.reciprocal(total[:, :, 0], total[:, :, 0]))
                for n, (x, t, at, gate) in enumerate(jobs):
                    nc.vector.scalar_tensor_tensor(Y[:, at, :], Y[:, at, :], total[:, at, :], gate, ALU.mult, ALU.mult).then_inc(updated, 1)
                for n, (x, t, at, gate) in enumerate(jobs):
                    dve.wait_ge(updated, n + 1)
                    st.inc(nc.vector.tensor_tensor(x[:, t, :], x[:, t, :], Y[:, at, :], ALU.add))


E_Q, E_K, E_GA, E_Z, E_BG = range(5)


def stage_even_proj(env, pT, vN):
    nc = env.nc
    COPIED, MULTIPLIED = 10, 4
    with ExitStack() as ctx:
        sem = lambda name: env.semaphore("even_" + name)
        tile_ready, x_out, c_out, gate_done, v_ready, v_out = (
            sem("tile_ready"), sem("x_out"), sem("c_out"), sem("gate_done"), sem("v_ready"), sem("v_out"))
        ring = Ring(env, "even", env.A["w_in_even"], COPIED + MULTIPLIED + 2)
        x_bank, c_bank = lambda j: bank(env, j), lambda j: bank(env, 4 + j, L)
        vjobs = [(s, t) for s in range(2) for t in range(NT)]
        with nc.Block() as block:

            @block.sync
            def _(sp):
                ring.load_rest(sp)

            @block.gpsimd
            def _(pool):
                ring.all_lo(pool)

            @block.tensor
            def _(pe):
                def pair(i, wait=True):
                    for j in range(4):
                        s, f = j // 2, j % 2
                        if f == 0:
                            pe.wait_ge(ring.lo_done, 2 * i + s + 1)
                        if wait:
                            pe.wait_ge(x_out, 4 * i + j - 3)
                            pe.wait_ge(c_out, 4 * i + j - 3)
                        ring.transposed(s, f, (x_bank(j), c_bank(j)), ((0, S), (S, ST))).then_inc(tile_ready, 1)

                pair(0, wait=False)
                with pe.Fori(1, (COPIED + MULTIPLIED) // 2) as i:
                    pair(i)
                for n, (s, t) in enumerate(vjobs):
                    if t == 0:
                        pe.wait_ge(ring.lo_done, COPIED + MULTIPLIED + s + 1)
                    if n < 4:
                        pe.wait_ge(x_out, 2 * (COPIED + MULTIPLIED) + n - 3)
                    else:
                        pe.wait_ge(v_out, n - 3)
                    ring.natural(s, t, bank(env, n % 4, CW)).then_inc(v_ready, 1)

            @block.scalar
            def _(act):
                ring.hi(act, 0, 0)
                ring.hi(act, 0, 1)
                with act.Fori(0, COPIED // 2) as i:
                    for j in range(4):
                        act.wait_ge(tile_ready, 4 * i + j + 1)
                        out = pT[:, bass.ds(4 * i + j, 1), S:ST].rearrange("p a t -> p (a t)")
                        nc.scalar.copy(out, c_bank(j)).then_inc(c_out, 1)
                        if j % 2:
                            ring.hi(act, i + 1, j // 2)
                act.wait_ge(x_out, 2 * COPIED)
                act.wait_ge(c_out, 2 * COPIED)
                for g in (E_BG, E_GA):
                    view = pT[:, g * FT : (g + 1) * FT, :]
                    nc.scalar.activation(view, view, ACT.Silu).then_inc(gate_done, 1)
                for c in range(COPIED, COPIED + MULTIPLIED):
                    ring.hi(act, c // 2 + 1, c % 2, (tile_ready, 2 * c + 2))

            @block.vector
            def _(dve):
                with dve.Fori(0, COPIED // 2) as i:
                    for j in range(4):
                        dve.wait_ge(tile_ready, 4 * i + j + 1)
                        out = pT[:, bass.ds(4 * i + j, 1), 0:S].rearrange("p a t -> p (a t)")
                        nc.vector.tensor_copy(out, x_bank(j)).then_inc(x_out, 1)
                for j in range(2 * MULTIPLIED):
                    n = 2 * COPIED + j
                    tile = E_Z * FT + j
                    dve.wait_ge(tile_ready, n + 1)
                    if j == 0:
                        dve.wait_ge(gate_done, 1)
                    nc.vector.tensor_tensor(pT[:, tile, 0:S], x_bank(j % 4), pT[:, tile, 0:S], ALU.mult).then_inc(x_out, 1)
                    nc.vector.tensor_tensor(pT[:, tile, S:ST], c_bank(j % 4), pT[:, tile, S:ST], ALU.mult).then_inc(c_out, 1)
                for n, (s, t) in enumerate(vjobs):
                    dve.wait_ge(v_ready, n + 1)
                    nc.vector.tensor_copy(vN[:, t, s * CW : (s + 1) * CW], bank(env, n % 4, CW)).then_inc(v_out, 1)


def stage_rope(env, pT, qk, taps):
    nc, A = env.nc, env.A
    with ExitStack() as ctx:
        sem = lambda name: env.semaphore("rc_" + name)
        sb = lambda name, shape: ctx.enter_context(nc.sbuf_tensor("rc_" + name, shape, F32))
        rope = sb("rope", [P, 2, 2, S])
        swap = sb("swap", [P, P])
        t1, t2 = sb("t1", [P, 2, S]), sb("t2", [P, 2, S])
        tables_in, swapped, rope_read, dve_step = sem("tables_in"), sem("swapped"), sem("rope_read"), sem("step")
        roped, hi_done, lo_done = sem("roped"), sem("hi_done"), sem("lo_done")
        with nc.Block() as block:

            @block.sync
            def _(sp):
                sp.dma_start(taps[:], A["conv_b"]).then_inc(tables_in, 16)
                sp.dma_start(swap[:], A["rope_swap"]).then_inc(tables_in, 16)
                sp.dma_start(rope[:], A["rope"]).then_inc(tables_in, 16)

            @block.scalar
            def _(act):
                for n in range(2 * FT):
                    act.wait_ge(roped, n + 1)
                    nc.scalar.copy(qk[:, 0, n, :], pT[:, n, :]).then_inc(hi_done, 1)

            @block.tensor
            def _(pe):
                pe.wait_ge(tables_in, 48)
                for n in range(2 * FT):
                    if n >= 4:
                        pe.wait_ge(rope_read, n - 3)
                    nc.tensor.matmul(bank(env, n % 4), swap[:], pT[:, n, 0:S], start=True, stop=True).then_inc(swapped, 1)

            @block.gpsimd
            def _(pool):
                for n in range(2 * FT):
                    pool.wait_ge(hi_done, n + 1)
                    nc.gpsimd.tensor_tensor(qk[:, 1, n, :], pT[:, n, :], qk[:, 0, n, :].bitcast(F32), ALU.subtract).then_inc(lo_done, 1)

            @block.vector
            def _(dve):
                st = Steps(dve, dve_step)
                dve.wait_ge(tables_in, 48)
                st.link(nc.vector.tensor_scalar(pT[:, 0:FT, S:ST], pT[:, 0:FT, S:ST], A_QK**-0.5, None, ALU.mult))
                for n in range(2 * FT):
                    j = n // FT
                    u = pT[:, n, 0:S]
                    st.inc(nc.vector.tensor_tensor(t1[:, n % 2, :], u, rope[:, j, 0, :], ALU.mult))
                    dve.wait_ge(swapped, n + 1)
                    nc.vector.tensor_tensor(t2[:, n % 2, :], bank(env, n % 4), rope[:, j, 1, :], ALU.mult).then_inc(rope_read, 1)
                    dve.wait_ge(rope_read, n + 1)
                    dve.wait_ge(dve_step, st.n)
                    nc.vector.tensor_tensor(u, t1[:, n % 2, :], t2[:, n % 2, :], ALU.add).then_inc(roped, 1)
                    dve.wait_ge(roped, n + 1)


def stage_diff_attention(env, pT, qk, vN, taps, O):
    nc = env.nc
    GROUP = P // A_QK
    GROUPS = A_HEADS // GROUP
    UNITS = GROUP * NT
    with ExitStack() as ctx:
        sem = lambda name: env.semaphore("da_" + name)
        sb = lambda name, shape: ctx.enter_context(nc.sbuf_tensor("da_" + name, shape, F32))
        stack = [ctx.enter_context(nc.sbuf_tensor(f"da_stack{h}", [P, 2, 2, ST], F32R)) for h in range(2)]
        neg_max, sums, recip, ratio = sb("neg_max", [P, 2]), sb("sums", [P, 2, 2]), sb("recip", [P, 8, 2]), sb("ratio", [P, 1])
        ex = [[pT[:, 2 * b + m, :] for m in range(2)] for b in range(2)]
        at = [pT[:, FT + b, :] for b in range(2)]
        atT = [pT[:, FT + 2 + b, :] for b in range(2)]
        stacked, scores_ready = env.even_stacked, [sem(f"scores{m}") for m in range(2)]
        max_ready, exp_done, combined, turned = [sem(f"max{m}") for m in range(2)], [sem(f"exp{m}") for m in range(2)], sem("combined"), sem("turned")
        turned_out, pv_ready, o_out, dve_step = sem("turned_out"), sem("pv"), sem("o_out"), sem("step")
        based, mixed = sem("based"), sem("mixed")
        y = pT[:, FT : 2 * FT, :]
        T0, O0 = 4 * BANK, 6 * BANK

        def unit(u):
            hh, qt = u // NT, u % NT
            return hh, qt, (ST if qt < TX else L), (list(range(NT)) if qt < TX else list(range(TX, NT)))

        with nc.Block() as block:

            @block.gpsimd
            def _(pool):
                transfers = [(0, slice(0, 2), 0), (3, slice(0, 2), 1)]
                transfers += [(z, slice(j, j + 1), (z // 2, z % 2)[j]) for z in (1, 2) for j in range(2)]

                def load(r, g):
                    rows = slice(r * A_QK, (r + 1) * A_QK)
                    for z, js, part in transfers:
                        source = qk[rows, part].rearrange("p (j m g) t -> p j m g t", j=2, m=2)[:, js]
                        source = source[:, :, :, bass.ds(g, 1), :].rearrange("p j m g t -> p j m (g t)")
                        pool.dma_start(stack[r % 2][z * A_QK : (z + 1) * A_QK, js], source).then_inc(stacked[r % 2], 16)

                with pool.Fori(0, GROUPS) as i:
                    for r in range(GROUP):
                        pool.wait_ge(scores_ready[1], UNITS * i + NT * (r + 1))
                        load(r, i)

            @block.tensor
            def _(pe):
                for m in range(2):
                    pe.sem_inc(scores_ready[m], 2 * NT)
                pe.sem_inc(turned, 2)
                pe.sem_inc(pv_ready, 2)
                with pe.Fori(0, GROUPS) as i:
                    n0 = UNITS * i

                    def scores(u):
                        hh, qt, n, _ = unit(u)
                        if qt == 0:
                            pe.wait_ge(stacked[hh % 2], 16 * 6 * (GROUP // 2) * i + 16 * 6 * (hh // 2 + 1))
                        for m in range(2):
                            q, k = stack[hh % 2][:, 0, m, qt * P : (qt + 1) * P], stack[hh % 2][:, 1, m, :]
                            pe.wait_ge(exp_done[m], n0 + u + 1)
                            if n == ST:
                                nc.tensor.matmul(bank(env, 2 * m), q, k[:, 0:S], start=True, stop=True)
                                r = nc.tensor.matmul(bank(env, 2 * m + 1, L), q, k[:, S:ST], start=True, stop=True)
                            else:
                                r = nc.tensor.matmul(bank(env, 2 * m, L), q, k[:, S:ST], start=True, stop=True)
                            r.then_inc(scores_ready[m], 1)

                    def turn(u):
                        _, _, _, kts = unit(u)
                        pe.wait_ge(combined, n0 + u + 3)
                        pe.wait_ge(turned_out, n0 + u + 1)
                        for j in range(len(kts)):
                            r = nc.tensor.transpose(env.PS[:, T0 + j * P : T0 + (j + 1) * P], at[u % 2][:, j * P : (j + 1) * P], env.ident[:])
                        r.then_inc(turned, 1)

                    def pv(u):
                        hh, _, _, kts = unit(u)
                        pe.wait_ge(turned_out, n0 + u + 2)
                        pe.wait_ge(o_out, n0 + u + 1)
                        for j, kt in enumerate(kts):
                            v = vN[:, kt, bass.ds((i * GROUP + hh) * A_V, A_V)]
                            r = nc.tensor.matmul(
                                env.PS[:, O0 + (u % 2) * BANK : O0 + (u % 2) * BANK + A_V],
                                atT[u % 2][:, j * P : (j + 1) * P], v, start=j == 0, stop=j == len(kts) - 1)
                        r.then_inc(pv_ready, 1)

                    for u in range(UNITS + 3):
                        if u < UNITS:
                            scores(u)
                        if 2 <= u < UNITS + 2:
                            turn(u - 2)
                        if u >= 3:
                            pv(u - 3)

            @block.scalar
            def _(act):
                for f in range(FT):
                    nc.scalar.activation(y[:, f, :], pT[:, E_Z * FT + f, :], ACT.Copy, scale=taps[:, f, 1:2]).then_inc(based, 1)
                for m in range(2):
                    act.sem_inc(exp_done[m], 1)
                act.sem_inc(turned_out, 1)
                with act.Fori(0, GROUPS) as i:
                    n0 = UNITS * i

                    def exps(u):
                        _, _, n, _ = unit(u)
                        act.wait_ge(combined, n0 + u + 1)
                        for m in range(2):
                            act.wait_ge(max_ready[m], n0 + u + 1)
                            nc.scalar.activation(
                                ex[u % 2][m][:, 0:n], env.PS[:, 2 * m * BANK : 2 * m * BANK + n], ACT.Exp,
                                bias=neg_max[:, m : m + 1], accum_out=sums[:, u % 2, m : m + 1]).then_inc(exp_done[m], 1)

                    def copy_out(u):
                        _, _, n, _ = unit(u)
                        act.wait_ge(turned, n0 + u + 3)
                        act.wait_ge(pv_ready, n0 + u + 1)
                        nc.scalar.copy(atT[u % 2][:, 0:n], env.PS[:, T0 : T0 + n]).then_inc(turned_out, 1)

                    for u in range(UNITS + 2):
                        if u < UNITS:
                            exps(u)
                        if u >= 2:
                            copy_out(u - 2)

            @block.vector
            def _(dve):
                dve.sem_inc(o_out, 2)
                dve.sem_inc(combined, 2)
                st = Steps(dve, dve_step)
                for f in range(FT):
                    z, out = pT[:, E_Z * FT + f, :], y[:, f, :]
                    dve.wait_ge(based, f + 1)
                    for n, (a, b) in enumerate(((0, S), (S, ST))):
                        st.inc(nc.vector.scalar_tensor_tensor(
                            out[:, a + 1 : b], z[:, a : b - 1], taps[:, f, 0:1], out[:, a + 1 : b], ALU.mult, ALU.add))
                    dve.wait_ge(dve_step, st.n)
                    for n, (a, b) in enumerate(((0, S), (S, ST))):
                        st.inc(nc.vector.scalar_tensor_tensor(
                            out[:, a : b - 1], z[:, a + 1 : b], taps[:, f, 2:3], out[:, a : b - 1], ALU.mult, ALU.add))
                    dve.wait_ge(dve_step, st.n)
                    nc.vector.tensor_tensor(z, out, pT[:, E_BG * FT + f, :], ALU.mult).then_inc(mixed, 1)
                conv_steps = st.n
                dve.wait_ge(mixed, FT)
                with dve.Fori(0, GROUPS) as i:
                    n0 = UNITS * i
                    st = Steps(dve, dve_step, conv_steps + 2 * UNITS * i)

                    def maximum(u, m):
                        _, _, n, _ = unit(u)
                        dve.wait_ge(scores_ready[m], n0 + u + 1 + 2 * NT)
                        nc.vector.tensor_reduce(
                            neg_max[:, m : m + 1], env.PS[:, 2 * m * BANK : 2 * m * BANK + n], AX.X, ALU.max, negate=True
                        ).then_inc(max_ready[m], 1)

                    def inverse(u):
                        for m in range(2):
                            dve.wait_ge(exp_done[m], n0 + u + 2)
                        st.inc(nc.vector.reciprocal(recip[:, u % 8, :], sums[:, u % 2, :]))

                    def weight(u):
                        dve.wait_ge(dve_step, st.base + st.n)
                        st.inc(nc.vector.scalar_tensor_tensor(
                            ratio[:], recip[:, u % 8, 1:2], env.neg_lam[:], sums[:, u % 2, 0:1], ALU.mult, ALU.mult))

                    def combine(u):
                        _, _, n, _ = unit(u)
                        dve.wait_ge(dve_step, st.base + st.n)
                        dve.wait_ge(turned, n0 + u + 1)
                        nc.vector.scalar_tensor_tensor(
                            at[u % 2][:, 0:n], ex[u % 2][1][:, 0:n], ratio[:], ex[u % 2][0][:, 0:n], ALU.mult, ALU.add
                        ).then_inc(combined, 1)

                    def out(u):
                        hh, qt, _, _ = unit(u)
                        dve.wait_ge(pv_ready, n0 + u + 3)
                        nc.vector.tensor_scalar(
                            O[:, qt, bass.ds((i * GROUP + hh) * A_V, A_V)],
                            env.PS[:, O0 + (u % 2) * BANK : O0 + (u % 2) * BANK + A_V],
                            recip[:, u % 8, 0:1], None, ALU.mult).then_inc(o_out, 1)

                    for u in range(UNITS + 4):
                        if u < UNITS:
                            maximum(u, 0)
                        if 1 <= u <= UNITS:
                            inverse(u - 1)
                        if u >= 4:
                            out(u - 4)
                        if 1 <= u <= UNITS:
                            weight(u - 1)
                        if u < UNITS:
                            maximum(u, 1)
                        if 1 <= u <= UNITS:
                            combine(u - 1)


def stage_diff_post(env, pT, O):
    nc = env.nc
    G = NT * A_HEADS
    with ExitStack() as ctx:
        sem = lambda name: env.semaphore("dp_" + name)
        sb = lambda name, shape: ctx.enter_context(nc.sbuf_tensor("dp_" + name, shape, F32))
        ss = sb("ss", [P, G])
        sq = pT[:, E_K * FT : (E_K + 1) * FT].rearrange("p f t -> p (f t)")
        heads = O[:].rearrange("p t (h d) -> p (t h) d", d=A_V)
        step, mean_ready, root_ready, normed, turned, mixed = (
            sem("step"), sem("mean"), sem("root"), sem("normed"), sem("turned"), sem("mixed"))
        with nc.Block() as block:

            @block.sync
            def _(sp):
                Ring.prefetch(env, sp, env.A["w_out"][0])

            @block.vector
            def _(dve):
                st = Steps(dve, step)
                o = O[:].rearrange("p t c -> p (t c)")
                st.link(nc.vector.tensor_tensor(sq, o, o, ALU.mult))
                st.link(nc.vector.tensor_reduce(ss[:], sq.rearrange("p (g d) -> p g d", d=A_V), AX.X, ALU.add))
                nc.vector.tensor_scalar(ss[:], ss[:], 1.0 / A_V, EPS, ALU.mult, ALU.add).then_inc(mean_ready, 1)
                dve.wait_ge(root_ready, 1)
                st.link(nc.vector.reciprocal(ss[:], ss[:]))
                nc.vector.tensor_tensor(heads, heads, ss[:].unsqueeze(2).to_broadcast([P, G, A_V]), ALU.mult).then_inc(normed, 1)
                for f in range(FT):
                    for n, (a, b) in enumerate(((0, S), (S, ST))):
                        dve.wait_ge(turned, 2 * f + n + 1)
                        nc.vector.scalar_tensor_tensor(
                            pT[:, E_Q * FT + f, a:b], bank(env, (2 * f + n) % 8, b - a), env.subln[:], pT[:, E_GA * FT + f, a:b], ALU.mult, ALU.mult
                        ).then_inc(mixed, 1)

            @block.scalar
            def _(act):
                act.wait_ge(mean_ready, 1)
                nc.scalar.activation(ss[:], ss[:], ACT.Sqrt).then_inc(root_ready, 1)

            @block.tensor
            def _(pe):
                pe.wait_ge(normed, 1)
                for f in range(FT):
                    for n, tiles in enumerate((range(TX), range(TX, NT))):
                        for j, t in enumerate(tiles):
                            m = nc.tensor.transpose(bank(env, (2 * f + n) % 8, P, j * P), O[:, t, f * P : (f + 1) * P], env.ident[:])
                        m.then_inc(turned, 1)


def layer_even(env, gain, shift):
    nc, A = env.nc, env.A
    with ExitStack() as layer:
        sb = lambda scope, name, shape: scope.enter_context(nc.sbuf_tensor("even_" + name, shape, F32))
        pT, vN = sb(layer, "pT", [P, 5 * FT, ST]), sb(layer, "v", [P, NT, BW])
        flat = pT[:].rearrange("p n t -> p (n t)")
        with ExitStack() as proj:
            env.split_operands(proj, "even", ST)
            xs = flat[:, 0 : NT * D].rearrange("p (t d) -> p t d", d=D)
            tmp = flat[:, NT * D : NT * D + 4 * S].rearrange("p (j t) -> p j t", t=S)
            stage_norm(env, "norm0", [(env.X, TX, 0, gain(0, 0), shift(0, 0)), (env.CX, TC, TX, gain(0, 1), shift(0, 1))], xs, tmp)
            stage_even_proj(env, pT, vN)
        with ExitStack() as attention:
            qk = attention.enter_context(nc.sbuf_tensor("even_qk_parts", [P, 2, 2 * FT, ST], F32R))
            taps = sb(attention, "taps", [P, FT, 3])
            stage_rope(env, pT, qk, taps)
            O = flat[:, E_BG * FT * ST : (E_BG + 1) * FT * ST].rearrange("p (t c) -> p t c", c=BW)
            stage_diff_attention(env, pT, qk, vN, taps, O)
            stage_diff_post(env, pT, O)
        env.split_operands(layer, "out0", ST)
        mix = [pT[:, g * FT + f, :] for g in (E_Q, E_Z) for f in range(FT)]
        Y = flat[:, E_K * FT * ST : E_Z * FT * ST].rearrange("p (t d) -> p t d", d=D)
        stage_out(
            env, "out0", [(env.X, TX, 0, env.gate[:, 0, :]), (env.CX, TC, TX, env.gate[:, 1, :])], mix, A["w_out"][0], Y, A["w_in_odd"])


O_Q, O_GN, O_GD = range(3)


def stage_odd_proj(env, pT, kT, vN, uN):
    nc = env.nc
    ONLY_X, KEYS = 6, 2
    with ExitStack() as ctx:
        sem = lambda name: env.semaphore("odd_" + name)
        tile_ready, x_out, c_out, n_ready, n_out = sem("tile_ready"), sem("x_out"), sem("c_out"), sem("natural_ready"), sem("natural_out")
        ring = Ring(env, "odd", env.A["w_in_odd"], ONLY_X + KEYS + 4)
        x_bank, c_bank = lambda j: bank(env, j % 4), lambda j: bank(env, 4 + j, L)
        jobs = [(ONLY_X + KEYS + s, vN, t) for s in range(2) for t in range(NT)]
        jobs += [(ONLY_X + KEYS + 2 + s, uN, t) for s in range(2) for t in range(TX)]
        with nc.Block() as block:

            @block.sync
            def _(sp):
                ring.load_rest(sp)

            @block.gpsimd
            def _(pool):
                ring.all_lo(pool)

            @block.tensor
            def _(pe):
                def tile(s, f, n, free, out, tokens):
                    if f == 0:
                        pe.wait_ge(ring.lo_done, n // 2 + 1)
                    if free is not None:
                        pe.wait_ge(x_out, free)
                    ring.transposed(s, f, out, tokens).then_inc(tile_ready, 1)

                for j in range(4):
                    tile(j // 2, j % 2, j, None, (x_bank(j),), ((0, S),))
                with pe.Fori(1, ONLY_X // 2) as i:
                    for j in range(4):
                        if j % 2 == 0:
                            pe.wait_ge(ring.lo_done, 2 * i + j // 2 + 1)
                        pe.wait_ge(x_out, 4 * i + j - 3)
                        ring.transposed(j // 2, j % 2, (x_bank(j),), ((0, S),)).then_inc(tile_ready, 1)
                for j in range(2 * KEYS):
                    n = 2 * ONLY_X + j
                    tile(j // 2, j % 2, n, n - 3, (x_bank(j), c_bank(j)), ((0, S), (S, ST)))
                for n, (c, _, t) in enumerate(jobs):
                    if t == 0:
                        pe.wait_ge(ring.lo_done, c + 1)
                    if n < 4:
                        pe.wait_ge(x_out, 2 * (ONLY_X + KEYS) + n - 3)
                    else:
                        pe.wait_ge(n_out, n - 3)
                    ring.natural(c % 2, t, bank(env, n % 4, CW)).then_inc(n_ready, 1)

            @block.scalar
            def _(act):
                ring.hi(act, 0, 0)
                ring.hi(act, 0, 1)
                with act.Fori(0, (ONLY_X + KEYS) // 2) as i:
                    for s in range(2):
                        ring.hi(act, i + 1, s, (tile_ready, 4 * i + 2 * s + 2))
                for j in range(2 * KEYS):
                    act.wait_ge(tile_ready, 2 * ONLY_X + j + 1)
                    nc.scalar.copy(kT[:, j, S:ST], c_bank(j)).then_inc(c_out, 1)
                for s in range(2):
                    ring.hi(act, (ONLY_X + KEYS) // 2 + 1, s, (n_ready, NT * (s + 1)))

            @block.vector
            def _(dve):
                with dve.Fori(0, ONLY_X // 2) as i:
                    for j in range(4):
                        dve.wait_ge(tile_ready, 4 * i + j + 1)
                        out = pT[:, bass.ds(4 * i + j, 1), :].rearrange("p a t -> p (a t)")
                        nc.vector.tensor_copy(out, x_bank(j)).then_inc(x_out, 1)
                for j in range(2 * KEYS):
                    dve.wait_ge(tile_ready, 2 * ONLY_X + j + 1)
                    nc.vector.tensor_copy(kT[:, j, 0:S], x_bank(j)).then_inc(x_out, 1)
                for n, (c, dst, t) in enumerate(jobs):
                    dve.wait_ge(n_ready, n + 1)
                    nc.vector.tensor_copy(dst[:, t, (c % 2) * CW : (c % 2 + 1) * CW], bank(env, n % 4, CW)).then_inc(n_out, 1)


def stage_fourier(env, pT, kT, uN, q_parts, k_parts):
    nc, A = env.nc, env.A
    with ExitStack() as ctx:
        sem = lambda name: env.semaphore("ff_" + name)
        sb = lambda name, shape: ctx.enter_context(nc.sbuf_tensor("ff_" + name, shape, F32))
        dft_t, dft_f = sb("dft_t", [P, 2, TX, S]), sb("dft_f", [P, 2, P])
        mid = sb("mid", [P, FT, 2, S])
        tables_in, token_ready, token_out, feat_ready, mixed, gated, scaled = (
            sem("tables_in"), sem("token"), sem("token_out"), sem("feature"), sem("mixed"), sem("gated"), sem("scaled"))
        hi_done, lo_done = sem("hi_done"), sem("lo_done")
        splits = [(q_parts, pT[:, f, :], f) for f in range(FT)] + [(k_parts, kT[:, f, :], f) for f in range(FT)]
        with nc.Block() as block:

            @block.sync
            def _(sp):
                sp.dma_start(dft_t[:], A["dft_t"]).then_inc(tables_in, 16)
                sp.dma_start(dft_f[:], A["dft_f"]).then_inc(tables_in, 16)

            @block.scalar
            def _(act):
                act.wait_ge(scaled, 1)
                for parts, x, f in splits:
                    nc.scalar.copy(parts[:, 0, f, :], x).then_inc(hi_done, 1)
                for j in range(1, 2 * FT, 2):
                    act.wait_ge(token_ready, j + 1)
                    nc.scalar.copy(mid[:, j // 2, j % 2, :], bank(env, j % 4)).then_inc(token_out, 1)
                    if j in (3, 5):
                        g = O_GD if j == 3 else O_GN
                        view = pT[:, g * FT : (g + 1) * FT, :]
                        nc.scalar.activation(view, view, ACT.Silu).then_inc(gated, 1)

            @block.gpsimd
            def _(pool):
                for n, (parts, x, f) in enumerate(splits):
                    pool.wait_ge(hi_done, n + 1)
                    nc.gpsimd.tensor_tensor(parts[:, 1, f, :], x, parts[:, 0, f, :].bitcast(F32), ALU.subtract).then_inc(lo_done, 1)

            @block.tensor
            def _(pe):
                pe.wait_ge(tables_in, 32)
                for j in range(2 * FT):
                    if j >= 4:
                        pe.wait_ge(mixed if j % 2 == 0 else token_out, j // 2 - 1)
                    for t in range(TX):
                        m = nc.tensor.matmul(
                            bank(env, j % 4), uN[:, t, (j // 2) * P : (j // 2 + 1) * P], dft_t[:, j % 2, t, :], start=t == 0, stop=t == TX - 1)
                    m.then_inc(token_ready, 1)
                for f in range(FT):
                    pe.wait_ge(mixed, f + 1)
                    pe.wait_ge(token_out, f + 1)
                    for c in range(2):
                        m = nc.tensor.matmul(bank(env, 4 + f), dft_f[:, c, :], mid[:, f, c, :], start=c == 0, stop=c == 1)
                    m.then_inc(feat_ready, 1)

            @block.vector
            def _(dve):
                nc.vector.tensor_scalar(pT[:, 0:FT, :], pT[:, 0:FT, :], C_HD**-0.5, None, ALU.mult).then_inc(scaled, 1)
                for f in range(FT):
                    dve.wait_ge(token_ready, 2 * f + 1)
                    nc.vector.tensor_copy(mid[:, f, 0, :], bank(env, 2 * f % 4)).then_inc(mixed, 1)
                dve.wait_ge(gated, 1)
                for f in range(FT):
                    dve.wait_ge(feat_ready, f + 1)
                    nc.vector.tensor_tensor(pT[:, O_GD * FT + f, :], bank(env, 4 + f), pT[:, O_GD * FT + f, :], ALU.mult).then_inc(mixed, 1)


def stage_neighbourhood(env, kT, vN, q_parts, k_parts, O):
    nc, A = env.nc, env.A
    UNITS = 2 * TX
    with ExitStack() as ctx:
        sem = lambda name: env.semaphore("na_" + name)
        sb = lambda name, shape: ctx.enter_context(nc.sbuf_tensor("na_" + name, shape, F32))
        bias = sb("bias", [P, C_HEADS, BIAS_SLOTS * GRID_W])
        q_stack = [ctx.enter_context(nc.sbuf_tensor(f"na_q_stack{h}", [P, 2, S], F32R)) for h in range(2)]
        k_stack = [ctx.enter_context(nc.sbuf_tensor(f"na_k_stack{h}", [P, ST], F32R)) for h in range(2)]
        scored = [sb(f"scored{b}", [P, S]) for b in range(2)]
        ex, exT = [kT[:, b, :] for b in range(2)], [kT[:, 2 + b, :] for b in range(2)]
        top, neg_max, sums, recip = sb("top", [P, 2, 2]), sb("neg_max", [P, 2]), sb("sums", [P, 4, 2]), sb("recip", [P, UNITS])
        bias_in, more_bias_in = sem("bias_in"), sem("more_bias_in")
        stacked, scores_ready = env.odd_stacked, sem("scores")
        max_ready, exp_done, turned, turned_out = sem("max"), sem("exp"), sem("turned"), sem("turned_out")
        pv_ready, o_out, dve_step = sem("pv"), sem("o_out"), sem("step")
        T0, O0 = 4 * BANK, 6 * BANK
        with nc.Block() as block:

            @block.sync
            def _(sp):
                for pairs, arrived in ((slice(0, 2), bias_in), (slice(2, C_HEADS), more_bias_in)):
                    sp.dma_start(bias[:, pairs], A["na_bias"][:, pairs]).then_inc(arrived, 16)
                Ring.prefetch(env, sp, A["w_out"][1])

            @block.gpsimd
            def _(pool):
                with pool.Fori(0, C_HEADS // 2) as i:
                    for h in range(2):
                        rows = slice(h * C_HD, (h + 1) * C_HD)
                        pool.wait_ge(scores_ready, UNITS * i + TX * (h + 1))
                        for z in range(2):
                            half = slice(z * C_HD, (z + 1) * C_HD)
                            source = q_parts[rows, :, bass.ds(i, 1), :].rearrange("p a f t -> p a (f t)")
                            pool.dma_start(q_stack[h][half], source).then_inc(stacked[h], 16)
                            source = k_parts[rows, z, bass.ds(i, 1), :].rearrange("p f t -> p (f t)")
                            pool.dma_start(k_stack[h][half], source).then_inc(stacked[h], 16)

            @block.tensor
            def _(pe):
                pe.sem_inc(scores_ready, UNITS)
                pe.sem_inc(turned, 2)
                pe.sem_inc(pv_ready, 2)
                with pe.Fori(0, C_HEADS // 2) as i:
                    n0 = UNITS * i

                    def scores(u):
                        h, qt = u // TX, u % TX
                        if qt == 0:
                            pe.wait_ge(stacked[h], 16 * 4 * i + 16 * 4)
                        pe.wait_ge(exp_done, n0 + u + 1)
                        for part in range(2):
                            q = q_stack[h][:, part, qt * P : (qt + 1) * P]
                            nc.tensor.matmul(bank(env, 2 * (u % 2)), q, k_stack[h][:, 0:S], start=part == 0, stop=part == 1)
                            r = nc.tensor.matmul(bank(env, 2 * (u % 2) + 1, L), q, k_stack[h][:, S:ST], start=part == 0, stop=part == 1)
                        r.then_inc(scores_ready, 1)

                    def turn(u):
                        pe.wait_ge(exp_done, n0 + u + 3)
                        pe.wait_ge(turned_out, n0 + u + 1)
                        for j in range(NT):
                            r = nc.tensor.transpose(env.PS[:, T0 + j * P : T0 + (j + 1) * P], ex[u % 2][:, j * P : (j + 1) * P], env.ident[:])
                        r.then_inc(turned, 1)

                    def pv(u):
                        pe.wait_ge(turned_out, n0 + u + 2)
                        pe.wait_ge(o_out, n0 + u + 1)
                        for j in range(NT):
                            v = vN[:, j, bass.ds(i * 2 * C_HD + (u // TX) * C_HD, C_HD)]
                            r = nc.tensor.matmul(
                                env.PS[:, O0 + (u % 2) * BANK : O0 + (u % 2) * BANK + C_HD],
                                exT[u % 2][:, j * P : (j + 1) * P], v, start=j == 0, stop=j == NT - 1)
                        r.then_inc(pv_ready, 1)

                    for u in range(UNITS + 3):
                        if u < UNITS:
                            scores(u)
                        if 2 <= u < UNITS + 2:
                            turn(u - 2)
                        if u >= 3:
                            pv(u - 3)

            @block.scalar
            def _(act):
                act.sem_inc(exp_done, 2)
                act.sem_inc(turned_out, 1)
                with act.Fori(0, C_HEADS // 2) as i:
                    n0 = UNITS * i

                    def exps(u):
                        act.wait_ge(max_ready, n0 + u + 1)
                        act.wait_ge(turned, n0 + u + 1)
                        nc.scalar.activation(ex[u % 2][:, 0:S], scored[u % 2][:], ACT.Exp, bias=neg_max[:, u % 2 : u % 2 + 1], accum_out=sums[:, u % 4, 0:1])
                        nc.scalar.activation(
                            ex[u % 2][:, S:ST], bank(env, 2 * (u % 2) + 1, L), ACT.Exp, bias=neg_max[:, u % 2 : u % 2 + 1],
                            accum_out=sums[:, u % 4, 1:2]).then_inc(exp_done, 1)

                    def copy_out(u):
                        act.wait_ge(turned, n0 + u + 3)
                        act.wait_ge(pv_ready, n0 + u + 1)
                        nc.scalar.copy(exT[u % 2][:], env.PS[:, T0 : T0 + ST]).then_inc(turned_out, 1)

                    for u in range(UNITS + 2):
                        if u >= 2:
                            copy_out(u - 2)
                        if u < UNITS:
                            exps(u)

            @block.vector
            def _(dve):
                dve.sem_inc(o_out, 2)
                dve.wait_ge(bias_in, 16)
                with dve.Fori(0, C_HEADS // 2) as i:
                    n0 = UNITS * i
                    st = Steps(dve, dve_step, 5 * UNITS * i)

                    def biased(u):
                        dve.wait_ge(scores_ready, n0 + u + 1 + UNITS)
                        dve.wait_ge(exp_done, n0 + u + 1)
                        first = (ROWS - 1 - 2 * (u % TX) - 1) * GRID_W
                        rows = bias[:, bass.ds(2 * i + u // TX, 1), first : first + S].rearrange("p a t -> p (a t)")
                        return st.inc(nc.vector.tensor_tensor(scored[u % 2][:], bank(env, 2 * (u % 2)), rows, ALU.add))

                    def maxima(u, written):
                        dve.wait_ge(dve_step, st.base + written)
                        st.inc(nc.vector.tensor_reduce(top[:, u % 2, 1:2], scored[u % 2][:], AX.X, ALU.max))
                        return st.inc(nc.vector.tensor_reduce(top[:, u % 2, 0:1], bank(env, 2 * (u % 2) + 1, L), AX.X, ALU.max))

                    def maximum(u, written):
                        dve.wait_ge(dve_step, st.base + written)
                        nc.vector.tensor_reduce(neg_max[:, u % 2 : u % 2 + 1], top[:, u % 2, :], AX.X, ALU.max, negate=True).then_inc(max_ready, 1)

                    def total(u):
                        dve.wait_ge(exp_done, n0 + u + 3)
                        return st.inc(nc.vector.tensor_tensor(recip[:, u : u + 1], sums[:, u % 4, 0:1], sums[:, u % 4, 1:2], ALU.add))

                    def inverse(u, written):
                        dve.wait_ge(dve_step, st.base + written)
                        st.inc(nc.vector.reciprocal(recip[:, u : u + 1], recip[:, u : u + 1]))

                    def out(u):
                        dve.wait_ge(pv_ready, n0 + u + 3)
                        nc.vector.tensor_scalar(
                            O[:, u % TX, bass.ds(i * 2 * C_HD + (u // TX) * C_HD, C_HD)],
                            env.PS[:, O0 + (u % 2) * BANK : O0 + (u % 2) * BANK + C_HD],
                            recip[:, u : u + 1], None, ALU.mult).then_inc(o_out, 1)

                    for u in range(UNITS + 4):
                        if u < UNITS:
                            scores_written = biased(u)
                        if 2 <= u < UNITS + 2:
                            total_written = total(u - 2)
                        if u >= 4:
                            if u >= UNITS + 2:
                                dve.wait_ge(dve_step, st.base + st.n)
                            out(u - 4)
                        if u < UNITS:
                            tops_written = maxima(u, scores_written)
                        if 2 <= u < UNITS + 2:
                            inverse(u - 2, total_written)
                        if u < UNITS:
                            maximum(u, tops_written)
                    dve.wait_ge(more_bias_in, 16)


def stage_neighbourhood_post(env, pT, O):
    nc = env.nc
    with ExitStack() as ctx:
        sem = lambda name: env.semaphore("np_" + name)
        turned, mixed = sem("turned"), sem("mixed")
        with nc.Block() as block:

            @block.tensor
            def _(pe):
                for f in range(FT):
                    for t in range(TX):
                        m = nc.tensor.transpose(bank(env, f, P, t * P), O[:, t, f * P : (f + 1) * P], env.ident[:])
                    m.then_inc(turned, 1)

            @block.vector
            def _(dve):
                for f in range(FT):
                    dve.wait_ge(turned, f + 1)
                    nc.vector.tensor_tensor(pT[:, O_GN * FT + f, :], bank(env, f), pT[:, O_GN * FT + f, :], ALU.mult).then_inc(mixed, 1)


def layer_odd(env, gain, shift):
    nc, A = env.nc, env.A
    with ExitStack() as layer:
        sb = lambda name, shape: layer.enter_context(nc.sbuf_tensor("odd_" + name, shape, F32))
        pT, kT, vN, uN = sb("pT", [P, 3 * FT, S]), sb("kT", [P, FT, ST]), sb("v", [P, NT, BW]), sb("u", [P, TX, BW])
        with ExitStack() as proj:
            env.split_operands(proj, "odd", ST)
            xs = pT[:].rearrange("p n t -> p (n t)").rearrange("p (t d) -> p t d", d=D)
            stage_norm(env, "norm1", [(env.X, TX, 0, gain(1, 0), shift(1, 0)), (env.CX, TC, TX, gain(1, 1), shift(1, 1))], xs, uN)
            stage_odd_proj(env, pT, kT, vN, uN)
        with ExitStack() as attention:
            q_parts = attention.enter_context(nc.sbuf_tensor("odd_q_parts", [P, 2, FT, S], F32R))
            k_parts = attention.enter_context(nc.sbuf_tensor("odd_k_parts", [P, 2, FT, ST], F32R))
            stage_fourier(env, pT, kT, uN, q_parts, k_parts)
            O = pT[:, 0:FT, :]
            stage_neighbourhood(env, kT, vN, q_parts, k_parts, O)
            stage_neighbourhood_post(env, pT, O)
        env.split_operands(layer, "out1", S)
        Y = sb("y", [P, TX, D])
        mix = [pT[:, g * FT + f, :] for g in (O_GN, O_GD) for f in range(FT)]
        stage_out(env, "out1", [(env.X, TX, 0, env.gate[:, 2, :])], mix, A["w_out"][1], Y, A["w_in_2"])


T_XS, T_B, T_C, T_R, T_K, T_V, T_LO, T_GL = 0, 4, 6, 8, 12, 16, 20, 21
RW_TILES = 14


def stage_second_proj(env, pT, zN, dtN):
    nc, A = env.nc, env.A
    TURNED, NATURAL = 11, 2
    LOOPS = TURNED // 2
    with ExitStack() as ctx:
        sem = lambda name: env.semaphore("sec_" + name)
        tile_ready, x_out, dt_ready, z_ready, z_out, consts_in = (
            sem("tile_ready"), sem("x_out"), sem("dt_ready"), sem("z_ready"), sem("z_out"), sem("consts_in"))
        w_dt_in, dt_hi, dt_lo = sem("w_dt_in"), sem("dt_hi"), sem("dt_lo")
        w_dt = ctx.enter_context(nc.sbuf_tensor("sec_w_dt", [P, KD, SSD_HEADS], F32))
        dt_parts = ctx.enter_context(nc.sbuf_tensor("sec_dt_parts", [P, 2, KD, SSD_HEADS], F32R))
        ring = Ring(env, "sec", A["w_in_2"], TURNED + NATURAL)
        zjobs = [(TURNED + h, h, t) for h in range(NATURAL) for t in range(TX)]
        with nc.Block() as block:

            @block.sync
            def _(sp):
                sp.dma_start(w_dt[:], A["w_dt"]).then_inc(w_dt_in, 16)
                ring.load_rest(sp)

            @block.gpsimd
            def _(pool):
                for name, tensor in env.C2.items():
                    source = A["c2_" + name]
                    if name in ROWS2:
                        source = source.partition_broadcast(P)
                    pool.dma_start(tensor[:], source).then_inc(consts_in, 16)
                ring.all_lo(pool)
                pool.wait_ge(dt_hi, 1)
                nc.gpsimd.tensor_tensor(dt_parts[:, 1], w_dt[:], dt_parts[:, 0].bitcast(F32), ALU.subtract).then_inc(dt_lo, 1)
                pool.wait_ge(consts_in, 16 * len(env.C2))

            @block.tensor
            def _(pe):
                def chunk(s, c, free):
                    pe.wait_ge(ring.lo_done, c + 1)
                    for f in range(2):
                        if free is not None:
                            pe.wait_ge(x_out, free + f)
                        ring.transposed(s, f, (bank(env, 2 * s + f),), ((0, S),)).then_inc(tile_ready, 1)

                for s in range(2):
                    chunk(s, s, None)
                with pe.Fori(1, LOOPS) as i:
                    for s in range(2):
                        chunk(s, 2 * i + s, 4 * i + 2 * s - 3)
                chunk(0, TURNED - 1, 2 * TURNED - 5)
                for n, (c, h, t) in enumerate(zjobs):
                    if t == 0:
                        pe.wait_ge(ring.lo_done, c + 1)
                    if n >= 2:
                        pe.wait_ge(z_out, n - 1)
                    ring.natural(c % 2, t, bank(env, 4 + n % 2, CW)).then_inc(z_ready, 1)
                pe.wait_ge(dt_lo, 1)
                for t in range(TX):
                    n = 0
                    for k in range(KD):
                        for wp, tp in PASSES:
                            m = nc.tensor.matmul(
                                bank(env, 6, SSD_HEADS, t * SSD_HEADS), env.tok[:, tp, k, t * P : (t + 1) * P], dt_parts[:, wp, k, :],
                                start=n == 0, stop=n == 3 * KD - 1)
                            n += 1
                m.then_inc(dt_ready, 1)

            @block.scalar
            def _(act):
                ring.hi(act, 0, 0)
                ring.hi(act, 0, 1)
                with act.Fori(0, LOOPS) as i:
                    for s in range(2):
                        ring.hi(act, i + 1, s, (tile_ready, 4 * i + 2 * s + 2))
                ring.hi(act, LOOPS + 1, 0, (tile_ready, 2 * TURNED))
                act.wait_ge(w_dt_in, 16)
                nc.scalar.copy(dt_parts[:, 0], w_dt[:]).then_inc(dt_hi, 1)
                for n, (c, h, t) in enumerate(zjobs):
                    act.wait_ge(z_ready, n + 1)
                    nc.scalar.activation(zN[:, t, h * CW : (h + 1) * CW], bank(env, 4 + n % 2, CW), ACT.Silu).then_inc(z_out, 1)
                act.wait_ge(dt_ready, 1)
                nc.scalar.copy(dtN[:], bank(env, 6, TX * SSD_HEADS)).then_inc(z_out, 1)

            @block.vector
            def _(dve):
                with dve.Fori(0, LOOPS) as i:
                    for j in range(4):
                        dve.wait_ge(tile_ready, 4 * i + j + 1)
                        out = pT[:, bass.ds(4 * i + j, 1), :].rearrange("p a t -> p (a t)")
                        nc.vector.tensor_copy(out, bank(env, j)).then_inc(x_out, 1)
                for n in range(4 * LOOPS, 2 * TURNED):
                    dve.wait_ge(tile_ready, n + 1)
                    nc.vector.tensor_copy(pT[:, n, :], bank(env, n % 4)).then_inc(x_out, 1)


GH = SSD_HEADS // 2
TH = TX * SSD_HEADS
HD = 64


def stage_ssd_prep(env, pT, dtN, V):
    nc, C2 = env.nc, env.C2
    with ExitStack() as ctx:
        sem = lambda name: env.semaphore("ssp_" + name)
        sb = lambda name, shape: ctx.enter_context(nc.sbuf_tensor("ssp_" + name, shape, F32))
        xd, mag, a, neg_a = sb("xd", [P, TH]), sb("mag", [P, TH]), sb("a", [P, TH]), sb("neg_a", [P, TH])
        conv_done, silu_done, turned, turned_out = sem("conv"), sem("silu"), sem("turned"), sem("turned_out")
        dt_in, dt_act, a_ready, cum_ready, cum_act, step, act_step = (
            sem("dt_in"), sem("dt_act"), sem("a"), sem("cum"), sem("cum_act"), sem("step"), sem("act_step"))
        with nc.Block() as block:

            @block.vector
            def _(dve):
                st = Steps(dve, step)
                nc.vector.tensor_tensor(xd[:], dtN[:], C2["dt_bias"][:], ALU.add).then_inc(dt_in, 1)
                dve.wait_ge(dt_act, 1)
                st.link(nc.vector.scalar_tensor_tensor(V["dt"][:], xd[:], 0.0, mag[:], ALU.max, ALU.add))
                nc.vector.scalar_tensor_tensor(a[:], V["dt"][:], -1.0, neg_a[:], ALU.mult, ALU.mult).then_inc(a_ready, 1)
                dve.wait_ge(a_ready, 1)
                dve.wait_ge(cum_ready, 1)
                st.link(nc.vector.tensor_copy(V["acs"][:], bank(env, 7, TH)))
                nc.vector.tensor_tensor(V["dstate"][:], bank(env, 7, TH, TH), V["acs"][:], ALU.subtract).then_inc(cum_act, 1)
                st.link(nc.vector.tensor_copy(V["a"][:], a[:]))
                for f in range(8):
                    y = V["conv"][:, f, :]
                    st.link(nc.vector.tensor_scalar(y, pT[:, f, :], C2["ssd_taps"][:, f, 3:4], C2["ssd_conv_b"][:, f : f + 1], ALU.mult, ALU.add))
                    for i in range(3):
                        back = 3 - i
                        m = nc.vector.scalar_tensor_tensor(
                            y[:, back:S], pT[:, f, 0 : S - back], C2["ssd_taps"][:, f, i : i + 1], y[:, back:S], ALU.mult, ALU.add)
                        if i < 2:
                            st.link(m)
                        else:
                            m.then_inc(conv_done, 1)
                for t in range(TX):
                    dve.wait_ge(turned, t + 1)
                    nc.vector.tensor_copy(V["xs"][:, t, :], bank(env, 2 * (t % 2))).then_inc(turned_out, 1)
                    nc.vector.tensor_copy(V["B"][:, t, :], bank(env, 2 * (t % 2) + 1, 2 * SSD_STATE)).then_inc(turned_out, 1)
                dve.wait_ge(turned_out, 2 * TX)
                xs = V["xs"][:].rearrange("p t (h d) -> p (t h) d", d=HD)
                wide = lambda v: v[:].unsqueeze(2).to_broadcast([P, TH, HD])
                for t in range(TX):
                    st.inc(nc.vector.tensor_tensor(V["skip"][:, t, :], V["xs"][:, t, :], C2["ssd_d"][:], ALU.mult))
                st.link(nc.vector.tensor_tensor(V["xdt"][:].rearrange("p t (h d) -> p (t h) d", d=HD), xs, wide(V["dt"]), ALU.mult))
                dve.wait_ge(cum_act, 2)
                st.link(nc.vector.tensor_tensor(
                    V["xds"][:].rearrange("p t (h d) -> p (t h) d", d=HD),
                    V["xdt"][:].rearrange("p t (h d) -> p (t h) d", d=HD), wide(V["dstate"]), ALU.mult))

            @block.scalar
            def _(act):
                st = Steps(act, act_step)
                st.link(nc.scalar.activation(neg_a[:], C2["a_log"][:], ACT.Exp))
                act.wait_ge(dt_in, 1)
                st.link(nc.scalar.activation(mag[:], xd[:], ACT.Abs))
                st.link(nc.scalar.activation(mag[:], mag[:], ACT.Exp, scale=-1.0))
                nc.scalar.activation(mag[:], mag[:], ACT.Ln, bias=1.0).then_inc(dt_act, 1)
                act.wait_ge(cum_act, 1)
                st.inc(nc.scalar.activation(V["eacs"][:], V["acs"][:], ACT.Exp))
                st.inc(nc.scalar.activation(V["etot"][:], bank(env, 7, TH, TH), ACT.Exp))
                nc.scalar.activation(V["dstate"][:], V["dstate"][:], ACT.Exp).then_inc(cum_act, 1)
                for f in range(8):
                    act.wait_ge(conv_done, f + 1)
                    nc.scalar.activation(V["conv"][:, f, :], V["conv"][:, f, :], ACT.Silu).then_inc(silu_done, 1)

            @block.tensor
            def _(pe):
                pe.wait_ge(a_ready, 1)
                nc.tensor.matmul(bank(env, 7, TH), C2["upto"][:], a[:], start=True, stop=True)
                nc.tensor.matmul(bank(env, 7, TH, TH), C2["ones"][:], a[:], start=True, stop=True).then_inc(cum_ready, 1)
                pe.wait_ge(silu_done, T_C)
                for t in range(TX):
                    if t >= 2:
                        pe.wait_ge(turned_out, 2 * (t - 1))
                    for f in range(FT):
                        nc.tensor.transpose(bank(env, 2 * (t % 2), P, f * P), V["conv"][:, f, t * P : (t + 1) * P], env.ident[:])
                    for g in range(2):
                        m = nc.tensor.transpose(bank(env, 2 * (t % 2) + 1, P, g * P), V["conv"][:, T_B + g, t * P : (t + 1) * P], env.ident[:])
                    m.then_inc(turned, 1)


def stage_ssd(env, V, zN, mix):
    nc, C2 = env.nc, env.C2
    with ExitStack() as ctx:
        sem = lambda name: env.semaphore("ssd_" + name)
        sb = lambda name, shape: ctx.enter_context(nc.sbuf_tensor("ssd_" + name, shape, F32))
        tri_a, decay, scores = sb("tri_a", [P, 2, GH, P]), sb("decay", [P, 2, GH, P]), sb("scores", [P, 2, P])
        state, y, ss = sb("state", [P, BW]), sb("y", [P, TX, BW]), sb("ss", [P, TX * 2])
        sq = V["xs"][:].rearrange("p t c -> p (t c)")
        tri_ready, row_ready, diff_ready, decayed, weighed, scores_read = (
            sem("tri"), sem("row"), sem("diff"), sem("decayed"), sem("weighed"), sem("scores_read"))
        diag_ready, scores_ready, new_ready, y_read, state_ready, step, root_ready, mean_ready, turned, normed, mixed = (
            sem("diag"), sem("scores"), sem("new"), sem("y_read"), sem("state"), sem("step"), sem("root"), sem("mean"), sem("turned"),
            sem("normed"), sem("mixed"))
        units = [(t, g) for t in range(TX) for g in range(2)]
        with nc.Block() as block:

            @block.gpsimd
            def _(pool):
                for n, (t, g) in enumerate(units):
                    if n >= 2:
                        pool.wait_ge(row_ready, n - 1)
                    for h in range(GH):
                        th = t * SSD_HEADS + g * GH + h
                        m = nc.gpsimd.tensor_scalar(tri_a[:, n % 2, h, :], C2["upto"][:], V["a"][:, th : th + 1], None, ALU.mult)
                    m.then_inc(tri_ready, 1)

            @block.tensor
            def _(pe):
                def rows(n):
                    t, g = units[n]
                    tok = slice(t * P, (t + 1) * P)
                    pe.wait_ge(tri_ready, n + 1)
                    if n >= 2:
                        pe.wait_ge(scores_read, n - 1)
                        pe.wait_ge(diff_ready, n - 1)
                    nc.tensor.matmul(bank(env, n % 2), C2["ones"][:], tri_a[:, n % 2].rearrange("p h l -> p (h l)"), start=True, stop=True).then_inc(
                        row_ready, 1)
                    nc.tensor.matmul(
                        bank(env, 2 + n % 2, P), V["conv"][:, T_B + g, tok], V["conv"][:, T_C + g, tok], start=True, stop=True).then_inc(
                        scores_ready, 1)

                rows(0)
                for n, (t, g) in enumerate(units):
                    tok = slice(t * P, (t + 1) * P)
                    if n + 1 < len(units):
                        rows(n + 1)
                    pe.wait_ge(weighed, n + 1)
                    if t >= 1:
                        pe.wait_ge(y_read, t)
                    for h in range(GH):
                        c = (g * GH + h) * HD
                        m = nc.tensor.matmul(
                            bank(env, 4, HD, c), decay[:, n % 2, h, :], V["xdt"][:, t, c : c + HD], start=True, stop=True)
                    m.then_inc(diag_ready, 1)
                    if g == 1:
                        if t >= 1:
                            pe.wait_ge(state_ready, t)
                            for q in range(2):
                                m = nc.tensor.matmul(
                                    bank(env, 5, 2 * P, q * 2 * P), V["conv"][:, T_C + q, tok], state[:, q * 2 * P : (q + 1) * 2 * P], start=True, stop=True)
                        for q in range(2):
                            m = nc.tensor.matmul(
                                bank(env, 6, 2 * P, q * 2 * P), V["B"][:, t, q * P : (q + 1) * P], V["xds"][:, t, q * 2 * P : (q + 1) * 2 * P], start=True, stop=True)
                        m.then_inc(new_ready, 1)
                pe.wait_ge(normed, 1)
                for f in range(FT):
                    for t in range(TX):
                        m = nc.tensor.transpose(bank(env, f, P, t * P), y[:, t, f * P : (f + 1) * P], env.ident[:])
                    m.then_inc(turned, 1)

            @block.scalar
            def _(act):
                for n in range(len(units)):
                    act.wait_ge(diff_ready, n + 1)
                    nc.scalar.activation(decay[:, n % 2], decay[:, n % 2], ACT.Exp).then_inc(decayed, 1)
                act.wait_ge(mean_ready, 1)
                nc.scalar.activation(ss[:], ss[:], ACT.Sqrt).then_inc(root_ready, 1)

            @block.vector
            def _(dve):
                st = Steps(dve, step)

                def differ(n):
                    t, g = units[n]
                    dve.wait_ge(row_ready, n + 1)
                    if n >= 2:
                        dve.wait_ge(diag_ready, n - 1)
                    for h in range(GH):
                        th = t * SSD_HEADS + g * GH + h
                        m = nc.vector.tensor_scalar(
                            decay[:, n % 2, h, :], bank(env, n % 2, P, h * P), V["acs"][:, th : th + 1], 0.0, ALU.subtract, ALU.min)
                    m.then_inc(diff_ready, 1)
                    dve.wait_ge(scores_ready, n + 1)
                    nc.vector.tensor_tensor(scores[:, n % 2, :], bank(env, 2 + n % 2, P), C2["upto"][:], ALU.mult).then_inc(scores_read, 1)

                differ(0)
                for n, (t, g) in enumerate(units):
                    if n + 1 < len(units):
                        differ(n + 1)
                    dve.wait_ge(decayed, n + 1)
                    dve.wait_ge(scores_read, n + 1)
                    nc.vector.tensor_tensor(
                        decay[:, n % 2], decay[:, n % 2], scores[:, n % 2, :].unsqueeze(1).to_broadcast([P, GH, P]), ALU.mult).then_inc(weighed, 1)
                    if g == 0:
                        continue
                    th = slice(t * SSD_HEADS, (t + 1) * SSD_HEADS)
                    wide = lambda v: v[:, th].unsqueeze(2).to_broadcast([P, SSD_HEADS, HD])
                    by_head = lambda v: v.rearrange("p (h d) -> p h d", d=HD)
                    out = y[:, t, :]
                    dve.wait_ge(new_ready, t + 1)
                    st.link(nc.vector.tensor_tensor(out, bank(env, 4), V["skip"][:, t, :], ALU.add))
                    if t >= 1:
                        st.link(nc.vector.tensor_tensor(by_head(sq[:, 0:BW]), by_head(bank(env, 5)), wide(V["eacs"]), ALU.mult))
                        st.link(nc.vector.tensor_tensor(out, out, sq[:, 0:BW], ALU.add))
                        st.link(nc.vector.tensor_tensor(by_head(state[:]), by_head(state[:]), wide(V["etot"]), ALU.mult))
                        m = nc.vector.tensor_tensor(state[:], state[:], bank(env, 6), ALU.add)
                    else:
                        m = nc.vector.tensor_copy(state[:], bank(env, 6))
                    m.then_inc(state_ready, 1)
                    dve.wait_ge(state_ready, t + 1)
                    nc.vector.tensor_tensor(out, out, zN[:, t, :], ALU.mult).then_inc(y_read, 1)
                dve.wait_ge(y_read, TX)
                flat = y[:].rearrange("p t c -> p (t c)")
                st.link(nc.vector.tensor_tensor(sq[:], flat, flat, ALU.mult))
                st.link(nc.vector.tensor_reduce(ss[:], sq[:].rearrange("p (g c) -> p g c", c=2 * P), AX.X, ALU.add))
                nc.vector.tensor_scalar(ss[:], ss[:], 1.0 / (2 * P), EPS, ALU.mult, ALU.add).then_inc(mean_ready, 1)
                dve.wait_ge(root_ready, 1)
                st.link(nc.vector.reciprocal(ss[:], ss[:]))
                groups = flat.rearrange("p (g c) -> p g c", c=2 * P)
                nc.vector.tensor_tensor(groups, groups, ss[:].unsqueeze(2).to_broadcast([P, TX * 2, 2 * P]), ALU.mult).then_inc(normed, 1)
                for f in range(FT):
                    dve.wait_ge(turned, f + 1)
                    nc.vector.tensor_scalar(mix[:, f, :], bank(env, f), C2["ssd_norm"][:, f : f + 1], None, ALU.mult).then_inc(mixed, 1)


LEVELS = RW_CHUNK.bit_length() - 1
CHUNKS = S // RW_CHUNK


def stage_rwkv_shift(env, pT, quarter):
    nc, C2 = env.nc, env.C2
    with ExitStack() as ctx:
        sem = lambda name: env.semaphore("rws_" + name)
        keep = ctx.enter_context(nc.sbuf_tensor("rws_keep", [P, RW_TILES], F32))
        diff, step, mixed = sem("diff"), sem("step"), sem("mixed")
        slot = lambda n: quarter[n // FT][:, n % FT, 0 : S - 1]
        with nc.Block() as block:

            @block.gpsimd
            def _(pool):
                for n in range(0, RW_TILES, 2):
                    p = pT[:, T_R + n, :]
                    nc.gpsimd.tensor_tensor(slot(n), p[:, 0 : S - 1], p[:, 1:S], ALU.subtract).then_inc(diff, 1)

            @block.vector
            def _(dve):
                st = Steps(dve, step)
                st.link(nc.vector.tensor_scalar(keep[:], C2["mu"][:], -1.0, 1.0, ALU.mult, ALU.add))
                for n in range(1, RW_TILES, 2):
                    p = pT[:, T_R + n, :]
                    st.link(nc.vector.tensor_tensor(slot(n), p[:, 0 : S - 1], p[:, 1:S], ALU.subtract))
                for k, n in enumerate([*range(1, RW_TILES, 2), *range(0, RW_TILES, 2)]):
                    if n % 2 == 0:
                        dve.wait_ge(diff, n // 2 + 1)
                    p = pT[:, T_R + n, :]
                    nc.vector.scalar_tensor_tensor(p[:, 1:S], slot(n), C2["mu"][:, n : n + 1], p[:, 1:S], ALU.mult, ALU.add).then_inc(mixed, 1)
                first = pT[:, T_R : T_R + RW_TILES, 0:1].rearrange("p n a -> p (n a)")
                nc.vector.tensor_tensor(first, first, keep[:], ALU.mult).then_inc(mixed, 1)


def stage_rwkv_features(env, pT, W, quarter):
    nc, C2 = env.nc, env.C2
    with ExitStack() as ctx:
        sem = lambda name: env.semaphore("rwf_" + name)
        sb = lambda name: ctx.enter_context(nc.sbuf_tensor("rwf_" + name, [P, FT, S], F32))
        lw, cum, inv, pex = quarter
        kkn, a, pin = sb("kkn"), sb("a"), sb("pin")
        less_ka = ctx.enter_context(nc.sbuf_tensor("rwf_less_ka", [P, FT], F32))
        r, k, v = (pT[:, x : x + FT, :] for x in (T_R, T_K, T_V))
        bT, kT = pT[:, 0:FT, :], pT[:, FT : 2 * FT, :]
        lora_act, u_ready, sig_done, g_ready, g_out, sq_done = sem("lora"), sem("u"), sem("sig"), sem("g"), sem("g_out"), sem("sq")
        norm_ready, norm_out, cum_ready, exp_done, step, act_step = sem("norm"), sem("norm_out"), sem("cum"), sem("exp"), sem("step"), sem("act_step")
        b_ready, k_ready, rk_ready, kp_ready, r_done, turned, turned_out, bonus_ready = (
            sem("b"), sem("k"), sem("rk"), sem("kp"), sem("r"), sem("turned"), sem("turned_out"), sem("bonus"))
        naturals = [(W["v"], v), (W["b"], bT), (W["k"], kT)]
        with nc.Block() as block:

            @block.scalar
            def _(act):
                st = Steps(act, act_step)
                lo, gl = pT[:, T_LO, :], pT[:, T_GL, :]
                nc.scalar.activation(lo[0:HD], lo[0:HD], ACT.Tanh).then_inc(lora_act, 1)
                nc.scalar.activation(gl, gl, ACT.Sigmoid).then_inc(lora_act, 1)
                for f in range(FT):
                    act.wait_ge(u_ready, 2 * f + 1)
                    nc.scalar.activation(lw[:, f, :], bank(env, f % 2), ACT.Sigmoid, bias=C2["w0"][:, f : f + 1]).then_inc(sig_done, 1)
                    act.wait_ge(u_ready, 2 * f + 2)
                    nc.scalar.activation(a[:, f, :], bank(env, 2 + f % 2), ACT.Sigmoid, bias=C2["a0"][:, f : f + 1]).then_inc(sig_done, 1)
                for f in range(FT):
                    nc.scalar.activation(kkn[:, f, :], k[:, f, :], ACT.Square, scale=C2["k_k"][:, f : f + 1]).then_inc(sq_done, 1)
                for f in range(FT):
                    act.wait_ge(g_ready, f + 1)
                    nc.scalar.copy(W["g"][:, f, :], bank(env, f % 2)).then_inc(g_out, 1)
                for f in range(FT):
                    act.wait_ge(norm_ready, f + 1)
                    nc.scalar.activation(pin[:, f, :], bank(env, 4 + f), ACT.Sqrt).then_inc(norm_out, 1)
                act.wait_ge(cum_ready, 1)
                nc.scalar.activation(inv, cum, ACT.Exp, scale=-1.0).then_inc(exp_done, 1)
                act.wait_ge(cum_ready, 2)
                nc.scalar.activation(pex, pex, ACT.Exp).then_inc(exp_done, 1)
                act.wait_ge(cum_ready, 3)
                nc.scalar.activation(pin[:], cum, ACT.Exp).then_inc(exp_done, 1)
                for n in range(3 * TX):
                    act.wait_ge(turned, n + 1)
                    nc.scalar.copy(naturals[n // TX][0][:, n % TX, :], bank(env, n % 4)).then_inc(turned_out, 1)

            @block.tensor
            def _(pe):
                pe.wait_ge(lora_act, 1)
                for f in range(FT):
                    if f >= 2:
                        pe.wait_ge(sig_done, 2 * (f - 1))
                    for j, rows in enumerate((slice(0, HD), slice(HD, P))):
                        nc.tensor.matmul(
                            bank(env, 2 * j + f % 2), C2["lora"][rows, f * P : (f + 1) * P], pT[rows, T_LO, :], start=True, stop=True
                        ).then_inc(u_ready, 1)
                pe.wait_ge(lora_act, 2)
                pe.wait_ge(sig_done, 2 * FT)
                for f in range(FT):
                    if f >= 2:
                        pe.wait_ge(g_out, f - 1)
                    nc.tensor.matmul(bank(env, f % 2), C2["g2"][:, f * P : (f + 1) * P], pT[:, T_GL, :], start=True, stop=True).then_inc(g_ready, 1)
                for f in range(FT):
                    pe.wait_ge(sq_done, f + 1)
                    nc.tensor.matmul(bank(env, 4 + f), C2["pair"][:], kkn[:, f, :], start=True, stop=True).then_inc(norm_ready, 1)
                pe.wait_ge(g_out, FT)
                for n in range(3 * TX):
                    if n >= 4:
                        pe.wait_ge(turned_out, n - 3)
                    src, t = naturals[n // TX][1], n % TX
                    if n == TX:
                        pe.wait_ge(b_ready, 1)
                    if n == 2 * TX:
                        pe.wait_ge(k_ready, 1)
                    for f in range(FT):
                        m = nc.tensor.transpose(bank(env, n % 4, P, f * P), src[:, f, t * P : (t + 1) * P], env.ident[:])
                    m.then_inc(turned, 1)
                pe.wait_ge(rk_ready, 1)
                pe.wait_ge(norm_out, FT)
                for t in range(TX):
                    for f in range(FT):
                        m = nc.tensor.matmul(
                            bank(env, 4, SSD_HEADS, t * SSD_HEADS), lw[:, f, t * P : (t + 1) * P], C2["r_k"][:, f, :], start=f == 0, stop=f == FT - 1)
                m.then_inc(bonus_ready, 1)

            @block.gpsimd
            def _(pool):
                pool.wait_ge(kp_ready, 1)
                nc.gpsimd.tensor_tensor(lw, r, kT, ALU.mult).then_inc(rk_ready, 1)
                pool.wait_ge(rk_ready, 1)
                pool.wait_ge(exp_done, 3)
                nc.gpsimd.tensor_tensor(r, r, pin[:], ALU.mult).then_inc(r_done, 1)

            @block.vector
            def _(dve):
                st = Steps(dve, step)
                st.link(nc.vector.tensor_scalar(less_ka[:], C2["k_a"][:], -1.0, 1.0, ALU.mult, ALU.add))
                for f in range(FT):
                    dve.wait_ge(sig_done, 2 * f + 1)
                    st.link(nc.vector.tensor_scalar(lw[:, f, :], lw[:, f, :], -RW_DECAY_SCALE, None, ALU.mult))
                    m = nc.vector.tensor_tensor_scan(cum[:, f, :], C2["reset"][:], lw[:, f, :], 0.0, ALU.mult, ALU.add)
                    if f < FT - 1:
                        st.link(m)
                m.then_inc(cum_ready, 1)
                dve.wait_ge(cum_ready, 1)
                nc.vector.tensor_tensor(pex, cum, lw, ALU.subtract).then_inc(cum_ready, 1)
                dve.wait_ge(norm_out, FT)
                st.link(nc.vector.tensor_scalar(pin[:], pin[:], 1e-12, None, ALU.max))
                st.link(nc.vector.reciprocal(pin[:], pin[:]))
                for f in range(FT):
                    m = nc.vector.scalar_tensor_tensor(kkn[:, f, :], k[:, f, :], C2["k_k"][:, f : f + 1], pin[:, f, :], ALU.mult, ALU.mult)
                    if f < FT - 1:
                        st.inc(m)
                m.then_inc(cum_ready, 1)
                dve.wait_ge(cum_ready, 3)
                dve.wait_ge(step, st.n)
                dve.wait_ge(sig_done, 2 * FT)
                st.link(nc.vector.tensor_tensor(bT, kkn[:], a[:], ALU.mult))
                dve.wait_ge(exp_done, 1)
                nc.vector.tensor_tensor(bT, bT, inv, ALU.mult).then_inc(b_ready, 1)
                for f in range(FT):
                    st.link(nc.vector.tensor_scalar(a[:, f, :], a[:, f, :], C2["k_a"][:, f : f + 1], less_ka[:, f : f + 1], ALU.mult, ALU.add))
                nc.vector.tensor_tensor(kT, k, a[:], ALU.mult).then_inc(kp_ready, 1)
                dve.wait_ge(exp_done, 2)
                dve.wait_ge(kp_ready, 1)
                st.link(nc.vector.scalar_tensor_tensor(k, kkn[:], -1.0, pex, ALU.mult, ALU.mult))
                dve.wait_ge(rk_ready, 1)
                nc.vector.tensor_tensor(kT, kT, inv, ALU.mult).then_inc(k_ready, 1)
                dve.wait_ge(exp_done, 3)
                ends = pin[:].rearrange("p f (c j) -> p f c j", j=RW_CHUNK)[:, :, :, RW_CHUNK - 1]
                st.link(nc.vector.tensor_copy(W["end"][:], ends))
                dve.wait_ge(bonus_ready, 1)
                st.link(nc.vector.tensor_copy(W["bonus"][:], bank(env, 4, TH)))


def stage_rwkv_matrices(env, pT, W, quarter):
    nc, C2 = env.nc, env.C2
    batches = [(t, q) for t in range(TX) for q in range(2)]
    with ExitStack() as ctx:
        sem = lambda name: env.semaphore("rwm_" + name)
        product, masked, kept, values, values_out = sem("product"), sem("masked"), sem("kept"), sem("values"), sem("values_out")
        AM = [quarter[b].rearrange("p k n -> p (k n)").rearrange("p (h m l) -> p h m l", h=GH, m=4) for b in range(2)]
        with nc.Block() as block:

            @block.tensor
            def _(pe):
                def products(n):
                    t, q = batches[n]
                    tok = slice(t * P, (t + 1) * P)
                    for hl in range(GH):
                        h = q * GH + hl
                        f, rows = h // 2, slice((h % 2) * HD, (h % 2 + 1) * HD)
                        if n:
                            pe.wait_ge(masked, (n - 1) * GH + hl + 1)
                        ra = pT[rows, T_R + f : T_K + f + 1 : FT, tok]
                        nc.tensor.matmul(bank(env, hl, 2 * P), pT[rows, f, tok], ra, start=True, stop=True)
                        nc.tensor.matmul(bank(env, hl, 2 * P, 2 * P), pT[rows, FT + f, tok], ra, start=True, stop=True).then_inc(product, 1)

                def times_v(n):
                    t, q = batches[n]
                    pe.wait_ge(masked, (n + 1) * GH)
                    if n >= 2:
                        pe.wait_ge(values_out, 2 * (n - 1))
                    for m in (3, 2):
                        for hl in range(GH):
                            c = (q * GH + hl) * HD
                            x = nc.tensor.matmul(
                                bank(env, 4 + 2 * (n % 2) + (3 - m), HD, hl * HD), AM[n % 2][:, hl, m, :], W["v"][:, t, c : c + HD], start=True, stop=True)
                        x.then_inc(values, 1)

                products(0)
                for n in range(len(batches)):
                    if n + 1 < len(batches):
                        products(n + 1)
                    times_v(n)

            @block.vector
            def _(dve):
                for n in range(len(batches)):
                    if n >= 2:
                        dve.wait_ge(values, 2 * (n - 1))
                        dve.wait_ge(kept, 2 * (n - 1))
                    for hl in range(GH):
                        dve.wait_ge(product, n * GH + hl + 1)
                        nc.vector.tensor_tensor(AM[n % 2][:, hl], bank(env, hl).rearrange("p (m l) -> p m l", m=4), C2["within"][:], ALU.mult).then_inc(masked, 1)

            @block.gpsimd
            def _(pool):
                for n, (t, q) in enumerate(batches):
                    pool.wait_ge(masked, (n + 1) * GH)
                    heads = slice(q * GH, (q + 1) * GH)
                    nc.gpsimd.tensor_copy(W["rb"][:, t, heads, :], AM[n % 2][:, :, 0, :]).then_inc(kept, 1)
                    nc.gpsimd.tensor_copy(W["inv"][:, t, heads, :], AM[n % 2][:, :, 1, :]).then_inc(kept, 1)

            @block.scalar
            def _(act):
                for n, (t, q) in enumerate(batches):
                    for m, out in enumerate((W["akv"], W["rkv"])):
                        act.wait_ge(values, 2 * n + m + 1)
                        nc.scalar.copy(out[:, t, q * GH * HD : (q + 1) * GH * HD], bank(env, 4 + 2 * (n % 2) + m, GH * HD)).then_inc(values_out, 1)


def stage_rwkv_inverse(env, W, quarter):
    nc, C2 = env.nc, env.C2
    batches = [(t, q) for t in range(TX) for q in range(2)]
    with ExitStack() as ctx:
        sem = lambda name: env.semaphore("rwi_" + name)
        cut, first, first_out, second, third, x_out, xt_out = ([sem(f"{n}{b}") for b in range(2)] for n in (
            "cut", "first", "first_out", "second", "third", "x_out", "xt_out"))
        part = lambda b, j: quarter[(5 * b + j) // FT][:, (5 * b + j) % FT, :].rearrange("p (h l) -> p h l", h=GH)
        ident4 = env.ident[:].unsqueeze(1).to_broadcast([P, GH, P])
        steps = [(p, lv) for p in range(len(batches) // 2) for lv in range(LEVELS)]
        nT = lambda b, n: part(b, n % 2)
        t1 = lambda b: part(b, 2)
        x = lambda b: part(b, 3)
        xt = lambda b: part(b, 4)

        def home(b, p):
            t, q = batches[2 * p + b]
            return W["inv"][:, t, q * GH : (q + 1) * GH, :]

        bk = lambda b, j: bank(env, 3 * b + j).rearrange("p (h l) -> p h l", h=GH)
        with nc.Block() as block:

            @block.gpsimd
            def _(pool):
                for n, (p, lv) in enumerate(steps):
                    for b in range(2):
                        if n >= 2:
                            pool.wait_ge(first[b], n - 1)
                        nc.gpsimd.tensor_tensor(nT(b, n), home(b, p), C2["level"][:, lv, :].unsqueeze(1).to_broadcast([P, GH, P]), ALU.mult).then_inc(cut[b], 1)

            @block.tensor
            def _(pe):
                def one(b, n):
                    p, lv = steps[n]
                    pe.wait_ge(cut[b], n + 1)
                    if n:
                        pe.wait_ge(x_out[b], n)
                        pe.wait_ge(xt_out[b], n)
                        pe.wait_ge(first_out[b], n)
                    for h in range(GH):
                        m = nc.tensor.matmul(bk(b, 0)[:, h], nT(b, n)[:, h], env.ident[:] if lv == 0 else x(b)[:, h], start=True, stop=True)
                    m.then_inc(first[b], 1)

                def two(b, n):
                    p, lv = steps[n]
                    pe.wait_ge(first_out[b], n + 1)
                    for h in range(GH):
                        m = nc.tensor.matmul(bk(b, 1)[:, h], env.ident[:] if lv == 0 else xt(b)[:, h], t1(b)[:, h], start=True, stop=True)
                    m.then_inc(second[b], 1)
                    for h in range(GH):
                        m = nc.tensor.matmul(bk(b, 2)[:, h], t1(b)[:, h], env.ident[:] if lv == 0 else xt(b)[:, h], start=True, stop=True)
                    m.then_inc(third[b], 1)

                for n in range(len(steps)):
                    for b in range(2):
                        one(b, n)
                    for b in range(2):
                        two(b, n)

            @block.scalar
            def _(act):
                for n in range(len(steps)):
                    for b in range(2):
                        act.wait_ge(first[b], n + 1)
                        if n:
                            act.wait_ge(third[b], n)
                        nc.scalar.copy(t1(b), bk(b, 0)).then_inc(first_out[b], 1)

            @block.vector
            def _(dve):
                for n, (p, lv) in enumerate(steps):
                    for b in range(2):
                        dve.wait_ge(second[b], n + 1)
                        nc.vector.tensor_tensor(x(b), bk(b, 1), ident4 if lv == 0 else x(b), ALU.add).then_inc(x_out[b], 1)
                        dve.wait_ge(third[b], n + 1)
                        dve.wait_ge(cut[b], n + 1)
                        out = home(b, p) if lv == LEVELS - 1 else xt(b)
                        nc.vector.tensor_tensor(out, bk(b, 2), ident4 if lv == 0 else xt(b), ALU.add).then_inc(xt_out[b], 1)


def stage_rwkv_scan(env, pT, W, y):
    nc, C2 = env.nc, env.C2
    with ExitStack() as ctx:
        sem = lambda name: env.semaphore("rwk_" + name)
        state, new = (pT[:, FT + j, :].rearrange("p (f n) -> p f n", f=FT) for j in range(2))
        rhs, U = pT[:, FT + 2, :], pT[:, FT + 3, :]
        zeroed, as_ready, rhs_ready, u_ready, u_out, y_ready, y_out, new_ready, state_ready, step = (
            sem("zeroed"), sem("as"), sem("rhs"), sem("u"), sem("u_out"), sem("y"), sem("y_out"), sem("new"), sem("state"), sem("step"))
        with nc.Block() as block:

            @block.sync
            def _(sp):
                Ring.prefetch(env, sp, env.A["w_out_2"])

            @block.tensor
            def _(pe):
                for c in range(CHUNKS):
                    t, half = c // 2, slice((c % 2) * HD, (c % 2 + 1) * HD)
                    tok = slice(t * P, (t + 1) * P)
                    pe.wait_ge(state_ready, c + 1)
                    for f in range(FT):
                        m = nc.tensor.matmul(bank(env, 0, P, f * P), pT[:, T_K + f, tok], state[:, f, :], start=True, stop=True)
                    m.then_inc(as_ready, 1)
                    pe.wait_ge(rhs_ready, c + 1)
                    for h in range(SSD_HEADS):
                        m = nc.tensor.matmul(bank(env, 1, HD, h * HD), W["inv"][:, t, h, :], rhs[:, h * HD : (h + 1) * HD], start=True, stop=True)
                    m.then_inc(u_ready, 1)
                    pe.wait_ge(u_out, c + 1)
                    for f in range(FT):
                        cols = slice(f * P, (f + 1) * P)
                        nc.tensor.matmul(bank(env, 4 + c % 2, P, f * P), W["b"][half, t, cols], U[half, cols], start=True, stop=False)
                        m = nc.tensor.matmul(bank(env, 4 + c % 2, P, f * P), W["k"][half, t, cols], W["v"][half, t, cols], start=False, stop=True)
                    m.then_inc(new_ready, 1)
                    if c >= 2:
                        pe.wait_ge(y_out, c - 1)
                    for f in range(FT):
                        nc.tensor.matmul(bank(env, 2 + c % 2, P, f * P), pT[:, T_R + f, tok], state[:, f, :], start=True, stop=False, skip_group_check=True)
                        for h in (2 * f, 2 * f + 1):
                            m = nc.tensor.matmul(
                                bank(env, 2 + c % 2, HD, h * HD), W["rb"][:, t, h, :], U[:, h * HD : (h + 1) * HD], start=False, stop=True, skip_group_check=True)
                    m.then_inc(y_ready, 1)

            @block.scalar
            def _(act):
                for c in range(CHUNKS):
                    act.wait_ge(u_ready, c + 1)
                    if c:
                        act.wait_ge(y_ready, c)
                    nc.scalar.copy(U, bank(env, 1)).then_inc(u_out, 1)

            @block.vector
            def _(dve):
                st = Steps(dve, step)
                nc.vector.memset(state, 0.0).then_inc(state_ready, 1)
                for c in range(CHUNKS):
                    t, half = c // 2, slice((c % 2) * HD, (c % 2 + 1) * HD)
                    dve.wait_ge(as_ready, c + 1)
                    nc.vector.tensor_tensor(rhs, bank(env, 0), W["akv"][:, t, :], ALU.add).then_inc(rhs_ready, 1)
                    dve.wait_ge(new_ready, c + 1)
                    b = bank(env, 4 + c % 2).rearrange("p (f n) -> p f n", f=FT)
                    st.link(nc.vector.tensor_tensor(new, b, C2["pair"][:].unsqueeze(1).to_broadcast([P, FT, P]), ALU.mult))
                    st.link(nc.vector.tensor_tensor(new, new, state, ALU.add))
                    dve.wait_ge(y_ready, c + 1)
                    nc.vector.tensor_tensor(
                        state, new, W["end"][:, :, c : c + 1].to_broadcast([P, FT, P]), ALU.mult).then_inc(state_ready, 1)
                    nc.vector.tensor_tensor(y[half, t, :], env.PS[half, (2 + c % 2) * BANK : (3 + c % 2) * BANK], W["rkv"][half, t, :], ALU.add).then_inc(y_out, 1)


def stage_rwkv_post(env, W, y, mix):
    nc, C2 = env.nc, env.C2
    with ExitStack() as ctx:
        sem = lambda name: env.semaphore("rwp_" + name)
        sb = lambda name, shape: ctx.enter_context(nc.sbuf_tensor("rwp_" + name, shape, F32))
        mean, var = sb("mean", [P, TH]), sb("var", [P, TH])
        sq = W["rb"][:].rearrange("p t h l -> p (t h l)")[:, 0 : TX * BW]
        step, var_ready, root_ready, bonus_ready, normed, turned, mixed = (
            sem("step"), sem("var"), sem("root"), sem("bonus"), sem("normed"), sem("turned"), sem("mixed"))
        heads = y.rearrange("p t (h d) -> p (t h) d", d=HD)
        wide = lambda v: v[:].unsqueeze(2).to_broadcast([P, TH, HD])
        rows = lambda v: v[:].unsqueeze(1).to_broadcast([P, TX, BW])
        with nc.Block() as block:

            @block.gpsimd
            def _(pool):
                v = W["v"][:].rearrange("p t (h d) -> p (t h) d", d=HD)
                nc.gpsimd.tensor_tensor(v, v, wide(W["bonus"]), ALU.mult).then_inc(bonus_ready, 1)

            @block.vector
            def _(dve):
                st = Steps(dve, step)
                st.link(nc.vector.tensor_reduce(mean[:], heads, AX.X, ALU.add))
                st.link(nc.vector.tensor_scalar(mean[:], mean[:], 1.0 / HD, None, ALU.mult))
                st.link(nc.vector.tensor_tensor(heads, heads, wide(mean), ALU.subtract))
                st.link(nc.vector.tensor_tensor(sq, y.rearrange("p t c -> p (t c)"), y.rearrange("p t c -> p (t c)"), ALU.mult))
                st.link(nc.vector.tensor_reduce(var[:], sq.rearrange("p (g d) -> p g d", d=HD), AX.X, ALU.add))
                nc.vector.tensor_scalar(var[:], var[:], 1.0 / HD, RWKV_GN_EPS, ALU.mult, ALU.add).then_inc(var_ready, 1)
                dve.wait_ge(root_ready, 1)
                st.link(nc.vector.reciprocal(var[:], var[:]))
                st.link(nc.vector.tensor_tensor(heads, heads, wide(var), ALU.mult))
                st.link(nc.vector.tensor_tensor(y, y, rows(C2["ln_w"]), ALU.mult))
                st.link(nc.vector.tensor_tensor(y, y, rows(C2["ln_b"]), ALU.add))
                dve.wait_ge(bonus_ready, 1)
                nc.vector.tensor_tensor(y, y, W["v"][:], ALU.add).then_inc(normed, 1)
                for f in range(FT):
                    dve.wait_ge(turned, f + 1)
                    nc.vector.tensor_tensor(mix[:, FT + f, :], bank(env, f), W["g"][:, f, :], ALU.mult).then_inc(mixed, 1)

            @block.scalar
            def _(act):
                act.wait_ge(var_ready, 1)
                nc.scalar.activation(var[:], var[:], ACT.Sqrt).then_inc(root_ready, 1)

            @block.tensor
            def _(pe):
                pe.wait_ge(normed, 1)
                for f in range(FT):
                    for t in range(TX):
                        m = nc.tensor.transpose(bank(env, f, P, t * P), y[:, t, f * P : (f + 1) * P], env.ident[:])
                    m.then_inc(turned, 1)


def stage_ffn_up(env, fT, yb, taps, conv_b):
    nc, A = env.nc, env.A
    with ExitStack() as ctx:
        sem = lambda name: env.semaphore("ffu_" + name)
        ready, based, conv_done, gated, product_done, hi_done, lo_done, step = (
            sem("ready"), sem("based"), sem("conv"), sem("gated"), sem("product"), sem("f_hi"), sem("f_lo"), sem("step"))
        ring = Ring(env, "ffu", A["ffn_up"], FF_T)
        LOOPS = FF_T // 2
        col = lambda n: bass.ds(n, 1)
        f_part = lambda part, n: fT[:, part, col(n), :].rearrange("p a t -> p (a t)")
        with nc.Block() as block:

            @block.sync
            def _(sp):
                ring.load_rest(sp)
                ring.prefetch_next(sp, A["ffn_down"].rearrange("c p r n -> c p (r n)").rearrange("c p (k n) -> c p k n", n=CW))

            @block.gpsimd
            def _(pool):
                ring.all_lo(pool)

            @block.tensor
            def _(pe):
                with pe.Fori(0, LOOPS) as i:
                    for s in range(2):
                        n = 2 * i + s
                        pe.wait_ge(ring.lo_done, n + 1)
                        pe.wait_ge(conv_done, n + 1)
                        for half in range(2):
                            m = ring.transposed(s, half, (bank(env, 2 * s + half),), ((0, S),))
                        m.then_inc(ready, 1)

            @block.scalar
            def _(act):
                def pair(n, s, i, more):
                    act.wait_ge(ready, n + 1)
                    if more:
                        ring.hi(act, i + 1, s)
                    act.wait_ge(lo_done, n + 1)
                    for half in range(2):
                        tap = taps[:, half, col(n), 2:3].rearrange("p a b -> p (a b)")
                        nc.scalar.activation(
                            yb[:, s, half, :], bank(env, 2 * s + half), ACT.Identity, bias=conv_b[:, half, col(n)], scale=tap).then_inc(based, 1)
                    act.wait_ge(conv_done, n + 3)
                    nc.scalar.activation(yb[:, s, 0, :], yb[:, s, 0, :], ACT.Silu).then_inc(gated, 1)
                    act.wait_ge(product_done, n + 1)
                    nc.scalar.copy(f_part(0, n), yb[:, s, 0, :]).then_inc(hi_done, 1)

                ring.hi(act, 0, 0)
                ring.hi(act, 0, 1)
                with act.Fori(0, LOOPS - 1) as i:
                    for s in range(2):
                        pair(2 * i + s, s, i, True)
                for s in range(2):
                    pair(FF_T - 2 + s, s, None, False)

            @block.vector
            def _(dve):
                dve.sem_inc(conv_done, 2)
                dve.sem_inc(lo_done, 2)
                with dve.Fori(0, LOOPS) as i:
                    st = Steps(dve, step, 4 * i)
                    for s in range(2):
                        n = 2 * i + s
                        dve.wait_ge(based, 2 * n + 2)
                        for back in (1, 2):
                            for half in range(2):
                                tap = taps[:, half, col(n), 2 - back : 3 - back].rearrange("p a b -> p (a b)")
                                out = yb[:, s, half, back:S]
                                m = nc.vector.scalar_tensor_tensor(out, bank(env, 2 * s + half, S - back), tap, out, ALU.mult, ALU.add)
                                if back == 1:
                                    st.inc(m)
                            if back == 1:
                                dve.wait_ge(step, st.base + st.n)
                        m.then_inc(conv_done, 1)
                        dve.wait_ge(gated, n + 1)
                        dve.wait_ge(conv_done, n + 3)
                        nc.vector.tensor_tensor(yb[:, s, 0, :], yb[:, s, 0, :], yb[:, s, 1, :], ALU.mult).then_inc(product_done, 1)
                        dve.wait_ge(hi_done, n + 1)
                        nc.vector.tensor_tensor(f_part(1, n), yb[:, s, 0, :], f_part(0, n).bitcast(F32), ALU.subtract).then_inc(lo_done, 1)


def stage_ffn_down(env, fT, gate, Y):
    nc, A = env.nc, env.A
    with ExitStack() as ctx:
        sem = lambda name: env.semaphore("ffd_" + name)
        ss = ctx.enter_context(nc.sbuf_tensor("ffd_ss", [P, TX], F32))
        multiplied, squared, mean_ready, root_ready, updated, step = (
            sem("multiplied"), sem("squared"), sem("mean"), sem("root"), sem("updated"), sem("step"))
        ring = Ring(env, "ffd", A["ffn_down"].rearrange("c p r n -> c p (r n)").rearrange("c p (k n) -> c p k n", n=CW), FF_T // 2)
        rows = lambda s, part: env.parts[s][:, part].rearrange("p k n -> p (k n)").rearrange("p (r n) -> p r n", r=2)
        LOOPS = FF_T // 4
        total = lambda t: env.PS[:, 2 * t * BANK : (2 * t + 2) * BANK]
        with nc.Block() as block:

            @block.sync
            def _(sp):
                ring.load_rest(sp)

            @block.gpsimd
            def _(pool):
                ring.all_lo(pool)

            @block.tensor
            def _(pe):
                for c in range(FF_T // 2):
                    s = c % 2
                    pe.wait_ge(ring.lo_done, c + 1)
                    for t in range(TX):
                        for r in range(2):
                            for n, (wp, tp) in enumerate(PASSES):
                                for h in range(2):
                                    first, last = c + r + n == 0, c == FF_T // 2 - 1 and r == 1 and n == 2
                                    m = nc.tensor.matmul(
                                        bank(env, 2 * t + h), fT[:, tp, 2 * c + r, t * P : (t + 1) * P], rows(s, wp)[:, r, h * BANK : (h + 1) * BANK],
                                        start=first, stop=last)
                        if t == TX - 1 or c == FF_T // 2 - 1:
                            m.then_inc(multiplied, 1)

            @block.scalar
            def _(act):
                ring.hi(act, 0, 0)
                ring.hi(act, 0, 1)
                with act.Fori(1, LOOPS) as i:
                    for s in range(2):
                        ring.hi(act, i, s, (multiplied, 2 * i + s - 1))
                ring.hi(act, LOOPS, 0, (multiplied, 2 * LOOPS - 1))
                for t in range(TX):
                    act.wait_ge(multiplied, FF_T // 2 + t)
                    if t >= 2:
                        act.wait_ge(updated, t - 1)
                    nc.scalar.activation(Y[:, t % 2, :], total(t), ACT.Square, accum_out=ss[:, t : t + 1]).then_inc(squared, 1)
                    act.wait_ge(mean_ready, t + 1)
                    nc.scalar.activation(ss[:, t : t + 1], ss[:, t : t + 1], ACT.Sqrt).then_inc(root_ready, 1)

            @block.vector
            def _(dve):
                st = Steps(dve, step)
                for t in range(TX):
                    s = ss[:, t : t + 1]
                    dve.wait_ge(squared, t + 1)
                    nc.vector.tensor_scalar(s, s, 1.0 / D, EPS, ALU.mult, ALU.add).then_inc(mean_ready, 1)
                    dve.wait_ge(root_ready, t + 1)
                    st.link(nc.vector.reciprocal(s, s))
                    st.link(nc.vector.scalar_tensor_tensor(Y[:, t % 2, :], total(t), s, gate, ALU.mult, ALU.mult))
                    nc.vector.tensor_tensor(env.X[:, t, :], env.X[:, t, :], Y[:, t % 2, :], ALU.add).then_inc(updated, 1)


ROWS2 = ("dt_bias", "a_log", "ssd_d", "ln_w", "ln_b")
SHAPES2 = {
    "upto": [P, P], "ones": [P, P], "pair": [P, P], "reset": [P, S], "within": [P, 4, P], "level": [P, LEVELS, P],
    "lora": [P, BW], "g2": [P, BW], "ssd_taps": [P, 8, 4], "ssd_conv_b": [P, 8], "mu": [P, RW_TILES],
    "w0": [P, FT], "a0": [P, FT], "k_k": [P, FT], "k_a": [P, FT], "r_k": [P, FT, SSD_HEADS], "ssd_norm": [P, FT],
    "dt_bias": [P, TH], "a_log": [P, TH], "ssd_d": [P, BW], "ln_w": [P, BW], "ln_b": [P, BW],
}


def layer_second(env):
    nc, A = env.nc, env.A
    pre = lambda k: env.pre2[:, k : k + 1]
    with ExitStack() as block2:
        sb2 = lambda name, shape: block2.enter_context(nc.sbuf_tensor("b2_" + name, shape, F32))
        gates, env.pre2, pre_ffn = sb2("gates", [P, 2, D]), sb2("pre_mix", [P, KD]), sb2("pre_ffn", [P, KD])
        taps, conv_b = sb2("ffn_taps", [P, 2, FF_T, 3]), sb2("ffn_conv_b", [P, 2, FF_T])
        small_in = block2.enter_context(nc.semaphore("b2_small_in"))
        with nc.Block() as block:

            @block.scalar
            def _(act):
                act.dma_start(env.pre2[:], A["pre_mix"]).then_inc(small_in, 16)
                act.dma_start(pre_ffn[:], A["pre_ffn"]).then_inc(small_in, 16)
                act.dma_start(gates[:, 0, :], A["post_mix"].partition_broadcast(P)).then_inc(small_in, 16)
                act.dma_start(gates[:, 1, :], A["post_ffn"].partition_broadcast(P)).then_inc(small_in, 16)
                act.dma_start(taps[:], A["ffn_taps"]).then_inc(small_in, 16)
                act.dma_start(conv_b[:], A["ffn_conv_b"]).then_inc(small_in, 16)
                act.wait_ge(small_in, 96)

        with ExitStack() as mixers:
            sb = lambda name, shape: mixers.enter_context(nc.sbuf_tensor("mix_" + name, shape, F32))
            env.C2 = {n: sb(n, s) for n, s in SHAPES2.items()}
            pT, mix = sb("pT", [P, 22, S]), sb("mix", [P, KD, S])
            flat = pT[:].rearrange("p n t -> p (n t)")
            wide = flat[:, 0 : TX * D].rearrange("p (t d) -> p t d", d=D)
            with ExitStack() as ssd:
                sbs = lambda name, shape: ssd.enter_context(nc.sbuf_tensor("ssd_" + name, shape, F32))
                zN, dtN = sbs("z", [P, TX, BW]), sbs("dt_raw", [P, TH])
                with ExitStack() as proj:
                    env.split_operands(proj, "sec", S)
                    stage_norm(env, "norm2", [(env.X, TX, 0, pre, None)], wide, pT[:, T_R : T_R + 4, :])
                    stage_second_proj(env, pT, zN, dtN)
                V = {n: sbs(n, [P, TH]) for n in ("dt", "a", "acs", "dstate", "eacs", "etot")}
                V |= {"conv": sbs("conv", [P, 8, S]), "xs": sbs("xs", [P, TX, BW]), "B": sbs("B", [P, TX, 2 * SSD_STATE]), "skip": sbs("skip", [P, TX, BW])}
                V |= {"xdt": pT[:, 0:FT, :], "xds": pT[:, FT : 2 * FT, :]}
                stage_ssd_prep(env, pT, dtN, V)
                stage_ssd(env, V, zN, mix)
            with ExitStack() as rwkv:
                sbr = lambda name, shape: rwkv.enter_context(nc.sbuf_tensor("rw_" + name, shape, F32))
                quarter = [w[:].rearrange("p k n -> p (k n)").rearrange("p (f t) -> p f t", t=S) for w in env.raw]
                quarter += [sbr(f"scratch{j}", [P, FT, S])[:] for j in range(2)]
                stage_rwkv_shift(env, pT, quarter)
                W = {n: sbr(n, [P, TX, BW]) for n in ("v", "b", "k")}
                W |= {"g": sbr("g", [P, FT, S]), "end": sbr("end", [P, FT, CHUNKS]), "bonus": sbr("bonus", [P, TH])}
                stage_rwkv_features(env, pT, W, quarter)
                W |= {"inv": sbr("inv", [P, TX, SSD_HEADS, P]), "rb": sbr("rb", [P, TX, SSD_HEADS, P])}
                W |= {"akv": pT[:, T_V : T_V + FT, :], "rkv": mix[:, FT:KD, :]}
                stage_rwkv_matrices(env, pT, W, quarter)
                stage_rwkv_inverse(env, W, quarter)
                y = pT[:, 0:FT, :]
                stage_rwkv_scan(env, pT, W, y)
                stage_rwkv_post(env, W, y, mix)
            env.split_operands(mixers, "out2", S)
            stage_out(env, "out2", [(env.X, TX, 0, gates[:, 0, :])], [mix[:, f, :] for f in range(KD)], A["w_out_2"], wide, A["ffn_up"])
        with ExitStack() as ffn:
            yb = ffn.enter_context(nc.sbuf_tensor("ffn_conv", [P, 2, 2, S], F32))
            env.split_operands(ffn, "ffn", S)
            with ExitStack() as norm:
                xs, tmp = (norm.enter_context(nc.sbuf_tensor(f"norm3_{n}", shape, F32)) for n, shape in (("x", [P, TX, D]), ("h", [P, 4, S])))
                stage_norm(env, "norm3", [(env.X, TX, 0, lambda k: pre_ffn[:, k : k + 1], None)], xs, tmp)
            fT = ffn.enter_context(nc.sbuf_tensor("ffn_f_parts", [P, 2, FF_T, S], F32R))
            stage_ffn_up(env, fT, yb, taps, conv_b)
            stage_ffn_down(env, fT, gates[:, 1, :], yb[:].rearrange("p b h t -> p b (h t)"))


def build_program(nc, A, out):
    env = Env()
    env.nc, env.A = nc, A
    env.stage_semaphores = []
    with ExitStack() as ctx:
        sb = lambda name, shape: ctx.enter_context(nc.sbuf_tensor(name, shape, F32))
        env.PS = ctx.enter_context(nc.psum_tensor("banks", [P, 8 * BANK], F32))
        env.X = sb("resid_x", [P, TX, D])
        env.ident = sb("identity", [P, P])
        env.gain = sb("gain", [P, 2, KD, 2])
        env.shift = sb("shift", [P, 2, KD, 2])
        env.neg_lam = sb("neg_lam", [P, 1])
        env.subln = sb("subln_col", [P, 1])
        env.raw = [sb(f"weight_chunk{s}", [P, KD, CW]) for s in range(2)]
        env.raw_in = [ctx.enter_context(nc.semaphore(f"weight_chunk_in{s}")) for s in range(2)]
        env.raw_count = [0, 0]
        env.even_stacked = [ctx.enter_context(nc.semaphore(f"even_stacked{s}")) for s in range(2)]
        env.odd_stacked = [ctx.enter_context(nc.semaphore(f"odd_stacked{s}")) for s in range(2)]
        gain = lambda l, r: lambda k: env.gain[:, l, k, r : r + 1]
        shift = lambda l, r: lambda k: env.shift[:, l, k, r : r + 1]
        with ExitStack() as first:
            env.CX = first.enter_context(nc.sbuf_tensor("resid_ctx", [P, TC, D], F32))
            env.gate = first.enter_context(nc.sbuf_tensor("gate", [P, 3, D], F32))
            stage_modulation(env)
            layer_even(env, gain, shift)
            layer_odd(env, gain, shift)
            env.clear_semaphores()
        layer_second(env)
        stored = ctx.enter_context(nc.semaphore("stored"))
        with nc.Block() as block:

            @block.sync
            def _(sp):
                sp.dma_start(out.rearrange("b (t p) d -> p (b t) d", p=P), env.X[:]).then_inc(stored, 16)
                sp.wait_ge(stored, 16)


def chunked(w, width=CW):
    K, N = w.shape
    return np.ascontiguousarray(w.reshape(K // P, P, N // width, width).transpose(2, 1, 0, 3))


def columns(v, tile=P):
    return np.ascontiguousarray(v.reshape(-1, tile).T)


def rope_constants():
    nf = A_QK // 4
    inv = (np.float32(10000.0) ** (-np.arange(nf, dtype=np.float32) / np.float32(nf))).astype(np.float32)
    t = np.arange(S)
    pos = np.stack([t // GRID_W, t % GRID_W]).astype(np.float32)
    p = np.arange(P)
    e = p % (2 * nf)
    ang = (pos[(p % A_QK) // (2 * nf)] * inv[e % nf][:, None]).astype(np.float32).astype(np.float64)
    sign = np.where(e < nf, -1.0, 1.0)[:, None]
    cs = np.stack([np.cos(ang), sign * np.sin(ang)], 1)
    both = np.stack([cs * A_QK**-0.5, cs], 1).astype(np.float32)
    swap = np.zeros((P, P), np.float32)
    swap[np.where(e < nf, p + nf, p - nf), p] = 1.0
    return both, swap


def dft_constants():
    t = np.arange(S)
    f = np.arange(C_HD)
    at = 2 * np.pi * (np.outer(t, t) % S) / S
    af = 2 * np.pi * (np.outer(f, f) % C_HD) / C_HD
    scale = 1.0 / np.sqrt(S * C_HD)
    token = np.stack([np.cos(at), np.sin(at)]).reshape(2, TX, P, S).transpose(2, 0, 1, 3)
    pair = np.eye(P // C_HD)
    feature = np.stack([np.kron(pair, np.cos(af)), -np.kron(pair, np.sin(af))]) * scale
    return np.ascontiguousarray(token, np.float32), np.ascontiguousarray(feature.transpose(1, 0, 2), np.float32)


def window_bias(rpb):
    cq, kc = np.arange(GRID_W)[:, None], np.arange(GRID_W)[None]
    first = np.clip(cq - NA_KW // 2, 0, GRID_W - NA_KW)
    inside = (kc >= first) & (kc < first + NA_KW)
    padded = np.concatenate([rpb, np.full(rpb.shape[:2] + (1,), -1e30, rpb.dtype)], -1)
    col = np.where(inside, kc - cq + NA_KW - 1, rpb.shape[-1])
    laid = padded[:, :, col].transpose(2, 0, 1, 3)
    both = np.concatenate([laid[:, :, 1 : BIAS_SLOTS + 1], laid[:, :, 0:BIAS_SLOTS]])
    return np.ascontiguousarray(both.reshape(P, C_HEADS, BIAS_SLOTS * GRID_W))


def second_constants():
    s, l = np.arange(P)[:, None], np.arange(P)[None]
    same = s // RW_CHUNK == l // RW_CHUNK
    incl, strict = same & (s <= l), same & (s < l)
    level = [(s // (2 * m) == l // (2 * m)) & (s // m % 2 == 0) & (l // m % 2 == 1) for m in (1 << j for j in range(LEVELS))]
    c = {
        "upto": s <= l, "ones": np.ones((P, P)), "pair": same,
        "reset": np.broadcast_to(np.arange(S) % RW_CHUNK != 0, (P, S)),
        "within": np.stack([incl, strict, incl, strict], 1), "level": np.stack(level, 1),
    }
    return {k: np.ascontiguousarray(v, np.float32) for k, v in c.items()}


def second_arrays(I):
    a = {"c2_" + k: v for k, v in second_constants().items()}
    w = I["w_in_2"][0]
    z, xbc, dt, rw = w[:, 0:512], w[:, 512:1536], w[:, 1536:1544], w[:, 1544:]
    r, w_lo, k, v, a_lo, g_lo = np.split(rw, np.cumsum([512, 64, 512, 512, 64]), 1)
    a["w_in_2"] = chunked(np.concatenate([xbc, r, k, v, w_lo, a_lo, g_lo, z], 1))
    a["w_dt"] = chunked(dt, SSD_HEADS)[0]
    mr, mw, mk, mv, ma, mg = np.split(I["rwkv_mu_2"][0], np.cumsum([512, 64, 512, 512, 64]))
    a["c2_mu"] = columns(np.concatenate([mr, mk, mv, mw, ma, mg]))
    a["c2_ssd_taps"] = I["ssd_conv_w_2"][0].reshape(4, 8, P).transpose(2, 1, 0)
    a["c2_ssd_conv_b"] = columns(I["ssd_conv_b_2"][0])
    for name, key in (("w0", "rwkv_w0"), ("a0", "rwkv_a0"), ("k_k", "rwkv_k_k"), ("k_a", "rwkv_k_a"), ("ssd_norm", "ssd_norm")):
        a["c2_" + name] = columns(I[key + "_2"][0])
    a["c2_lora"] = np.concatenate([I["rwkv_w2_2"][0], I["rwkv_a2_2"][0]])
    a["c2_g2"] = I["rwkv_g2_2"][0]
    rk = np.zeros((SSD_HEADS, HD, SSD_HEADS), np.float32)
    rk[np.arange(SSD_HEADS), :, np.arange(SSD_HEADS)] = I["rwkv_r_k_2"][0]
    a["c2_r_k"] = rk.reshape(FT, P, SSD_HEADS).transpose(1, 0, 2)
    a["c2_dt_bias"], a["c2_a_log"] = np.tile(I["ssd_dt_bias_2"][0], TX), np.tile(I["ssd_a_log_2"][0], TX)
    a["c2_ssd_d"] = np.repeat(I["ssd_d_2"][0], HD)
    a["c2_ln_w"], a["c2_ln_b"] = I["rwkv_ln_w_2"][0], I["rwkv_ln_b_2"][0]
    a["w_out_2"] = chunked(I["w_out_2"][0])
    a["pre_mix"], a["pre_ffn"] = columns(I["pre_mix_norm_2"][0]), columns(I["pre_ffn_norm_2"][0])
    a["post_mix"], a["post_ffn"] = I["post_mix_norm_2"][0], I["post_ffn_norm_2"][0]
    up = I["ffn_w_up_2"][0].reshape(D, 2, FF_T, P).transpose(0, 2, 1, 3).reshape(D, 2 * D_FF)
    a["ffn_up"] = chunked(up)
    a["ffn_taps"] = I["ffn_conv_w_2"][0].reshape(3, 2, FF_T, P).transpose(3, 1, 2, 0)
    a["ffn_conv_b"] = I["ffn_conv_b_2"][0].reshape(2, FF_T, P).transpose(2, 0, 1)
    a["ffn_down"] = I["ffn_w_down_2"][0].reshape(FF_T // 2, 2, P, D).transpose(0, 2, 1, 3)
    return a


def host_arrays(I):
    a = {}
    a["x"], a["ctx"] = I["x"][0], I["ctx"][0]
    a["cond"] = np.ascontiguousarray(np.stack([I["c"][0], I["c_ctx"]], -1).reshape(KD, P, 2).transpose(1, 0, 2))
    a["w_mod"] = np.concatenate([chunked(I["w_mod"][l], BANK) for l in range(2)])
    a["b_mod"] = I["b_mod"].reshape(-1)
    a["sel"] = np.ascontiguousarray(np.broadcast_to(np.eye(2, dtype=np.float32)[:, :, None], (2, 2, P)))
    a["norm_pre"] = np.ascontiguousarray(np.broadcast_to(I["norm_pre"].reshape(2, KD, P).transpose(2, 0, 1)[..., None], (P, 2, KD, 2)))
    a["norm_post"] = I["norm_post"]
    a["lam_a"] = I["lam_a"][0]
    a["ident"] = np.eye(P, dtype=np.float32)
    a["subln"] = np.ascontiguousarray(np.tile(I["subln_a"][0], 2)[:, None])
    halves = lambda branches: [2 * b + h for b in branches for h in range(BW // CW)]
    w = I["w_in_even"][0].copy()
    maps = w[:, 0 : 2 * BW].reshape(D, 2, A_HEADS * A_QK // P, P // A_QK, 2, A_QK)
    w[:, 0 : 2 * BW] = maps.transpose(0, 1, 4, 2, 3, 5).reshape(D, 2 * BW)
    a["w_in_even"] = chunked(w)[halves([0, 1, 3, 6, 7, 5, 4, 2])]
    a["rope"], a["rope_swap"] = rope_constants()
    a["conv_b"] = np.ascontiguousarray(I["conv_b"][0].reshape(3, FT, P).transpose(2, 1, 0))
    a["w_out"] = np.stack([chunked(I["w_out"][l]) for l in range(2)])
    a["w_in_odd"] = chunked(I["w_in_odd"][0])[halves([0, 3, 5, 1, 2, 4])]
    a["dft_t"], a["dft_f"] = dft_constants()
    a |= second_arrays(I)
    a["na_bias"] = window_bias(I["rpb_c"][0])
    return a


def kernel(**inputs):
    from concourse import bacc
    from concourse.bass_utils import run_bass_kernel_spmd

    inputs = {k: np.asarray(v) for k, v in inputs.items()}
    arrays = {"in_" + k: np.ascontiguousarray(v) for k, v in host_arrays(inputs).items()}
    nc = bacc.Bacc("TRN2", target_bir_lowering=False, num_devices=1)
    A = {k[3:]: nc.dram_tensor(k, v.shape, mybir.dt.from_np(v.dtype), kind="ExternalInput").ap() for k, v in arrays.items()}
    out = nc.dram_tensor("out", (1, S, D), F32, kind="ExternalOutput").ap()
    build_program(nc, A, out)
    r = run_bass_kernel_spmd(nc, [arrays], core_ids=[0])
    return r.results[0]["out"]
```
